# Optimizing a Trainium2 kernel written in Bass

```python
import jax, jax.numpy as jnp
from jax import lax
import numpy as np

D_MODEL = 1024
BATCH = 1
SEQ = 256
DEPTH = 2

N_MIXERS = 2
N_SSM_LAYERS = (DEPTH + 1) // 2
N_ATTN_LAYERS = DEPTH // 2
SSM_WIDTH = D_MODEL
SSM_GROUP = 16
SSM_GROUPS = SSM_WIDTH // SSM_GROUP
SSM_STATE = 64
DT_MIN = 1e-3
DT_MAX = 1e-1
HEAD_DIM = 128
N_HEADS = D_MODEL // HEAD_DIM
ATTN_WIDTH = N_HEADS * HEAD_DIM
ROT_DIM = HEAD_DIM // 4
ROPE_THETA = 500000.0
MOBA_BLOCK = 256
MOBA_TOPK = 3
Q_CHUNK = 128
NORM_EPS = 1e-6


def rms_norm(x, g):
    xf = x.astype(jnp.float32)
    y = xf * lax.rsqrt(jnp.mean(xf * xf, axis=-1, keepdims=True) + NORM_EPS)
    return (y * g.astype(jnp.float32)).astype(x.dtype)

def partial_rotary(x, pos):
    half = ROT_DIM // 2
    inv_freq = ROPE_THETA ** (-(jnp.arange(half, dtype=jnp.float32) * 2.0) / ROT_DIM)
    ang = pos.astype(jnp.float32)[:, None] * inv_freq[None, :]
    cos, sin = jnp.cos(ang), jnp.sin(ang)
    xf = x.astype(jnp.float32)
    x1, x2, rest = xf[..., :half], xf[..., half:ROT_DIM], xf[..., ROT_DIM:]
    out = jnp.concatenate([x1 * cos - x2 * sin, x2 * cos + x1 * sin, rest], axis=-1)
    return out.astype(x.dtype)

def _complex_linear_combine(e1, e2):
    a1r, a1i, b1r, b1i = e1
    a2r, a2i, b2r, b2i = e2
    ar = a2r * a1r - a2i * a1i
    ai = a2r * a1i + a2i * a1r
    br = a2r * b1r - a2i * b1i + b2r
    bi = a2r * b1i + a2i * b1r + b2i
    return (ar, ai, br, bi)

def s5_mixer(h, w_in, a_re, a_im, log_dt, b_re, b_im, c_re, c_im, d_skip, w_glu, b_glu, w_out):
    bsz, seq, _ = h.shape
    proj = h @ w_in
    u, z = proj[..., :SSM_WIDTH], proj[..., SSM_WIDTH:]
    uf = u.astype(jnp.float32)
    ug = uf.reshape(bsz, seq, SSM_GROUPS, SSM_GROUP)
    dt = jnp.exp(log_dt.astype(jnp.float32))[:, None]
    lr, li = a_re.astype(jnp.float32), a_im.astype(jnp.float32)
    mag = jnp.exp(lr * dt)
    ab_re, ab_im = mag * jnp.cos(li * dt), mag * jnp.sin(li * dt)
    den = lr * lr + li * li
    nr, ni = ab_re - 1.0, ab_im
    f_re = (nr * lr + ni * li) / den
    f_im = (ni * lr - nr * li) / den
    bu_re = jnp.einsum('blgc,gpc->blgp', ug, b_re.astype(jnp.float32))
    bu_im = jnp.einsum('blgc,gpc->blgp', ug, b_im.astype(jnp.float32))
    in_re = f_re * bu_re - f_im * bu_im
    in_im = f_re * bu_im + f_im * bu_re
    a_re_t = jnp.broadcast_to(ab_re, in_re.shape)
    a_im_t = jnp.broadcast_to(ab_im, in_re.shape)
    _, _, s_re, s_im = lax.associative_scan(
        _complex_linear_combine, (a_re_t, a_im_t, in_re, in_im), axis=1)
    y = (jnp.einsum('blgp,gcp->blgc', s_re, c_re.astype(jnp.float32))
         - jnp.einsum('blgp,gcp->blgc', s_im, c_im.astype(jnp.float32)))
    y = y.reshape(bsz, seq, SSM_WIDTH) + d_skip.astype(jnp.float32) * uf
    y = jax.nn.gelu(y)
    y = y * jax.nn.sigmoid(y @ w_glu.astype(jnp.float32) + b_glu.astype(jnp.float32))
    y = y.astype(h.dtype) * jax.nn.silu(z)
    return y @ w_out

def moba_mixer(h, w_in, q_gain, k_gain, w_out):
    bsz, seq, _ = h.shape
    proj = h @ w_in
    q, k, v, z = jnp.split(proj, 4, axis=-1)

    def heads(t):
        return t.reshape(bsz, seq, N_HEADS, HEAD_DIM).transpose(0, 2, 1, 3)

    pos = jnp.arange(seq)
    q = partial_rotary(rms_norm(heads(q), q_gain), pos)
    k = partial_rotary(rms_norm(heads(k), k_gain), pos)
    v = heads(v)
    n_blocks = -(-seq // MOBA_BLOCK)
    pad = n_blocks * MOBA_BLOCK - seq
    k_pad = jnp.pad(k, ((0, 0), (0, 0), (0, pad), (0, 0)))
    v_pad = jnp.pad(v, ((0, 0), (0, 0), (0, pad), (0, 0)))
    k_blocks = k_pad.reshape(bsz, N_HEADS, n_blocks, MOBA_BLOCK, HEAD_DIM)
    v_blocks = v_pad.reshape(bsz, N_HEADS, n_blocks, MOBA_BLOCK, HEAD_DIM)
    k_mean = jnp.mean(k_blocks.astype(jnp.float32), axis=3)
    top_k = min(MOBA_TOPK, n_blocks)
    scale = HEAD_DIM ** -0.5
    b_idx = jnp.arange(bsz)[:, None, None, None]
    h_idx = jnp.arange(N_HEADS)[None, :, None, None]
    blk_ids = jnp.arange(n_blocks)
    key_off = jnp.arange(MOBA_BLOCK)

    def chunk(c):
        start = c * Q_CHUNK
        qc = lax.dynamic_slice_in_dim(q, start, Q_CHUNK, axis=2).astype(jnp.float32)
        own = start // MOBA_BLOCK
        q_pos = start + jnp.arange(Q_CHUNK)
        gate = jnp.einsum('bhqd,bhnd->bhqn', qc, k_mean)
        gate = jnp.where(blk_ids[None, None, None, :] < own, gate, -jnp.inf)
        _, sel = lax.top_k(gate, top_k)
        sel_valid = sel < own
        k_sel = k_blocks[b_idx, h_idx, sel].astype(jnp.float32)
        v_sel = v_blocks[b_idx, h_idx, sel].astype(jnp.float32)
        s_sel = jnp.einsum('bhqd,bhqnkd->bhqnk', qc, k_sel) * scale
        s_sel = jnp.where(sel_valid[..., None], s_sel, -jnp.inf)
        k_own = lax.dynamic_slice_in_dim(k_pad, own * MOBA_BLOCK, MOBA_BLOCK, axis=2).astype(jnp.float32)
        v_own = lax.dynamic_slice_in_dim(v_pad, own * MOBA_BLOCK, MOBA_BLOCK, axis=2).astype(jnp.float32)
        s_own = jnp.einsum('bhqd,bhkd->bhqk', qc, k_own) * scale
        causal = (own * MOBA_BLOCK + key_off)[None, :] <= q_pos[:, None]
        s_own = jnp.where(causal, s_own, -jnp.inf)
        logits = jnp.concatenate(
            [s_own, s_sel.reshape(bsz, N_HEADS, Q_CHUNK, top_k * MOBA_BLOCK)], axis=-1)
        p = jax.nn.softmax(logits, axis=-1)
        p_own = p[..., :MOBA_BLOCK]
        p_sel = p[..., MOBA_BLOCK:].reshape(bsz, N_HEADS, Q_CHUNK, top_k, MOBA_BLOCK)
        o = (jnp.einsum('bhqk,bhkd->bhqd', p_own, v_own)
             + jnp.einsum('bhqnk,bhqnkd->bhqd', p_sel, v_sel))
        return o.astype(h.dtype)

    out = lax.map(chunk, jnp.arange(seq // Q_CHUNK))
    out = out.transpose(1, 0, 3, 2, 4).reshape(bsz, seq, ATTN_WIDTH)
    return (out * jax.nn.silu(z)) @ w_out

def first_inputs(seed: int = 0) -> dict:
    key = jax.random.key(seed)
    ks = jax.random.split(key, 20)
    f32 = jnp.float32
    na, nb = N_SSM_LAYERS, N_ATTN_LAYERS
    G, P, C = SSM_GROUPS, SSM_STATE, SSM_GROUP
    x = jax.random.normal(ks[0], (BATCH, SEQ, D_MODEL), f32)
    norm_g = 1.0 + 0.02 * jax.random.normal(ks[1], (DEPTH, D_MODEL), f32)
    ssm_w_in = jax.random.normal(ks[2], (na, D_MODEL, 2 * SSM_WIDTH), f32) * D_MODEL ** -0.5
    ssm_a_re = -0.5 + 0.01 * jax.random.normal(ks[3], (na, G, P), f32)
    ssm_a_im = (jnp.pi * jnp.arange(P, dtype=f32))[None, None, :] + 0.01 * jax.random.normal(ks[4], (na, G, P), f32)
    ssm_log_dt = jax.random.uniform(ks[5], (na, G), f32, minval=float(np.log(DT_MIN)), maxval=float(np.log(DT_MAX)))
    ssm_b_re = jax.random.normal(ks[6], (na, G, P, C), f32) * (2 * C) ** -0.5
    ssm_b_im = jax.random.normal(ks[7], (na, G, P, C), f32) * (2 * C) ** -0.5
    ssm_c_re = jax.random.normal(ks[8], (na, G, C, P), f32) * P ** -0.5
    ssm_c_im = jax.random.normal(ks[9], (na, G, C, P), f32) * P ** -0.5
    ssm_d = jax.random.normal(ks[10], (na, SSM_WIDTH), f32)
    ssm_w_glu = jax.random.normal(ks[11], (na, SSM_WIDTH, SSM_WIDTH), f32) * SSM_WIDTH ** -0.5
    ssm_b_glu = 0.01 * jax.random.normal(ks[12], (na, SSM_WIDTH), f32)
    ssm_w_out = jax.random.normal(ks[13], (na, SSM_WIDTH, D_MODEL), f32) * SSM_WIDTH ** -0.5
    attn_w_in = jax.random.normal(ks[14], (nb, D_MODEL, 4 * ATTN_WIDTH), f32) * D_MODEL ** -0.5
    attn_q_gain = 1.0 + 0.02 * jax.random.normal(ks[15], (nb, HEAD_DIM), f32)
    attn_k_gain = 1.0 + 0.02 * jax.random.normal(ks[16], (nb, HEAD_DIM), f32)
    attn_w_out = jax.random.normal(ks[17], (nb, ATTN_WIDTH, D_MODEL), f32) * ATTN_WIDTH ** -0.5
    return {"x": x, "norm_g": norm_g, "ssm_w_in": ssm_w_in, "ssm_a_re": ssm_a_re,
            "ssm_a_im": ssm_a_im, "ssm_log_dt": ssm_log_dt, "ssm_b_re": ssm_b_re,
            "ssm_b_im": ssm_b_im, "ssm_c_re": ssm_c_re, "ssm_c_im": ssm_c_im,
            "ssm_d": ssm_d, "ssm_w_glu": ssm_w_glu, "ssm_b_glu": ssm_b_glu,
            "ssm_w_out": ssm_w_out, "attn_w_in": attn_w_in, "attn_q_gain": attn_q_gain,
            "attn_k_gain": attn_k_gain, "attn_w_out": attn_w_out}

def first_block(x, norm_g, ssm_w_in, ssm_a_re, ssm_a_im, ssm_log_dt, ssm_b_re, ssm_b_im,
              ssm_c_re, ssm_c_im, ssm_d, ssm_w_glu, ssm_b_glu, ssm_w_out,
              attn_w_in, attn_q_gain, attn_k_gain, attn_w_out):
    h = x
    for i in range(DEPTH):
        hn = rms_norm(h, norm_g[i])
        j = i // N_MIXERS
        if i % N_MIXERS == 0:
            y = s5_mixer(hn, ssm_w_in[j], ssm_a_re[j], ssm_a_im[j], ssm_log_dt[j],
                         ssm_b_re[j], ssm_b_im[j], ssm_c_re[j], ssm_c_im[j], ssm_d[j],
                         ssm_w_glu[j], ssm_b_glu[j], ssm_w_out[j])
        else:
            y = moba_mixer(hn, attn_w_in[j], attn_q_gain[j], attn_k_gain[j], attn_w_out[j])
        h = h + y
    return h


MLA_HEADS = 8
MLA_NOPE = 64
MLA_ROPE = 32
MLA_V = 64
MLA_Q_RANK = 256
MLA_KV_RANK = 128
Q_BLOCK = 128
CONV_CH = 512
CONV_WIDTH = 31
RET_HEADS = 4
RET_DK = 128
RET_DV = 256
RET_CHUNK = 128
FFN_HIDDEN = -(-8 * D_MODEL // (3 * 256)) * 256
N_BRANCH = 3
ROPE_BASE = 10000.0
EPS = 1e-6

IN_SPLITS = (MLA_Q_RANK, MLA_KV_RANK, MLA_ROPE, 2 * CONV_CH,
             RET_HEADS * RET_DK, RET_HEADS * RET_DK, RET_HEADS * RET_DV, RET_HEADS * RET_DV,
             N_BRANCH * D_MODEL)
IN_COLS = (MLA_Q_RANK + MLA_KV_RANK + MLA_ROPE + 2 * CONV_CH + 2 * RET_HEADS * RET_DK
           + 2 * RET_HEADS * RET_DV + N_BRANCH * D_MODEL)


def rms_norm_2(x, g):
    xf = x.astype(jnp.float32)
    y = xf * lax.rsqrt(jnp.mean(xf * xf, -1, keepdims=True) + EPS)
    return (y * g.astype(jnp.float32)).astype(x.dtype)

def layer_norm(x, g, b):
    xf = x.astype(jnp.float32)
    mu = jnp.mean(xf, -1, keepdims=True)
    var = jnp.mean(jnp.square(xf - mu), -1, keepdims=True)
    y = (xf - mu) * lax.rsqrt(var + EPS)
    return (y * g.astype(jnp.float32) + b.astype(jnp.float32)).astype(x.dtype)

def rope_tables(positions, dim):
    inv = ROPE_BASE ** (-jnp.arange(0, dim, 2, dtype=jnp.float32) / dim)
    ang = positions.astype(jnp.float32)[..., None] * inv
    return jnp.cos(ang), jnp.sin(ang)

def apply_rope(x, cos, sin):
    if x.ndim == 4:
        cos, sin = cos[:, :, None, :], sin[:, :, None, :]
    cos, sin = cos.astype(x.dtype), sin.astype(x.dtype)
    x1, x2 = jnp.split(x, 2, axis=-1)
    return jnp.concatenate([x1 * cos - x2 * sin, x2 * cos + x1 * sin], axis=-1)

def mla_branch(c_q, c_kv, k_pe, cos, sin, q_norm, w_uq, kv_norm, w_ukv, w_o):
    B, S, _ = c_q.shape
    q = (rms_norm_2(c_q, q_norm) @ w_uq).reshape(B, S, MLA_HEADS, MLA_NOPE + MLA_ROPE)
    q_nope = q[..., :MLA_NOPE]
    q_pe = apply_rope(q[..., MLA_NOPE:], cos, sin)
    kv = (rms_norm_2(c_kv, kv_norm) @ w_ukv).reshape(B, S, MLA_HEADS, MLA_NOPE + MLA_V)
    k_nope, v = kv[..., :MLA_NOPE], kv[..., MLA_NOPE:]
    k_pe = apply_rope(k_pe, cos, sin)
    scale = (MLA_NOPE + MLA_ROPE) ** -0.5
    nq = S // Q_BLOCK
    qn_b = q_nope.reshape(B, nq, Q_BLOCK, MLA_HEADS, MLA_NOPE).swapaxes(0, 1)
    qp_b = q_pe.reshape(B, nq, Q_BLOCK, MLA_HEADS, MLA_ROPE).swapaxes(0, 1)

    def block(args):
        qn, qp = args
        s = (jnp.einsum('bqhd,bkhd->bhqk', qn, k_nope)
             + jnp.einsum('bqhr,bkr->bhqk', qp, k_pe))
        p = jax.nn.softmax(s.astype(jnp.float32) * scale, axis=-1).astype(v.dtype)
        return jnp.einsum('bhqk,bkhd->bqhd', p, v)

    o = lax.map(block, (qn_b, qp_b))
    o = o.swapaxes(0, 1).reshape(B, S, MLA_HEADS * MLA_V)
    return o @ w_o

def conv_branch(u, w_dw, b_dw, ln_g, ln_b, w_pw):
    a, gate = jnp.split(u, 2, axis=-1)
    a = a * jax.nn.sigmoid(gate)
    y = lax.conv_general_dilated(
        a, w_dw[:, None, :].astype(a.dtype), window_strides=(1,),
        padding=[(CONV_WIDTH // 2, CONV_WIDTH // 2)],
        dimension_numbers=('NWC', 'WIO', 'NWC'), feature_group_count=CONV_CH) + b_dw
    y = jax.nn.silu(layer_norm(y, ln_g, ln_b))
    return y @ w_pw

def retention_direction(q, k, v, log_gamma, strict):
    C = q.shape[3]
    idx = jnp.arange(C, dtype=jnp.float32)
    diff = idx[:, None] - idx[None, :]
    mask = (diff > 0) if strict else (diff >= 0)
    lg = log_gamma[:, None, None]
    decay = jnp.where(mask, jnp.exp(jnp.where(mask, diff, 0.0) * lg), 0.0).astype(q.dtype)
    scores = jnp.einsum('bhnqd,bhnkd->bhnqk', q, k) * decay[None, :, None]
    inner = jnp.einsum('bhnqk,bhnke->bhnqe', scores, v)
    k_dec = k * jnp.exp((C - 1 - idx)[None, :] * log_gamma[:, None]).astype(k.dtype)[None, :, None, :, None]
    u = jnp.einsum('bhnkd,bhnke->nbhde', k_dec, v)
    chunk_decay = jnp.exp(C * log_gamma).astype(u.dtype)[None, :, None, None]

    def step(state, xs):
        q_c, u_c = xs
        out = jnp.einsum('bhqd,bhde->bhqe', q_c, state)
        return chunk_decay * state + u_c, out

    state0 = jnp.zeros(u.shape[1:], u.dtype)
    _, cross = lax.scan(step, state0, (jnp.moveaxis(q, 2, 0), u))
    cross = jnp.moveaxis(cross, 0, 2) * jnp.exp((idx + 1)[None, :] * log_gamma[:, None]).astype(q.dtype)[None, :, None, :, None]
    return inner + cross

def retention_branch(q, k, v, g, cos, sin, decay_logits, gn_g, w_o):
    B, S, _ = q.shape
    nc = S // RET_CHUNK
    q = apply_rope(q.reshape(B, S, RET_HEADS, RET_DK), cos, sin)
    k = apply_rope(k.reshape(B, S, RET_HEADS, RET_DK), cos, sin) * (RET_DK ** -0.5)
    v = v.reshape(B, S, RET_HEADS, RET_DV)

    def chunked(t):
        return t.reshape(B, nc, RET_CHUNK, RET_HEADS, -1).transpose(0, 3, 1, 2, 4)

    def unchunk(t):
        return t.transpose(0, 2, 3, 1, 4).reshape(B, S, RET_HEADS, -1)

    def flip(t):
        return jnp.flip(t, axis=1)

    log_gamma = jax.nn.log_sigmoid(decay_logits.astype(jnp.float32))
    fwd = retention_direction(chunked(q), chunked(k), chunked(v), log_gamma[0], False)
    bwd = retention_direction(chunked(flip(q)), chunked(flip(k)), chunked(flip(v)), log_gamma[1], True)
    o = unchunk(fwd) + flip(unchunk(bwd))
    of = o.astype(jnp.float32)
    mu = jnp.mean(of, -1, keepdims=True)
    var = jnp.mean(jnp.square(of - mu), -1, keepdims=True)
    on = ((of - mu) * lax.rsqrt(var + EPS)).reshape(B, S, RET_HEADS * RET_DV)
    on = (on * gn_g.astype(jnp.float32)).astype(g.dtype)
    return (jax.nn.silu(g) * on) @ w_o

def second_inputs(seed: int = 0) -> dict:
    key = jax.random.key(seed)
    ks = jax.random.split(key, 32)
    f32 = jnp.float32

    def w(k, shape, fan_in):
        return jax.random.normal(k, shape, f32) * (fan_in ** -0.5)

    def gain(k, shape):
        return 1.0 + 0.02 * jax.random.normal(k, shape, f32)

    def bias(k, shape):
        return 0.02 * jax.random.normal(k, shape, f32)

    L = DEPTH
    x = jax.random.normal(ks[0], (BATCH, SEQ, D_MODEL), f32)
    offset = jax.random.randint(ks[1], (BATCH, 1), 0, SEQ, dtype=jnp.int32)
    positions = offset + jnp.arange(SEQ, dtype=jnp.int32)[None, :]
    k_exp = 5.0 + jnp.arange(RET_HEADS, dtype=f32)
    base_logit = jnp.log(jnp.exp2(k_exp) - 1.0)
    ret_decay_logits = base_logit[None, None, :] + 0.1 * jax.random.normal(ks[2], (L, 2, RET_HEADS), f32)
    return {
        "x": x,
        "positions": positions,
        "ln_mix_pre": gain(ks[3], (L, D_MODEL)),
        "ln_mix_post": gain(ks[4], (L, D_MODEL)),
        "ln_ffn_pre": gain(ks[5], (L, D_MODEL)),
        "ln_ffn_post": gain(ks[6], (L, D_MODEL)),
        "w_in": w(ks[7], (L, D_MODEL, IN_COLS), D_MODEL),
        "mla_q_norm": gain(ks[8], (L, MLA_Q_RANK)),
        "mla_w_uq": w(ks[9], (L, MLA_Q_RANK, MLA_HEADS * (MLA_NOPE + MLA_ROPE)), MLA_Q_RANK),
        "mla_kv_norm": gain(ks[10], (L, MLA_KV_RANK)),
        "mla_w_ukv": w(ks[11], (L, MLA_KV_RANK, MLA_HEADS * (MLA_NOPE + MLA_V)), MLA_KV_RANK),
        "mla_w_o": w(ks[12], (L, MLA_HEADS * MLA_V, D_MODEL), MLA_HEADS * MLA_V),
        "conv_w_dw": w(ks[13], (L, CONV_WIDTH, CONV_CH), CONV_WIDTH),
        "conv_b_dw": bias(ks[14], (L, CONV_CH)),
        "conv_ln_g": gain(ks[15], (L, CONV_CH)),
        "conv_ln_b": bias(ks[16], (L, CONV_CH)),
        "conv_w_pw": w(ks[17], (L, CONV_CH, D_MODEL), CONV_CH),
        "ret_decay_logits": ret_decay_logits,
        "ret_gn_g": gain(ks[18], (L, RET_HEADS * RET_DV)),
        "ret_w_o": w(ks[19], (L, RET_HEADS * RET_DV, D_MODEL), RET_HEADS * RET_DV),
        "w_out": w(ks[20], (L, D_MODEL, D_MODEL), D_MODEL),
        "ffn_w_gate": w(ks[21], (L, D_MODEL, FFN_HIDDEN), D_MODEL),
        "ffn_w_up": w(ks[22], (L, D_MODEL, FFN_HIDDEN), D_MODEL),
        "ffn_w_down": w(ks[23], (L, FFN_HIDDEN, D_MODEL), FFN_HIDDEN),
    }

def second_block(x, positions, ln_mix_pre, ln_mix_post, ln_ffn_pre, ln_ffn_post, w_in,
              mla_q_norm, mla_w_uq, mla_kv_norm, mla_w_ukv, mla_w_o,
              conv_w_dw, conv_b_dw, conv_ln_g, conv_ln_b, conv_w_pw,
              ret_decay_logits, ret_gn_g, ret_w_o, w_out,
              ffn_w_gate, ffn_w_up, ffn_w_down):
    B, S, _ = x.shape
    points = np.cumsum(IN_SPLITS)[:-1].tolist()
    cos_m, sin_m = rope_tables(positions, MLA_ROPE)
    cos_r, sin_r = rope_tables(positions, RET_DK)
    for l in range(DEPTH):
        h = rms_norm_2(x, ln_mix_pre[l])
        proj = h @ w_in[l]
        c_q, c_kv, k_pe, conv_u, r_q, r_k, r_v, r_g, gate_logits = jnp.split(proj, points, axis=-1)
        y_mla = mla_branch(c_q, c_kv, k_pe, cos_m, sin_m, mla_q_norm[l], mla_w_uq[l],
                           mla_kv_norm[l], mla_w_ukv[l], mla_w_o[l])
        y_conv = conv_branch(conv_u, conv_w_dw[l], conv_b_dw[l], conv_ln_g[l], conv_ln_b[l], conv_w_pw[l])
        y_ret = retention_branch(r_q, r_k, r_v, r_g, cos_r, sin_r, ret_decay_logits[l],
                                 ret_gn_g[l], ret_w_o[l])
        gates = jax.nn.sigmoid(gate_logits).reshape(B, S, N_BRANCH, D_MODEL)
        merged = gates[:, :, 0] * y_mla + gates[:, :, 1] * y_conv + gates[:, :, 2] * y_ret
        x = x + rms_norm_2(merged @ w_out[l], ln_mix_post[l])
        h = rms_norm_2(x, ln_ffn_pre[l])
        f = (jax.nn.silu(h @ ffn_w_gate[l]) * (h @ ffn_w_up[l])) @ ffn_w_down[l]
        x = x + rms_norm_2(f, ln_ffn_post[l])
    return x


def setup_inputs(seed=0):
    out = dict(first_inputs(seed))
    for name, value in second_inputs(seed + 1).items():
        if name != "x":
            out[name + "_2"] = value
    return out


def reference(
    x, norm_g, ssm_w_in, ssm_a_re, ssm_a_im, ssm_log_dt, ssm_b_re, ssm_b_im, ssm_c_re, ssm_c_im,
    ssm_d, ssm_w_glu, ssm_b_glu, ssm_w_out, attn_w_in, attn_q_gain, attn_k_gain, attn_w_out,
    positions_2, ln_mix_pre_2, ln_mix_post_2, ln_ffn_pre_2, ln_ffn_post_2, w_in_2, mla_q_norm_2,
    mla_w_uq_2, mla_kv_norm_2, mla_w_ukv_2, mla_w_o_2, conv_w_dw_2, conv_b_dw_2, conv_ln_g_2,
    conv_ln_b_2, conv_w_pw_2, ret_decay_logits_2, ret_gn_g_2, ret_w_o_2, w_out_2, ffn_w_gate_2,
    ffn_w_up_2, ffn_w_down_2,
):
    x = first_block(
        x, norm_g, ssm_w_in, ssm_a_re, ssm_a_im, ssm_log_dt, ssm_b_re, ssm_b_im, ssm_c_re,
        ssm_c_im, ssm_d, ssm_w_glu, ssm_b_glu, ssm_w_out, attn_w_in, attn_q_gain, attn_k_gain,
        attn_w_out,
    )
    return second_block(
        x, positions_2, ln_mix_pre_2, ln_mix_post_2, ln_ffn_pre_2, ln_ffn_post_2, w_in_2,
        mla_q_norm_2, mla_w_uq_2, mla_kv_norm_2, mla_w_ukv_2, mla_w_o_2, conv_w_dw_2,
        conv_b_dw_2, conv_ln_g_2, conv_ln_b_2, conv_w_pw_2, ret_decay_logits_2, ret_gn_g_2,
        ret_w_o_2, w_out_2, ffn_w_gate_2, ffn_w_up_2, ffn_w_down_2,
    )


_drawn_inputs = setup_inputs


def setup_inputs(seed=0):
    import zlib

    import numpy as np

    out = dict(_drawn_inputs(seed))
    spreads = {}
    factors = {'norm_g': 3.538,
     'ssm_a_re': 43.493,
     'ssm_b_glu': 8.0,
     'attn_q_gain': 8.0,
     'attn_k_gain': 8.0,
     'ln_ffn_post_2': 16.783,
     'mla_q_norm_2': 21.819,
     'mla_kv_norm_2': 8.0,
     'conv_ln_g_2': 22.512,
     'conv_ln_b_2': 23.856,
     'ret_gn_g_2': 27.552,
     'ln_mix_post_2': 8.0,
     'ln_ffn_pre_2': 3.658,
     'conv_b_dw_2': 8.0,
     'ret_decay_logits_2': 29.72}
    for name, (base, spread) in spreads.items():
        noise = np.random.default_rng([zlib.crc32(name.encode()), seed]).standard_normal(out[name].shape)
        drawn = base * np.exp(spread * noise) if base else spread * noise
        out[name] = __import__('jax').numpy.asarray(drawn.astype(out[name].dtype))
    for name, factor in factors.items():
        out[name] = (out[name] * factor).astype(out[name].dtype)
    return out
```

```python
import math
from contextlib import ExitStack

import numpy as np

import concourse.bass as bass
from concourse import mybir

F32 = mybir.dt.float32
F32R = mybir.dt.float32r
I32 = mybir.dt.int32
ALU = mybir.AluOpType
ACT = mybir.ActivationFunctionType
AX = mybir.AxisListType.X

P = 128
SEQ = 256
TT = SEQ // P
D = 1024
DT = D // P
EPS = 1e-6

GROUPS, GROUP, STATE = 64, 16, 64
SUB = 8
NSUB = SEQ // SUB
Q = GROUPS // 2
PARTS = 4
PQ = Q // PARTS
PCOLS = D // PARTS
JB = P // NSUB
GB = GROUPS // PARTS // JB

HEADS, HD = 8, 128
ROT = HD // 4
DEPTH2 = 2
MLA_H, NOPE, ROPE, MV = 8, 64, 32, 64
MQK = NOPE + ROPE
QR, KVR = 256, 128
CONV, TAPS = 512, 31
PAD = TAPS // 2
RH, RDK, RDV = 4, 128, 256
HID = 2816
HT = HID // P
FCH = 256

R = 4
SLOT = 1024


def weight_plan():
    chunks = []

    def add(name, n, width, ktiles):
        slots = [(k, min(2, ktiles - k)) for k in range(0, ktiles, 2)]
        for i in range(n):
            chunks.append((f"{name}{i}", width, slots))

    add("ssm_in.", 4, 512, DT)
    add("glu.", 2, 512, DT)
    add("ssm_out.", 2, 512, DT)
    add("attn_in.", 8, 512, DT)
    add("attn_out.", 2, 512, DT)
    for l in range(DEPTH2):
        add(f"L{l}.lat.", 1, QR + KVR + ROPE, DT)
        add(f"L{l}.glu.", 2, 512, DT)
        add(f"L{l}.uq.", 2, 384, QR // P)
        add(f"L{l}.ukv.", 2, 512, KVR // P)
        add(f"L{l}.ret.", 6, 512, DT)
        add(f"L{l}.gate.", 6, 512, DT)
        add(f"L{l}.mla_o.", 2, 512, 4)
        add(f"L{l}.conv_o.", 2, 512, 4)
        add(f"L{l}.ret_o.", 2, 512, DT)
        add(f"L{l}.out.", 2, 512, DT)
        add(f"L{l}.ffn.", HID // FCH, 2 * FCH, DT)
        add(f"L{l}.down.", 2, 512, HT)
    slot, off, table, slots = 0, 0, {}, []
    for c, (name, width, parts) in enumerate(chunks):
        table[name] = dict(index=c, width=width, first=slot, n=len(parts))
        for k, nk in parts:
            slots.append(dict(chunk=name, k=k, nk=nk, width=width, off=off))
            off += P * nk * width
            slot += 1
    return table, slots, off


def rope_tables_host(dim, theta, n):
    half = dim // 2
    inv = (np.float32(theta) ** (-(np.arange(half, dtype=np.float32) * np.float32(2.0)) / np.float32(dim))).astype(np.float32)
    ang = np.arange(n, dtype=np.float32)[:, None] * inv[None, :]
    return np.cos(ang.astype(np.float64)).astype(np.float32), np.sin(ang.astype(np.float64)).astype(np.float32)


C_ID, C_MASK = 0, 128
C_COS1 = C_MASK + TT * SEQ
C_SIN1 = C_COS1 + TT * ROT // 2
C_DF = C_SIN1 + TT * ROT // 2
C_DB = C_DF + TT * SEQ
C_INVR = C_DB + TT * SEQ
C_INVM = C_INVR + RDK // 2
N_CONST = C_INVM + ROPE // 2
N_ANG = GROUPS // 2 + RDK + ROPE

NORMS = ["hn", "h1"] + [f"L{l}.{n}" for l in range(DEPTH2) for n in ("h", "h2")]


def shape_constants():
    c = np.zeros((P, N_CONST), np.float32)
    c[:, C_ID:C_ID + P] = np.eye(P, dtype=np.float32)
    q = np.arange(SEQ).reshape(TT, P).T
    k = np.arange(SEQ)
    c[:, C_MASK:C_MASK + TT * SEQ] = np.where(k[None, None, :] <= q[:, :, None], 0.0, -1e30).reshape(P, -1)
    cos, sin = rope_tables_host(ROT, 500000.0, SEQ)
    c[:, C_COS1:C_SIN1] = cos.reshape(TT, P, -1).transpose(1, 0, 2).reshape(P, -1)
    c[:, C_SIN1:C_DF] = sin.reshape(TT, P, -1).transpose(1, 0, 2).reshape(P, -1)
    c[:, C_DF:C_DB] = np.maximum(k[None, None, :] - q[:, :, None], 0).reshape(P, -1)
    c[:, C_DB:C_INVR] = np.maximum(q[:, :, None] - k[None, None, :], 0).reshape(P, -1)
    base = np.float32(10000.0)
    c[:, C_INVR:C_INVM] = (base ** (-np.arange(0, RDK, 2, dtype=np.float32) / np.float32(RDK)))[None]
    c[:, C_INVM:N_CONST] = (base ** (-np.arange(0, ROPE, 2, dtype=np.float32) / np.float32(ROPE)))[None]
    return c


TWO_PI = 2.0 * math.pi
PI_A = 6.28125
PI_B = float(np.float32(round((TWO_PI - PI_A) * 2.0 ** 21) / 2.0 ** 21))
PI_C = TWO_PI - PI_A - PI_B
ROUND = 12582912.0
PI_IN = 3.1415925



class Count:

    def __init__(self):
        self.n = 0

    def __call__(self):
        self.n += 1
        return 1


def build(nc, stream, consts, x_in, ssm_ab, ssm_ldt, ssm_bc, rows, qk_gain, positions, decay, conv_p, lat_gain, out):
    table, slots, _ = weight_plan()
    NS = len(slots)
    u_scr = nc.dram_tensor("u_scratch", [SEQ, D], F32, kind="Internal").ap()
    y_scr = nc.dram_tensor("y_scratch", [SEQ, D], F32, kind="Internal").ap()

    ctx = ExitStack()
    with ctx:
        def sb(name, shape, dt=F32, scope=None):
            return (scope or ctx).enter_context(nc.sbuf_tensor(name, shape, dt))

        def sem(name):
            return ctx.enter_context(nc.semaphore(name))

        raw = sb("weights_raw", [P, R, SLOT])
        w_hi = sb("weights_hi", [P, R, SLOT], F32R)
        w_lo = sb("weights_lo", [P, R, SLOT], F32R)
        cst = sb("consts", [P, N_CONST])
        ident = cst[:, C_ID:C_ID + P]
        xT = sb("x_T", [P, TT, D])
        hT = sb("h_T", [P, TT, D])
        f_hi = sb("act_F_hi", [P, DT, SEQ], F32R)
        f_lo = sb("act_F_lo", [P, DT, SEQ], F32R)
        gains = sb("gains", [P, 2, D])
        junk = sb("junk", [P, D])
        stat = sb("stat", [P, 256])
        minus_half = sb("minus_half", [P, 16])
        lg = sb("log_gamma", [P, 16])
        lgw = sb("log_gamma_work", [P, 6, 16])
        rcs = sb("ret_cos_sin", [P, 2, TT, RDK // 2])
        mcs = sb("mla_cos_sin", [P, 2, TT, ROPE // 2])
        posf = sb("positions_f", [P, TT])
        posi = sb("positions_i", [P, TT], I32)

        with ExitStack() as s1:
            uT = sb("u_T", [P, TT, D], F32, s1)
            zT = sb("z_T", [P, TT, D], F32, s1)
            ab = sb("ssm_ab", [P, 2, Q], F32, s1)
            pdt = sb("ssm_dt", [P, Q], F32, s1)
            par = sb("ssm_par", [P, 20, Q], F32, s1)
            pw = sb("powers", [P, 2, SUB + 1, Q], F32, s1)
            pwb = sb("powers_reversed", [P, 2, SUB, Q], F32, s1)
            bc = sb("ssm_bc", [P, 4, GROUP, Q], F32, s1)
            fb = sb("ssm_fb", [P, 2, GROUP, Q], F32, s1)
            turn = sb("turns", [P, 2, Q, NSUB], F32, s1)
            rho = sb("decays", [P, Q, NSUB], F32, s1)
            bm = sb("b_mats", [P, 2, PQ, SUB * GROUP], F32, s1)
            cm = sb("c_mats", [P, 2, PQ, SUB * GROUP], F32, s1)
            tmp = sb("mat_tmp", [P, PQ, SUB, GROUP], F32, s1)
            bt = sb("b_mats_T", [P, 2, PQ, P], F32, s1)
            kts = sb("taps_T", [P, PQ, 2, GROUP], F32, s1)
            mm = sb("toeplitz", [P, SUB, PCOLS], F32, s1)
            uk = sb("u_sub", [P, SUB, GB * GROUP], F32, s1)
            uo = sb("u_by_group", [P, GB, SUB, GROUP], F32, s1)
            ug = sb("u_groups", [P, GB, P], F32, s1)
            sw = sb("scan_work", [P, 4, PQ, NSUB], F32, s1)
            st = sb("states", [P, 2, PQ, NSUB], F32, s1)
            yk = sb("y_sub", [P, SUB, GB * GROUP], F32, s1)
            gw = sb("gelu_work", [P, TT, PCOLS], F32, s1)
            tmp2 = sb("c_mat_tmp", [P, PQ, SUB, GROUP], F32, s1)
            ev = sb("turn_step", [P, 4, Q], F32, s1)
            yT = hT
        with ExitStack() as s2:
            qT = sb("q_T", [P, TT, D], F32, s2)
            kT = sb("k_T", [P, TT, D], F32, s2)
            vT = sb("v_T", [P, TT, D], F32, s2)
            szT = sb("silu_z_T", [P, TT, D], F32, s2)
            qkg = sb("qk_gain", [P, 2, HD], F32, s2)
            sq = sb("squares", [P, TT, 512], F32, s2)
            ropt = sb("rope_tmp", [P, TT, 4, 64], F32, s2)
            a_qk = sb("a_qk_F", [P, 2, 512], F32, s2)
            a_s = sb("a_scores", [P, 2, TT, SEQ], F32, s2)
            a_p = sb("a_probs", [P, 2, TT, SEQ], F32, s2)
            a_pt = sb("a_probs_T", [P, 2, TT, TT, P], F32, s2)
            a_st = sb("a_stat", [P, 2, 8], F32, s2)
        with ExitStack() as s3:
            h2_hi = sb("ffn_F_hi", [P, HT, SEQ], F32R, s3)
            h2_lo = sb("ffn_F_lo", [P, HT, SEQ], F32R, s3)
            ft = sb("ffn_tanh_rows", [P, 2, TT, FCH], F32, s3)
            fh = sb("ffn_h", [P, 2, TT, FCH], F32, s3)
        with ExitStack() as s4:
            latp = sb("lat_gain", [P, QR + KVR], F32, s4)
            cfp = sb("conv_params", [P, 4, TAPS + 3], F32, s4)
            c_hi = sb("lat_F_hi", [P, 3, SEQ], F32R, s4)
            c_lo = sb("lat_F_lo", [P, 3, SEQ], F32R, s4)
            mo = sb("mla_o_T", [P, TT, MLA_H, MV], F32, s4)
            ga = sb("conv_a", [P, TT, CONV], F32, s4)
            gt = sb("conv_tanh", [P, TT, CONV], F32, s4)
            cp = sb("conv_in_F", [P, 4, SEQ + 2 * PAD], F32, s4)
            cacc = sb("conv_acc_F", [P, 4, SEQ], F32, s4)
            bns = sb("bn_stats", [P, 10, 8], F32, s4)
            rqT = sb("ret_q_T", [P, TT, 512], F32, s4)
            rkT = sb("ret_k_T", [P, TT, 512], F32, s4)
            rg = sb("ret_g_T", [P, TT, D], F32, s4)
            gat = sb("gates_T", [P, 3, TT, D], F32, s4)
            with ExitStack() as s5:
                cT = sb("lat_T", [P, TT, QR + KVR + ROPE], F32, s5)
                cnT = sb("lat_norm_T", [P, TT, QR + KVR], F32, s5)
                mq = sb("mla_q_T", [P, TT, MLA_H, MQK], F32, s5)
                mk = sb("mla_k_T", [P, TT, MLA_H, MQK], F32, s5)
                mv = sb("mla_v_T", [P, TT, MLA_H, MV], F32, s5)
                mt = sb("mla_rope_tmp", [P, 4, MLA_H, ROPE // 2], F32, s5)
                m_qk = sb("m_qk_F", [P, 2, 512], F32, s5)
                m_p = sb("m_probs", [P, 2, TT, SEQ], F32, s5)
                m_pt = sb("m_probs_T", [P, 2, TT, TT, P], F32, s5)
                m_st = sb("m_stat", [P, 2, 8], F32, s5)
            with ExitStack() as s6:
                r_qk = sb("r_qk_F", [P, RH, 512], F32, s6)
                r_s = sb("r_scores_T", [P, 2, TT, SEQ], F32, s6)
                r_d = sb("r_decay_T", [P, RH, TT, SEQ], F32, s6)
        rv = hT

        acc = [[ctx.enter_context(nc.psum_tensor(f"acc{p}{t}", [P, 512], F32)) for t in range(TT)] for p in range(2)]
        tp = [ctx.enter_context(nc.psum_tensor(f"turned{i}", [P, 512], F32)) for i in range(2)]
        mx = [ctx.enter_context(nc.psum_tensor(f"mixed{i}", [P, 512], F32)) for i in range(2)]

        consts_in, x_ld, ssm_in = sem("consts_in"), sem("x_in"), sem("ssm_in")
        raw_in = [sem(f"weights_in{i}") for i in range(R)]
        hi_made = sem("weights_hi_made")
        lo_made = sem("weights_lo_made")
        slot_used = sem("slots_used")
        turned = sem("turned_ready")
        turned_hi = sem("turned_hi_made")
        turned_lo = sem("turned_lo_made")
        mixed = sem("mixed_ready")

        dt_exp = sem("dt_exp")
        norm_sums = sem("norm_sums")
        norm_roots = sem("norm_roots")
        rows_normed = sem("rows_normed")
        ssm_rates = sem("ssm_rates")
        ssm_mag = sem("ssm_mag")
        decay_abs = sem("decay_abs")
        decay_exp = sem("decay_exp")
        angles = sem("angles")
        sines = sem("sines")
        turn_base = sem("turn_base")
        turns_made = sem("turns_made")
        powers_made = sem("powers_made")
        c_negated = sem("c_negated")
        minus_half_set = sem("minus_half_set")
        toeplitz_zero = sem("toeplitz_zero")
        b_mats_made = sem("b_mats_made")
        c_mats_made = sem("c_mats_made")
        taps_copied = sem("taps_copied")
        b_T_copied = sem("b_T_copied")
        u_copied = sem("u_copied")
        z_tanh = sem("z_tanh")
        z_silu = sem("z_silu")
        u_ordered = sem("u_ordered")
        u_groups_copied = sem("u_groups_copied")
        state_terms_read = sem("state_terms_read")
        states_made = sem("states_made")
        y_copied = sem("y_copied")
        gelu_in = sem("gelu_in")
        gelu_tanh_made = sem("gelu_tanh_made")
        gelu_made = sem("gelu_made")
        glu_biased = sem("glu_biased")
        glu_tanh = sem("glu_tanh")
        glu_rows_half = sem("glu_rows_half")
        glu_rows = sem("glu_rows")
        x_updated = sem("x_updated")
        squares_made = sem("squares_made")
        squares_summed = sem("squares_summed")
        qk_roots = sem("qk_roots")
        attn_qk_roped = sem("attn_qk_roped")
        v_copied = sem("v_copied")
        attn_z_tanh = sem("attn_z_tanh")
        attn_z_silu = sem("attn_z_silu")
        attn_rows = sem("attn_rows")
        qk_copied = sem("qk_copied")
        scores_masked = sem("scores_masked")
        max_found = sem("max_found")
        probs_made = sem("probs_made")
        probs_T_copied = sem("probs_T_copied")
        outs_scaled = sem("outs_scaled")
        lat_copied = sem("lat_copied")
        lat_sums = sem("lat_sums")
        lat_roots = sem("lat_roots")
        lat_rows = sem("lat_rows")
        conv_a_copied = sem("conv_a_copied")
        conv_tanh_made = sem("conv_tanh_made")
        conv_glu_rows = sem("conv_glu_rows")
        conv_in = sem("conv_in")
        pads_zero = sem("pads_zero")
        conv_summed = sem("conv_summed")
        conv_stats = sem("conv_stats")
        conv_roots = sem("conv_roots")
        conv_normed = sem("conv_normed")
        conv_affine = sem("conv_affine")
        conv_out_tanh = sem("conv_out_tanh")
        conv_silu = sem("conv_silu")
        conv_hi = sem("conv_hi")
        conv_split = sem("conv_split")
        mla_q_copied = sem("mla_q_copied")
        mla_v_copied = sem("mla_v_copied")
        mla_roped = sem("mla_roped")
        ret_rope_read = sem("ret_rope_read")
        ret_roped = sem("ret_roped")
        ret_v_copied = sem("ret_v_copied")
        ret_g_tanh = sem("ret_g_tanh")
        ret_g_silu = sem("ret_g_silu")
        ret_qk_copied = sem("ret_qk_copied")
        decay_args = sem("decay_args")
        decays_made = sem("decays_made")
        ret_scores = sem("ret_scores")
        ret_o_copied = sem("ret_o_copied")
        ret_stats = sem("ret_stats")
        ret_roots = sem("ret_roots")
        ret_rows = sem("ret_rows")
        gate_tanh = sem("gate_tanh")
        mla_weighed = sem("mla_weighed")
        conv_weighed = sem("conv_weighed")
        ret_weighed = sem("ret_weighed")
        merged = sem("merged")
        mix_copied = sem("mix_copied")
        ffn_copied = sem("ffn_copied")
        post_sums = sem("post_sums")
        post_roots = sem("post_roots")
        x_normed = sem("x_normed")
        ffn_tanh = sem("ffn_tanh")
        ffn_rows = sem("ffn_rows")
        decay_in = sem("decay_in")
        ssm_mats_in = sem("ssm_mats_in")
        u_sub_in = sem("u_sub_in")
        toeplitz_in = sem("toeplitz_in")
        y_stored = sem("y_stored")
        y_in = sem("y_in")
        qk_gain_in = sem("qk_gain_in")
        layer_params_in = sem("layer_params_in")
        out_stored = sem("out_stored")
        dve_steps = sem("dve_steps")
        pool_steps = sem("pool_steps")
        u_stored = [sem(f"u_stored{i}") for i in range(2)]

        mix_at, turn_at = {}, {}

        stat_cols = {}

        def stats_of(name, n):
            if name not in stat_cols:
                stat_cols[name] = (sum(k for _, k in stat_cols.values()), n)
            a = stat_cols[name][0]
            return stat[:, a:a + n]

        def split_name(name):
            layer = int(name[1]) if name[0] == "L" else 0
            kind = name.split(".", 1)[1] if name[0] == "L" else name
            base = kind.rstrip("0123456789")
            return layer, base, int(kind[len(base):])

        def reader_of(name, t):
            l, kind, i = split_name(name)
            n = 2 * i + t + 1
            return {
                "ssm_in.": (u_copied, n) if i < 2 else (z_silu, n - 4),
                "glu.": ((glu_biased, n) if name[0] != "L" else
                         (conv_a_copied, 2 * l + t + 1) if i == 0 else (conv_tanh_made, 2 * l + t + 1)),
                "ssm_out.": (x_updated, n), "attn_out.": (x_updated, 4 + n),
                "attn_in.": (squares_made, n) if i < 4 else (v_copied, n - 8) if i < 6 else (attn_z_silu, n - 12),
                "lat.": (lat_copied, 2 * l + t + 1),
                "uq.": (mla_q_copied, 4 * l + n), "ukv.": (mla_v_copied, 4 * l + n),
                "ret.": ((ret_rope_read, 4 * l + n) if i < 2 else (ret_v_copied, 4 * l + n - 4) if i < 4
                         else (ret_g_silu, 4 * l + n - 8)),
                "gate.": (gate_tanh, 12 * l + n),
                "mla_o.": (mla_weighed, 4 * l + n), "conv_o.": (conv_weighed, 4 * l + n),
                "ret_o.": (ret_weighed, 4 * l + n),
                "out.": (mix_copied, 4 * l + n), "down.": (ffn_copied, 4 * l + n),
                "ffn.": (ffn_rows, HT * l + n),
            }[kind]

        GAINS = [("norm0", rows_normed, 2), ("d_skip", gelu_made, 4), ("b_glu", glu_biased, 4),
                 ("norm1", rows_normed, 4)]
        for l in range(DEPTH2):
            GAINS += [(f"L{l}.mix_pre", rows_normed, 6 + 4 * l), (f"L{l}.gn", ret_rows, 2 * l + 2),
                      (f"L{l}.mix_post", x_normed, 4 * l + 2), (f"L{l}.ffn_pre", rows_normed, 8 + 4 * l),
                      (f"L{l}.ffn_post", x_normed, 4 * l + 4)]
        gain_no = {g[0]: n for n, g in enumerate(GAINS)}
        gain_in = [sem(f"gain_in{i}") for i in range(2)]

        def gain_row(eng, name):
            n = gain_no[name]
            eng.wait_ge(gain_in[n % 2], 16 * (n // 2 + 1))
            return gains[:, n % 2, :]

        def chunks_ending(a, b):
            return [(n, c["first"] + c["n"]) for n, c in table.items() if a < c["first"] + c["n"] <= b]

        def splitter(make):
            state = [0]

            def upto(n):
                while state[0] < min(n, NS):
                    make(state[0])
                    state[0] += 1
            return upto

        def banks_of(eng, name):
            c = table[name]
            eng.wait_ge(slot_used, c["first"] + c["n"])
            return [acc[c["index"] % 2][t][:, 0:c["width"]] for t in range(TT)]

        block = ctx.enter_context(nc.Block())

        @block.tensor
        def _(pe):
            pos = 0
            acc_user = [None, None]
            mix_user = [None, None]

            def f_tiles(chunk):
                if ".uq." in chunk:
                    return c_hi, c_lo, 0
                if ".ukv." in chunk:
                    return c_hi, c_lo, QR // P
                if ".down." in chunk:
                    return h2_hi, h2_lo, 0
                if ".conv_o." in chunk:
                    return f_hi, f_lo, 4
                return f_hi, f_lo, 0

            def run(n):
                nonlocal pos
                for _ in range(n):
                    s = slots[pos]
                    c = table[s["chunk"]]
                    par, w = c["index"] % 2, s["width"]
                    hi, lo, k0 = f_tiles(s["chunk"])
                    first, last = pos == c["first"], pos == c["first"] + c["n"] - 1
                    pe.wait_ge(lo_made, pos + 1)
                    for t in range(TT):
                        if first and acc_user[par]:
                            who, value = reader_of(acc_user[par], t)
                            pe.wait_ge(who, value)
                        for kk in range(s["nk"]):
                            k = k0 + s["k"] + kk
                            wh = w_hi[:, pos % R, kk * w:(kk + 1) * w]
                            wl = w_lo[:, pos % R, kk * w:(kk + 1) * w]
                            xh, xl = (f[:, k, t * P:(t + 1) * P] for f in (hi, lo))
                            o = acc[par][t][:, 0:w]
                            pe.matmul(o, xh, wh, start=first and kk == 0, stop=False)
                            pe.matmul(o, xl, wh, start=False, stop=False)
                            i = pe.matmul(o, xh, wl, start=False, stop=last and kk == s["nk"] - 1)
                    i.then_inc(slot_used, 1)
                    acc_user[par] = s["chunk"]
                    pos += 1

            def mix(name, who, value):
                n = len(mix_at)
                mix_at[name] = (n, pos)
                if mix_user[n % 2]:
                    pe.wait_ge(mix_user[n % 2][0], mix_user[n % 2][1])
                mix_user[n % 2] = (who, value)
                return mx[n % 2]

            def turn(name, ktiles, src, ready):
                for k in range(0, ktiles, 2):
                    n = len(turn_at)
                    turn_at[f"{name}.{k // 2}"] = (n, pos)
                    if n >= 2:
                        pe.wait_ge(turned_lo, n - 1)
                    for t in range(TT):
                        who, value = ready(t)
                        pe.wait_ge(who, value)
                        for kk in range(min(2, ktiles - k)):
                            i = pe.transpose(tp[n % 2][:, kk * SEQ + t * P:kk * SEQ + (t + 1) * P], src(t, k + kk), ident)
                    i.then_inc(turned, 1)

            def split_made():
                pe.wait_ge(turned_lo, len(turn_at))

            def tiles_of(tensor):
                return lambda t, k: tensor[:, t, k * P:(k + 1) * P]

            pe.wait_ge(consts_in, 16)
            turn("hn", DT, tiles_of(hT), lambda t: (rows_normed, t + 1))
            split_made()
            run(8)

            def taps_and_turned_b(qd):
                pe.wait_ge(b_mats_made, qd + 1)
                for e in range(2):
                    b = mix(f"ssm{qd}.taps{e}", taps_copied, 2 * qd + e + 1)
                    rowsel = slice(64 * e, 64 * e + 64)
                    for q in range(PQ):
                        o = b[:, q * GROUP:(q + 1) * GROUP]
                        pe.matmul(o, bm[rowsel, 0, q, :], bc[rowsel, 2, :, PQ * qd + q], start=True, stop=False)
                        i = pe.matmul(o, bm[rowsel, 1, q, :], bc[rowsel, 3, :, PQ * qd + q], start=False, stop=True)
                    i.then_inc(mixed, 1)
                for n in range(4):
                    b = mix(f"ssm{qd}.bt{n}", b_T_copied, 4 * qd + n + 1)
                    for k in range(4):
                        c, q = divmod(4 * n + k, PQ)
                        i = pe.transpose(b[:, k * P:(k + 1) * P], bm[:, c, q, :], ident)
                    i.then_inc(mixed, 1)

            taps_and_turned_b(0)
            for qd in range(PARTS):
                pe.wait_ge(u_ordered, qd + 1)
                b = mix(f"ssm{qd}.u", u_groups_copied, qd + 1)
                for g in range(GB):
                    i = pe.transpose(b[:, g * P:(g + 1) * P], uo[:, g, :, :].rearrange("p m c -> p (m c)"), ident)
                i.then_inc(mixed, 1)
                pe.wait_ge(b_T_copied, 4 * (qd + 1))
                pe.wait_ge(u_groups_copied, qd + 1)
                b = mix(f"ssm{qd}.b", state_terms_read, qd + 1)
                for j in range(JB):
                    for g in range(GB):
                        q, e = 2 * j + g // 2, g % 2
                        for c in range(2):
                            i = pe.matmul(b[64 * e:64 * e + 64, (c * PQ + q) * NSUB:(c * PQ + q + 1) * NSUB],
                                          bt[:, c, q, 64 * e:64 * e + 64], ug[:, g, j * NSUB:(j + 1) * NSUB],
                                          start=True, stop=True, skip_group_check=True)
                i.then_inc(mixed, 1)
                run(2)
                pe.wait_ge(toeplitz_in, 16 * SUB * (qd + 1))
                banks = [mix(f"ssm{qd}.y{e}", y_copied, 2 * qd + e + 1) for e in range(2)]
                for e in range(2):
                    for j in range(JB):
                        for g in range(e, GB, 2):
                            col = (GB * j + g) * GROUP
                            o = banks[e][32 * j:32 * j + 32, (g // 2) * P:(g // 2 + 1) * P]
                            pe.matmul(o, ug[:, g, j * NSUB:(j + 1) * NSUB], mm[:, :, col:col + GROUP],
                                      start=(g == e), stop=False, skip_group_check=True)
                pe.wait_ge(states_made, qd + 1)
                pe.wait_ge(c_mats_made, qd + 1)
                for e in range(2):
                    rowsel = slice(64 * e, 64 * e + 64)
                    for j in range(JB):
                        for g in range(e, GB, 2):
                            q = 2 * j + g // 2
                            o = banks[e][32 * j:32 * j + 32, (g // 2) * P:(g // 2 + 1) * P]
                            for c in range(2):
                                i = pe.matmul(o, st[rowsel, c, q, :], cm[rowsel, c, q, :], start=False,
                                              stop=(c == 1), skip_group_check=True)
                    i.then_inc(mixed, 1)
                if qd + 1 < PARTS:
                    taps_and_turned_b(qd + 1)
            turn("y", DT, tiles_of(yT), lambda t: (gelu_made, PARTS))
            split_made()
            run(8)
            turn("yg", DT, tiles_of(yT), lambda t: (glu_rows, 2 + t + 1))
            split_made()
            run(8)
            turn("h1", DT, tiles_of(hT), lambda t: (rows_normed, 2 + t + 1))
            split_made()
            run(16)

            def heads(tag, n_heads, dk, dv, src_q, src_k, src_v, qk, probs, probs_t, base, masked, v_ready, spare):
                def fill_gap():
                    nonlocal spare
                    n = min(2, spare)
                    run(n)
                    spare -= n

                for i in range(n_heads + 1):
                    h, done = i - 1, base + i
                    if i < n_heads:
                        b = mix(f"{tag}.qk{i}", qk_copied, done + 1)
                        for n, src in enumerate((src_q, src_k)):
                            for t in range(TT):
                                x = pe.transpose(b[0:dk, (2 * n + t) * P:(2 * n + t + 1) * P], src(t, i), ident)
                        x.then_inc(mixed, 1)
                    fill_gap()
                    if i > 0:
                        pe.wait_ge(probs_made, 2 * done)
                        b = mix(f"{tag}.pt{h}", probs_T_copied, done)
                        for qt in range(TT):
                            for kt in range(TT):
                                x = pe.transpose(b[:, (2 * qt + kt) * P:(2 * qt + kt + 1) * P],
                                                 probs[:, h % 2, qt, kt * P:(kt + 1) * P], ident)
                        x.then_inc(mixed, 1)
                    if i < n_heads:
                        pe.wait_ge(qk_copied, done + 1)
                        b = mix(f"{tag}.s{i}", *((scores_masked, done + 1) if masked else (probs_made, 2 * done + 2)))
                        for qt in range(TT):
                            x = pe.matmul(b[:, qt * SEQ:(qt + 1) * SEQ], qk[0:dk, i % 2, qt * P:(qt + 1) * P],
                                          qk[0:dk, i % 2, SEQ:2 * SEQ], start=True, stop=True)
                        x.then_inc(mixed, 1)
                    fill_gap()
                    if i > 0:
                        pe.wait_ge(probs_T_copied, done)
                        pe.wait_ge(v_copied if masked else mla_v_copied, v_ready(h))
                        b = mix(f"{tag}.o{h}", outs_scaled, 2 * done)
                        for qt in range(TT):
                            for kt in range(TT):
                                x = pe.matmul(b[:, qt * dv:(qt + 1) * dv], probs_t[:, h % 2, qt, kt, :],
                                              src_v(kt, h), start=(kt == 0), stop=(kt == TT - 1))
                        x.then_inc(mixed, 1)

            pe.wait_ge(attn_qk_roped, 8)
            heads("attn", HEADS, HD, HD, lambda t, h: qT[:, t, h * HD:(h + 1) * HD],
                  lambda t, h: kT[:, t, h * HD:(h + 1) * HD], lambda t, h: vT[:, t, h * HD:(h + 1) * HD],
                  a_qk, a_p, a_pt, 0, True, lambda h: 2 * (h // 4) + 2, 16)
            turn("attn_o", DT, tiles_of(hT), lambda t: (attn_rows, t + 1))
            split_made()
            run(8)
            for l in range(DEPTH2):
                turn(f"L{l}.h", DT, tiles_of(hT), lambda t: (rows_normed, 4 + 4 * l + t + 1))
                split_made()
                run(12)
                turn(f"L{l}.lat", 3, tiles_of(cnT), lambda t: (lat_rows, 2 * l + t + 1))
                split_made()
                run(12)
                pe.wait_ge(conv_glu_rows, TT * (l + 1))
                for n in range(2):
                    b = mix(f"L{l}.cin{n}", conv_in, 2 * l + n + 1)
                    for kk in range(2):
                        for t in range(TT):
                            k = 2 * n + kk
                            x = pe.transpose(b[:, kk * SEQ + t * P:kk * SEQ + (t + 1) * P], ga[:, t, k * P:(k + 1) * P], ident)
                    x.then_inc(mixed, 1)
                pe.wait_ge(mla_roped, 2 * TT * (l + 1))
                pe.wait_ge(mla_v_copied, 4 * (l + 1))
                heads(f"L{l}.mla", MLA_H, MQK, MV, lambda t, h: mq[:, t, h, :], lambda t, h: mk[:, t, h, :],
                      lambda t, h: mv[:, t, h, :], m_qk, m_p, m_pt, HEADS + MLA_H * l, False,
                      lambda h: 4 * (l + 1), 36)
                pe.wait_ge(ret_roped, 2 * TT * (l + 1))
                for h in range(RH):
                    b = mix(f"L{l}.rqk{h}", ret_qk_copied, RH * l + h + 1)
                    for n, src in enumerate((rqT, rkT)):
                        for t in range(TT):
                            x = pe.transpose(b[:, (2 * n + t) * P:(2 * n + t + 1) * P], src[:, t, h * RDK:(h + 1) * RDK], ident)
                    x.then_inc(mixed, 1)
                run(4)
                pe.wait_ge(ret_v_copied, 4 * (l + 1))
                for h in range(RH + 1):
                    if h < RH:
                        pe.wait_ge(ret_qk_copied, RH * l + h + 1)
                        b = mix(f"L{l}.rs{h}", ret_scores, RH * l + h + 1)
                        for m in range(TT):
                            x = pe.matmul(b[:, m * SEQ:(m + 1) * SEQ], r_qk[:, h, SEQ + m * P:SEQ + (m + 1) * P],
                                          r_qk[:, h, 0:SEQ], start=True, stop=True)
                        x.then_inc(mixed, 1)
                    if h > 0:
                        pe.wait_ge(ret_scores, RH * l + h)
                        b = mix(f"L{l}.ro{h - 1}", ret_o_copied, RH * l + h)
                        for n in range(TT):
                            for m in range(TT):
                                x = pe.matmul(b[:, n * RDV:(n + 1) * RDV], r_s[:, (h - 1) % 2, m, n * P:(n + 1) * P],
                                              rv[:, m, (h - 1) * RDV:h * RDV], start=(m == 0), stop=(m == TT - 1))
                        x.then_inc(mixed, 1)
                turn(f"L{l}.mo", 4, lambda t, k: mo[:, t, 2 * k:2 * k + 2, :].rearrange("p h d -> p (h d)"),
                     lambda t: (outs_scaled, 2 * (HEADS + MLA_H * (l + 1))))
                pe.wait_ge(conv_summed, l + 1)
                for t in range(TT):
                    b = mix(f"L{l}.cback{t}", conv_normed, 2 * l + t + 1)
                    for k in range(4):
                        x = pe.transpose(b[:, k * P:(k + 1) * P], cacc[:, k, t * P:(t + 1) * P], ident)
                    x.then_inc(mixed, 1)
                split_made()
                run(4)
                pe.wait_ge(conv_normed, TT * (l + 1))
                for n in range(2):
                    b = mix(f"L{l}.cn{n}", conv_affine, 4 * l + 2 * n + 2)
                    for kk in range(2):
                        for t in range(TT):
                            k = 2 * n + kk
                            x = pe.transpose(b[:, kk * SEQ + t * P:kk * SEQ + (t + 1) * P], gt[:, t, k * P:(k + 1) * P], ident)
                    x.then_inc(mixed, 1)
                pe.wait_ge(conv_split, l + 1)
                run(4)
                turn(f"L{l}.ro", DT, tiles_of(hT), lambda t: (ret_rows, 2 * l + t + 1))
                split_made()
                run(8)
                turn(f"L{l}.merged", DT, lambda t, k: gat[:, 0, t, k * P:(k + 1) * P], lambda t: (merged, 4 * (l + 1)))
                split_made()
                run(8)
                turn(f"L{l}.h2", DT, tiles_of(hT), lambda t: (rows_normed, 6 + 4 * l + t + 1))
                split_made()
                for c in range(HT // 2 + 1):
                    if c < HT // 2:
                        run(4)
                    if c > 0:
                        turn(f"L{l}.hid{c - 1}", 2, lambda t, k: fh[:, (c - 1) % 2, t, k * P:(k + 1) * P],
                             lambda t: (ffn_rows, HT * l + 2 * c - 1 + t))
                split_made()
                run(22)
            assert pos == NS, (pos, NS)

        @block.sync
        def _(sp):
            sp.dma_start(xT[:, :, :], x_in).then_inc(x_ld, 16)
            sp.dma_start(cst[:, :], consts).then_inc(consts_in, 16)
            for s, d in enumerate(slots):
                n = d["nk"] * d["width"]
                if s >= R:
                    sp.wait_ge(lo_made, s - R + 1)
                src = stream[d["off"]:d["off"] + P * n].rearrange("(p n) -> p n", p=P)
                sp.dma_start(raw[:, s % R, 0:n], src).then_inc(raw_in[s % R], 16)
            sp.wait_ge(x_normed, 4 * DEPTH2)
            sp.dma_start(out, xT[:, :, :]).then_inc(out_stored, 16)
            sp.wait_ge(out_stored, 16)

        @block.scalar
        def _(act):
            pos = 0

            def make_hi(s):
                n = slots[s]["nk"] * slots[s]["width"]
                act.wait_ge(raw_in[s % R], 16 * (s // R + 1))
                if s >= R:
                    act.wait_ge(slot_used, s - R + 1)
                act.activation(w_hi[:, s % R, 0:n], raw[:, s % R, 0:n], ACT.Copy).then_inc(hi_made, 1)

            splits = splitter(make_hi)

            def take(name):
                n, p = mix_at[name]
                splits(p + R - 1)
                act.wait_ge(mixed, n + 1)
                return mx[n % 2]

            def run(n):
                nonlocal pos
                for name, end in chunks_ending(pos, pos + n):
                    splits(end + R - 1)
                    evac(name)
                pos += n

            def turn_hi(name, dst, ktiles, scale=1.0, k0=0):
                for k in range(0, ktiles, 2):
                    n, p = turn_at[f"{name}.{k // 2}"]
                    splits(p + R - 1)
                    act.wait_ge(turned, n + 1)
                    nk = min(2, ktiles - k)
                    act.activation(dst[:, k0 + k:k0 + k + nk, :], tp[n % 2][:, 0:nk * SEQ].rearrange("p (k t) -> p k t", t=SEQ),
                                   ACT.Copy, scale=scale).then_inc(turned_hi, 1)

            last_squares = None

            def squares(src, total, done, value):
                nonlocal last_squares
                if last_squares:
                    act.wait_ge(last_squares[0], last_squares[1])
                act.activation(junk[:, 0:src.shape[1]], src, ACT.Square, accum_out=total).then_inc(done, 1)
                last_squares = (done, value)

            def square_sums(name):
                a = stats_of(name, 4)
                for t in range(TT):
                    squares(xT[:, t, :], a[:, t:t + 1], norm_sums, 2 * NORMS.index(name) + t + 1)

            def evac(name):
                l, kind, i = split_name(name)
                cols = slice(i * 512, (i + 1) * 512)
                odd = slice((i % 2) * 512, (i % 2 + 1) * 512)
                who = [reader_of(name, t) for t in range(TT)]
                if kind in ("ssm_out.", "attn_out.", "mla_o.", "conv_o.", "ret_o.") or (kind == "ret." and i < 2):
                    return
                if kind == "glu." and name[0] != "L":
                    for t in range(TT):
                        act.wait_ge(glu_biased, 2 * i + t + 1)
                        part = junk[:, 512 * t:512 * (t + 1)]
                        act.activation(part, part, ACT.Tanh, scale=0.5).then_inc(glu_tanh, 1)
                    return
                for t, b in enumerate(banks_of(act, name)):
                    read, value = who[t][0], who[t][1]
                    if kind == "ssm_in." and i < 2:
                        act.activation(uT[:, t, cols], b, ACT.Copy).then_inc(read, 1)
                        act.wait_ge(read, value)
                        act.dma_start(u_scr[t * P:(t + 1) * P, cols], uT[:, t, cols]).then_inc(u_stored[i], 16)
                    elif kind == "ssm_in.":
                        act.activation(zT[:, t, odd], b, ACT.Tanh, scale=0.5).then_inc(z_tanh, 1)
                    elif kind == "attn_in." and i < 4:
                        if 2 * i + t >= 2:
                            act.wait_ge(squares_summed, 2 * i + t - 1)
                        act.activation((qT, kT)[i // 2][:, t, odd], b, ACT.Copy)
                        act.activation(sq[:, t, :], b, ACT.Square).then_inc(read, 1)
                    elif kind == "attn_in." and i < 6:
                        act.activation(vT[:, t, odd], b, ACT.Copy).then_inc(read, 1)
                    elif kind == "attn_in.":
                        act.activation(szT[:, t, odd], b, ACT.Tanh, scale=0.5).then_inc(attn_z_tanh, 1)
                    elif kind == "lat.":
                        a = stats_of(f"L{l}.lat", 8)
                        act.activation(cT[:, t, :], b, ACT.Copy).then_inc(read, 1)
                        act.wait_ge(read, value)
                        squares(cT[:, t, 0:QR], a[:, t:t + 1], lat_sums, 4 * l + 2 * t + 1)
                        squares(cT[:, t, QR:QR + KVR], a[:, 2 + t:3 + t], lat_sums, 4 * l + 2 * t + 2)
                    elif kind == "glu." and i == 0:
                        act.activation(ga[:, t, :], b, ACT.Copy).then_inc(read, 1)
                    elif kind == "glu.":
                        act.activation(gt[:, t, :], b, ACT.Tanh, scale=0.5).then_inc(read, 1)
                    elif kind == "uq.":
                        act.activation(mq[:, t, 4 * i:4 * i + 4, :], b.rearrange("p (h d) -> p h d", h=4), ACT.Copy).then_inc(read, 1)
                    elif kind == "ukv.":
                        v = b.rearrange("p (h d) -> p h d", h=4)
                        act.activation(mk[:, t, 4 * i:4 * i + 4, 0:NOPE], v[:, :, 0:NOPE], ACT.Copy)
                        act.activation(mv[:, t, 4 * i:4 * i + 4, :], v[:, :, NOPE:NOPE + MV], ACT.Copy).then_inc(read, 1)
                    elif kind == "ret." and i < 4:
                        act.activation(rv[:, t, odd], b, ACT.Copy).then_inc(read, 1)
                    elif kind == "ret.":
                        act.activation(rg[:, t, odd], b, ACT.Tanh, scale=0.5).then_inc(ret_g_tanh, 1)
                    elif kind == "gate.":
                        act.activation(gat[:, i // 2, t, odd], b, ACT.Tanh, scale=0.5).then_inc(read, 1)
                    elif kind in ("out.", "down."):
                        a = stats_of(f"L{l}.{kind}post", 8)
                        act.activation(hT[:, t, cols], b, ACT.Copy).then_inc(read, 1)
                        act.wait_ge(read, value)
                        squares(hT[:, t, cols], a[:, 2 * t + i:2 * t + i + 1], post_sums,
                                8 * l + (kind == "down.") * 4 + 2 * i + t + 1)
                    elif kind == "ffn.":
                        n = HT * l + 2 * i + t
                        if n >= 4:
                            act.wait_ge(ffn_rows, n - 3)
                        act.activation(ft[:, i % 2, t, :], b[:, 0:FCH], ACT.Tanh, scale=0.5).then_inc(ffn_tanh, 1)

            act.wait_ge(ssm_in, 64)
            act.activation(pdt[:, :], pdt[:, :], ACT.Exp).then_inc(dt_exp, 1)
            act.wait_ge(x_ld, 16)
            square_sums("hn")
            act.wait_ge(ssm_rates, 1)
            act.activation(par[:, 2, :], par[:, 0, :], ACT.Exp).then_inc(ssm_mag, 1)
            act.wait_ge(decay_abs, 1)
            act.activation(lgw[:, 1, :], lgw[:, 0, :], ACT.Exp, scale=-1.0).then_inc(decay_exp, 1)
            act.wait_ge(angles, 1)
            flat = sw[:, :, :, :].rearrange("p a q k -> p (a q k)")
            act.activation(flat[:, 2 * N_ANG:4 * N_ANG], flat[:, 2 * N_ANG:4 * N_ANG], ACT.Sin).then_inc(sines, 1)
            splits(R - 1)
            turn_hi("hn", f_hi, DT)
            run(8)

            def taps_and_turned_b(qd):
                for e in range(2):
                    b = take(f"ssm{qd}.taps{e}")
                    if qd > 0:
                        act.wait_ge(toeplitz_in, 16 * SUB * qd)
                    act.activation(kts[:, :, e, :], b[:, 0:PQ * GROUP].rearrange("p (q c) -> p q c", c=GROUP),
                                   ACT.Copy).then_inc(taps_copied, 1)
                act.wait_ge(taps_copied, 2 * qd + 2)
                if qd > 0:
                    act.wait_ge(mixed, mix_at[f"ssm{qd - 1}.y1"][0] + 1)
                act.wait_ge(toeplitz_zero, 1)
                taps = kts[:, :, :, :].rearrange("p q e c -> p (q e c)")
                for s in range(SUB):
                    act.dma_start(mm[0:GROUP * (s + 1), s, :], taps[GROUP * (SUB - 1 - s):P, :]).then_inc(toeplitz_in, 16)
                for n in range(4):
                    b = take(f"ssm{qd}.bt{n}")
                    act.activation(bt[:, n // 2, 4 * (n % 2):4 * (n % 2) + 4, :], b[:, :].rearrange("p (q c) -> p q c", c=P),
                                   ACT.Copy).then_inc(b_T_copied, 1)

            def y_out(qd):
                for e in range(2):
                    b = take(f"ssm{qd}.y{e}")
                    if qd > 0:
                        act.wait_ge(y_stored, 16 * JB * qd)
                    for g in range(GB // 2):
                        col = (2 * g + e) * GROUP
                        x = act.activation(yk[:, :, col:col + GROUP], b[:, g * P:(g + 1) * P].rearrange("p (l c) -> p l c", c=GROUP), ACT.Copy)
                    x.then_inc(y_copied, 1)
                act.wait_ge(y_copied, 2 * qd + 2)
                for j in range(JB):
                    col = qd * PCOLS + j * GB * GROUP
                    act.dma_start(y_scr[:, col:col + GB * GROUP].rearrange("(k l) d -> k l d", l=SUB),
                                  yk[32 * j:32 * j + 32, :, :]).then_inc(y_stored, 16)

            def gelu_tanh(qd):
                act.wait_ge(gelu_in, qd + 1)
                act.activation(gw[:, :, :], gw[:, :, :], ACT.Tanh, scale=math.sqrt(2.0 / math.pi)).then_inc(gelu_tanh_made, 1)

            taps_and_turned_b(0)
            for qd in range(PARTS):
                act.wait_ge(u_sub_in, 16 * JB * (qd + 1))
                if qd > 0:
                    act.wait_ge(mixed, mix_at[f"ssm{qd - 1}.u"][0] + 1)
                act.activation(uo[:, :, :, :], uk[:, :, :].rearrange("p m (g c) -> p g m c", c=GROUP), ACT.Copy).then_inc(u_ordered, 1)
                b = take(f"ssm{qd}.u")
                act.activation(ug[:, :, :], b[:, :].rearrange("p (g k) -> p g k", k=P), ACT.Copy).then_inc(u_groups_copied, 1)
                if qd > 0:
                    gelu_tanh(qd - 1)
                run(2)
                y_out(qd)
                if qd + 1 < PARTS:
                    taps_and_turned_b(qd + 1)
            gelu_tanh(PARTS - 1)
            turn_hi("y", f_hi, DT, 0.5)
            run(8)
            turn_hi("yg", f_hi, DT, 0.125)
            run(8)
            act.wait_ge(x_updated, 4)
            square_sums("h1")
            turn_hi("h1", f_hi, DT)
            run(16)

            def heads(tag, n_heads, dk, qk, probs, probs_t, stt, base, masked, spare):
                def gap():
                    nonlocal spare
                    n = min(2, spare)
                    run(n)
                    spare -= n

                for i in range(n_heads + 1):
                    if i < n_heads:
                        b = take(f"{tag}.qk{i}")
                        act.activation(qk[0:dk, i % 2, :], b[0:dk, :], ACT.Copy).then_inc(qk_copied, 1)
                    gap()
                    if i > 0:
                        b = take(f"{tag}.pt{i - 1}")
                        act.activation(probs_t[:, (i - 1) % 2, :, :, :].rearrange("p a b c -> p (a b c)"), b[:, :],
                                       ACT.Copy).then_inc(probs_T_copied, 1)
                    if i < n_heads:
                        b = take(f"{tag}.s{i}")
                        act.wait_ge(max_found, base + i + 1)
                        for t in range(TT):
                            src, col, scale = ((a_s[:, i % 2, t, :], t, 1.0) if masked else
                                               (b[:, t * SEQ:(t + 1) * SEQ], 6 + t, MQK ** -0.5))
                            act.activation(probs[:, i % 2, t, :], src, ACT.Exp, bias=stt[:, i % 2, col:col + 1], scale=scale,
                                           accum_out=stt[:, i % 2, 2 + t:3 + t]).then_inc(probs_made, 1)
                    gap()

            heads("attn", HEADS, HD, a_qk, a_p, a_pt, a_st, 0, True, 16)
            turn_hi("attn_o", f_hi, DT, 0.5)
            run(8)
            act.wait_ge(x_updated, 8)
            for l in range(DEPTH2):
                if l > 0:
                    act.wait_ge(x_normed, 4 * l)
                square_sums(f"L{l}.h")
                turn_hi(f"L{l}.h", f_hi, DT)
                run(12)
                turn_hi(f"L{l}.lat", c_hi, 3)
                run(12)
                act.wait_ge(pads_zero, l + 1)
                for n in range(2):
                    b = take(f"L{l}.cin{n}")
                    act.activation(cp[:, 2 * n:2 * n + 2, PAD:PAD + SEQ], b[:, :].rearrange("p (k t) -> p k t", t=SEQ),
                                   ACT.Copy, scale=0.5).then_inc(conv_in, 1)
                heads(f"L{l}.mla", MLA_H, MQK, m_qk, m_p, m_pt, m_st, HEADS + MLA_H * l, False, 36)
                for h in range(RH):
                    b = take(f"L{l}.rqk{h}")
                    act.activation(r_qk[:, h, :], b[:, :], ACT.Copy).then_inc(ret_qk_copied, 1)
                for h in range(RH):
                    act.wait_ge(decay_args, RH * l + h + 1)
                    act.activation(r_d[:, h, :, :], r_d[:, h, :, :], ACT.Exp).then_inc(decays_made, 1)
                run(4)
                for h in range(RH):
                    b = take(f"L{l}.ro{h}")
                    o = (rqT, rkT)[h // 2][:, :, (h % 2) * RDV:(h % 2 + 1) * RDV]
                    act.activation(o, b[:, :].rearrange("p (t e) -> p t e", t=TT), ACT.Copy).then_inc(ret_o_copied, 1)
                turn_hi(f"L{l}.mo", f_hi, 4)
                run(4)
                for n in range(2):
                    b = take(f"L{l}.cn{n}")
                    for kk in range(2):
                        k = 2 * n + kk
                        act.activation(cacc[:, k, :], b[:, kk * SEQ:(kk + 1) * SEQ], ACT.Identity,
                                       scale=cfp[:, k, TAPS + 1:TAPS + 2], bias=cfp[:, k, TAPS + 2:TAPS + 3]).then_inc(conv_affine, 1)
                act.wait_ge(conv_affine, 4 * l + 4)
                flat = cacc[:, :, :].rearrange("p k t -> p (k t)")
                act.activation(junk[:, :], flat, ACT.Tanh, scale=0.5).then_inc(conv_out_tanh, 1)
                act.wait_ge(conv_silu, l + 1)
                act.activation(f_hi[:, 4:8, :].rearrange("p k t -> p (k t)"), flat, ACT.Copy, scale=0.5).then_inc(conv_hi, 1)
                run(4)
                turn_hi(f"L{l}.ro", f_hi, DT, 0.5)
                run(8)
                turn_hi(f"L{l}.merged", f_hi, DT, 0.5)
                run(8)
                act.wait_ge(x_normed, 4 * l + 2)
                square_sums(f"L{l}.h2")
                turn_hi(f"L{l}.h2", f_hi, DT)
                for c in range(HT // 2 + 1):
                    if c < HT // 2:
                        run(4)
                    if c > 0:
                        turn_hi(f"L{l}.hid{c - 1}", h2_hi, 2, 0.5, 2 * (c - 1))
                run(22)

        @block.vector
        def _(dve):
            count = Count()
            pos = 0

            def make_lo(s):
                n = slots[s]["nk"] * slots[s]["width"]
                dve.wait_ge(hi_made, s + 1)
                if s >= R:
                    dve.wait_ge(slot_used, s - R + 1)
                dve.tensor_tensor(w_lo[:, s % R, 0:n], raw[:, s % R, 0:n], w_hi[:, s % R, 0:n].bitcast(F32),
                                  ALU.subtract).then_inc(lo_made, 1)

            splits = splitter(make_lo)

            def take(name):
                n, p = mix_at[name]
                splits(p + R - 1)
                dve.wait_ge(mixed, n + 1)
                return mx[n % 2]

            def run(n):
                nonlocal pos
                for name, end in chunks_ending(pos, pos + n):
                    splits(end + R - 1)
                    evac(name)
                pos += n

            def turn_lo(name, hi, lo, ktiles, scale=1.0, k0=0):
                for k in range(0, ktiles, 2):
                    n, p = turn_at[f"{name}.{k // 2}"]
                    splits(p + R - 1)
                    dve.wait_ge(turned_hi, n + 1)
                    nk = min(2, ktiles - k)
                    dve.scalar_tensor_tensor(out=lo[:, k0 + k:k0 + k + nk, :].rearrange("p k t -> p (k t)"),
                                             in0=tp[n % 2][:, 0:nk * SEQ], scalar=scale,
                                             in1=hi[:, k0 + k:k0 + k + nk, :].rearrange("p k t -> p (k t)").bitcast(F32),
                                             op0=ALU.mult, op1=ALU.subtract).then_inc(turned_lo, 1)

            def stt(o, a, s, b, op0=ALU.mult, op1=ALU.mult):
                return dve.scalar_tensor_tensor(out=o, in0=a, scalar=s, in1=b, op0=op0, op1=op1)

            def tt(o, a, b, op):
                return dve.tensor_tensor(o, a, b, op)

            def ts(o, a, s1_, s2_, op0, op1=None):
                return dve.tensor_scalar(o, a, s1_, s2_, op0, op1) if op1 else dve.tensor_scalar(o, a, s1_, s2_, op0)

            def cmul(o_r, o_i, a_r, a_i, b_r, b_i, w):
                tt(w[0], a_r, b_r, ALU.mult).then_inc(dve_steps, count())
                tt(w[1], a_i, b_i, ALU.mult).then_inc(dve_steps, count())
                tt(w[2], a_r, b_i, ALU.mult).then_inc(dve_steps, count())
                tt(w[3], a_i, b_r, ALU.mult).then_inc(dve_steps, count())
                dve.wait_ge(dve_steps, count.n)
                tt(o_r, w[0], w[1], ALU.subtract).then_inc(dve_steps, count())
                tt(o_i, w[2], w[3], ALU.add).then_inc(dve_steps, count())
                dve.wait_ge(dve_steps, count.n)

            def apply_norm(no, gain):
                dve.wait_ge(norm_roots, no + 1)
                g = gain_row(dve, gain)
                a = stats_of(NORMS[no], 4)
                for t in range(TT):
                    stt(hT[:, t, :], xT[:, t, :], a[:, 2 + t:3 + t], g).then_inc(rows_normed, 1)

            def evac(name):
                l, kind, i = split_name(name)
                cols = slice(i * 512, (i + 1) * 512)
                odd = slice((i % 2) * 512, (i % 2 + 1) * 512)
                who = [reader_of(name, t) for t in range(TT)]
                if kind == "attn_in." and i < 4:
                    qk_norm_rope(i)
                    return
                if kind == "lat.":
                    latent(l)
                    return
                if kind == "uq." and i == 1:
                    mla_rope(l)
                    return
                if (kind in ("uq.", "ukv.", "gate.", "out.", "down.") or (kind == "ssm_in." and i < 2)
                        or (kind == "attn_in." and i < 6) or (kind == "ret." and 2 <= i < 4)
                        or (kind == "glu." and name[0] == "L" and i == 0)):
                    return
                for t, b in enumerate(banks_of(dve, name)):
                    read = who[t][0]
                    if kind == "ssm_in.":
                        dve.wait_ge(z_tanh, 2 * (i - 2) + t + 1)
                        stt(zT[:, t, odd], zT[:, t, odd], 1.0, b, ALU.add).then_inc(read, 1)
                    elif kind == "glu." and name[0] != "L":
                        g = gain_row(dve, "b_glu")
                        if i > 0:
                            dve.wait_ge(glu_rows_half, t + 1)
                        tt(junk[:, 512 * t:512 * (t + 1)], b, g[:, cols], ALU.add).then_inc(read, 1)
                    elif kind in ("ssm_out.", "attn_out."):
                        tt(xT[:, t, cols], b, xT[:, t, cols], ALU.add).then_inc(read, 1)
                    elif kind == "attn_in.":
                        dve.wait_ge(attn_z_tanh, 2 * (i - 6) + t + 1)
                        stt(szT[:, t, odd], szT[:, t, odd], 1.0, b, ALU.add).then_inc(read, 1)
                    elif kind == "glu.":
                        dve.wait_ge(conv_tanh_made, 2 * l + t + 1)
                        stt(ga[:, t, :], gt[:, t, :], 1.0, ga[:, t, :], ALU.add).then_inc(conv_glu_rows, 1)
                    elif kind == "ret." and i < 2:
                        ret_rope(l, i, t, b, read)
                    elif kind == "ret.":
                        dve.wait_ge(ret_g_tanh, 4 * l + 2 * (i - 4) + t + 1)
                        stt(rg[:, t, odd], rg[:, t, odd], 1.0, b, ALU.add).then_inc(read, 1)
                    elif kind == "mla_o.":
                        stt(gat[:, 0, t, cols], gat[:, 0, t, cols], 1.0, b, ALU.add).then_inc(read, 1)
                    elif kind in ("conv_o.", "ret_o."):
                        n = 1 if kind == "conv_o." else 2
                        stt(gat[:, n, t, cols], gat[:, n, t, cols], 1.0, b, ALU.add).then_inc(read, 1)
                        dve.wait_ge(read, who[t][1])
                        x = tt(gat[:, 0, t, cols], gat[:, 0, t, cols], gat[:, n, t, cols], ALU.add)
                        if n == 2:
                            x.then_inc(merged, 1)
                        else:
                            x.then_inc(dve_steps, count())
                    elif kind == "ffn.":
                        n = HT * l + 2 * i + t
                        dve.wait_ge(ffn_tanh, n + 1)
                        stt(ft[:, i % 2, t, :], ft[:, i % 2, t, :], 1.0, b[:, 0:FCH], ALU.add).then_inc(dve_steps, count())
                        dve.wait_ge(dve_steps, count.n)
                        tt(fh[:, i % 2, t, :], ft[:, i % 2, t, :], b[:, FCH:2 * FCH], ALU.mult).then_inc(read, 1)
                if kind == "glu." and name[0] != "L":
                    for t in range(TT):
                        dve.wait_ge(glu_tanh, 2 * i + t + 1)
                        stt(yT[:, t, cols], junk[:, 512 * t:512 * (t + 1)], 1.0, yT[:, t, cols], ALU.add).then_inc(glu_rows_half, 1)
                        dve.wait_ge(glu_rows_half, 2 * i + t + 1)
                        tt(yT[:, t, cols], yT[:, t, cols], zT[:, t, cols], ALU.mult).then_inc(glu_rows, 1)

            dve.memset(minus_half[:, :], -0.5).then_inc(minus_half_set, 1)
            dve.memset(mm[:, :, :], 0.0).then_inc(toeplitz_zero, 1)
            dve.memset(pw[:, 0, 0, :], 1.0).then_inc(dve_steps, count())
            dve.memset(pw[:, 1, 0, :], 0.0).then_inc(dve_steps, count())
            dve.memset(st[:, :, :, 0:1], 0.0).then_inc(dve_steps, count())
            dve.wait_ge(consts_in, 16)
            dve.wait_ge(ssm_in, 64)
            flat = sw[:, :, :, :].rearrange("p a q k -> p (a q k)")
            ang = flat[:, 0:N_ANG]
            turns_w, cos_w, sin_w = (flat[:, k * N_ANG:(k + 1) * N_ANG] for k in (1, 2, 3))
            lr, li = ab[:, 0, :], ab[:, 1, :]
            dve.tensor_copy(posf[:, :], posi[:, :]).then_inc(dve_steps, count())
            dve.wait_ge(dt_exp, 1)
            tt(par[:, 0, :], lr, pdt[:, :], ALU.mult).then_inc(ssm_rates, 1)
            tt(ang[:, 0:Q], li, pdt[:, :], ALU.mult).then_inc(dve_steps, count())
            dve.wait_ge(dve_steps, count.n)
            for t in range(TT):
                a = Q + t * (RDK // 2)
                ts(ang[:, a:a + RDK // 2], cst[:, C_INVR:C_INVM], posf[:, t:t + 1], None, ALU.mult).then_inc(dve_steps, count())
                a = Q + RDK + t * (ROPE // 2)
                ts(ang[:, a:a + ROPE // 2], cst[:, C_INVM:N_CONST], posf[:, t:t + 1], None, ALU.mult).then_inc(dve_steps, count())
            dve.wait_ge(dve_steps, count.n)
            for w, quarter in ((sin_w, 0.0), (cos_w, 0.25)):
                ts(turns_w, ang, 1.0 / TWO_PI, quarter, ALU.mult, ALU.add).then_inc(dve_steps, count())
                dve.wait_ge(dve_steps, count.n)
                ts(turns_w, turns_w, ROUND, ROUND, ALU.add, ALU.subtract).then_inc(dve_steps, count())
                dve.wait_ge(dve_steps, count.n)
                stt(w, turns_w, -PI_A, ang, ALU.mult, ALU.add).then_inc(dve_steps, count())
                dve.wait_ge(dve_steps, count.n)
                stt(w, turns_w, -PI_B, w, ALU.mult, ALU.add).then_inc(dve_steps, count())
                dve.wait_ge(dve_steps, count.n)
                stt(w, turns_w, -PI_C, w, ALU.mult, ALU.add).then_inc(dve_steps, count())
                dve.wait_ge(dve_steps, count.n)
                if quarter:
                    ts(w, w, math.pi / 2, None, ALU.add).then_inc(dve_steps, count())
                    dve.wait_ge(dve_steps, count.n)
                last = ts(w, w, PI_IN, -PI_IN, ALU.min, ALU.max)
                if not quarter:
                    last.then_inc(dve_steps, count())
            last.then_inc(angles, 1)
            dve.wait_ge(decay_in, 16)
            ts(lgw[:, 2, :], lgw[:, 5, :], -1.0, None, ALU.mult).then_inc(dve_steps, count())
            dve.wait_ge(dve_steps, count.n)
            tt(lgw[:, 0, :], lgw[:, 2, :], lgw[:, 5, :], ALU.max).then_inc(decay_abs, 1)
            apply_norm(0, "norm0")
            turn_lo("hn", f_hi, f_lo, DT)
            dve.wait_ge(decay_exp, 1)
            e_, s_, s2_, p_ = (lgw[:, k, :] for k in (1, 2, 3, 4))
            ts(p_, e_, 2.0, None, ALU.add).then_inc(dve_steps, count())
            dve.wait_ge(dve_steps, count.n)
            dve.reciprocal(s2_, p_).then_inc(dve_steps, count())
            dve.wait_ge(dve_steps, count.n)
            tt(s_, e_, s2_, ALU.mult).then_inc(dve_steps, count())
            dve.wait_ge(dve_steps, count.n)
            tt(s2_, s_, s_, ALU.mult).then_inc(dve_steps, count())
            dve.wait_ge(dve_steps, count.n)
            ts(p_, s2_, 1.0 / 21, None, ALU.mult).then_inc(dve_steps, count())
            dve.wait_ge(dve_steps, count.n)
            for k in range(19, 1, -2):
                stt(p_, p_, 1.0 / k, s2_, ALU.add, ALU.mult).then_inc(dve_steps, count())
                dve.wait_ge(dve_steps, count.n)
            stt(p_, p_, 1.0, s_, ALU.add, ALU.mult).then_inc(dve_steps, count())
            ts(e_, lgw[:, 5, :], 0.0, None, ALU.min).then_inc(dve_steps, count())
            dve.wait_ge(dve_steps, count.n)
            stt(lg[:, :], p_, -2.0, e_, ALU.mult, ALU.add).then_inc(dve_steps, count())
            dve.wait_ge(sines, 1)
            dve.wait_ge(ssm_mag, 1)
            both = flat[:, 2 * N_ANG:4 * N_ANG].rearrange("p (a n) -> p a n", a=2)
            dve.tensor_copy(rcs[:, :, :, :].rearrange("p a t n -> p a (t n)"), both[:, :, Q:Q + RDK]).then_inc(dve_steps, count())
            dve.tensor_copy(mcs[:, :, :, :].rearrange("p a t n -> p a (t n)"), both[:, :, Q + RDK:N_ANG]).then_inc(dve_steps, count())
            dve.tensor_copy(par[:, 3:5, :], both[:, :, 0:Q]).then_inc(dve_steps, count())
            splits(R)
            dve.wait_ge(dve_steps, count.n)
            c_, sn_, mag = par[:, 3, :], par[:, 4, :], par[:, 2, :]
            tt(pw[:, 0, 1, :], mag, c_, ALU.mult).then_inc(dve_steps, count())
            tt(pw[:, 1, 1, :], mag, sn_, ALU.mult).then_inc(dve_steps, count())
            w4 = [par[:, k, :] for k in (16, 17, 18, 19)]
            for k in range(3):
                src = (c_, sn_) if k == 0 else (par[:, 14, :], par[:, 15, :])
                cmul(par[:, 14, :], par[:, 15, :], *src, *src, w4)
                tt(par[:, 13, :], *((mag, mag) if k == 0 else (par[:, 13, :], par[:, 13, :])), ALU.mult).then_inc(dve_steps, count())
                dve.wait_ge(dve_steps, count.n)
            dve.tensor_copy(par[:, 12, :], par[:, 13, :]).then_inc(turn_base, 1)
            splits(R + 1)
            wide = gw[:, :, :].rearrange("p t n -> p (t n)").rearrange("p (a t q) -> p a t q", a=4, q=Q)
            cmul(pw[:, 0, 2, :], pw[:, 1, 2, :], pw[:, 0, 1, :], pw[:, 1, 1, :], pw[:, 0, 1, :], pw[:, 1, 1, :], w4)
            for k, n in ((2, 2), (4, 4)):
                by = [pw[:, c, k:k + 1, :].broadcast_to([P, n, Q]) for c in range(2)]
                cmul(pw[:, 0, k + 1:k + 1 + n, :], pw[:, 1, k + 1:k + 1 + n, :], *by,
                     pw[:, 0, 1:1 + n, :], pw[:, 1, 1:1 + n, :], [wide[:, a, 0:n, :] for a in range(4)])
            for m in range(SUB):
                x = dve.tensor_copy(pwb[:, :, m, :], pw[:, :, SUB - 1 - m, :])
                if m < SUB - 1:
                    x.then_inc(dve_steps, count())
                else:
                    x.then_inc(powers_made, 1)
            splits(R + 2)
            den, rden, nr, t1, t2 = (par[:, k, :] for k in (5, 6, 7, 8, 9))
            f_r, f_i = par[:, 10, :], par[:, 11, :]
            tt(t1, lr, lr, ALU.mult).then_inc(dve_steps, count())
            tt(t2, li, li, ALU.mult).then_inc(dve_steps, count())
            ts(nr, pw[:, 0, 1, :], -1.0, None, ALU.add).then_inc(dve_steps, count())
            dve.wait_ge(dve_steps, count.n)
            tt(den, t1, t2, ALU.add).then_inc(dve_steps, count())
            dve.wait_ge(dve_steps, count.n)
            dve.reciprocal(rden, den).then_inc(dve_steps, count())
            ni = pw[:, 1, 1, :]
            for o, a, b, op in ((f_r, lr, li, ALU.add), (f_i, li, lr, ALU.subtract)):
                tt(t1, nr if op == ALU.add else ni, lr, ALU.mult).then_inc(dve_steps, count())
                tt(t2, ni if op == ALU.add else nr, li, ALU.mult).then_inc(dve_steps, count())
                dve.wait_ge(dve_steps, count.n)
                tt(t1, t1, t2, op).then_inc(dve_steps, count())
                dve.wait_ge(dve_steps, count.n)
                tt(o, t1, rden, ALU.mult).then_inc(dve_steps, count())
                dve.wait_ge(dve_steps, count.n)
            dve.wait_ge(ssm_mats_in, 16)
            fbb = [f.unsqueeze(1).broadcast_to([P, GROUP, Q]) for f in (f_r, f_i)]
            w = [junk[:, 0:512].rearrange("p (c q) -> p c q", q=Q), junk[:, 512:1024].rearrange("p (c q) -> p c q", q=Q)]
            for o, b0, b1, op in ((fb[:, 0, :, :], 0, 1, ALU.subtract), (fb[:, 1, :, :], 1, 0, ALU.add)):
                tt(w[0], bc[:, b0, :, :], fbb[0], ALU.mult).then_inc(dve_steps, count())
                tt(w[1], bc[:, b1, :, :], fbb[1], ALU.mult).then_inc(dve_steps, count())
                dve.wait_ge(dve_steps, count.n)
                tt(o, w[0], w[1], op).then_inc(dve_steps, count())
                dve.wait_ge(dve_steps, count.n)
            ts(bc[:, 3, :, :], bc[:, 3, :, :], -1.0, None, ALU.mult).then_inc(c_negated, 1)
            dve.wait_ge(c_negated, 1)

            def b_mats(qd):
                if qd > 0:
                    dve.wait_ge(mixed, mix_at[f"ssm{qd - 1}.bt3"][0] + 1)
                q0 = PQ * qd
                pr, pi = (pwb[:, c, :, q0:q0 + PQ].rearrange("p m q -> p q m").unsqueeze(3).broadcast_to([P, PQ, SUB, GROUP]) for c in range(2))
                fr, fi = (fb[:, c, :, q0:q0 + PQ].rearrange("p c q -> p q c").unsqueeze(2).broadcast_to([P, PQ, SUB, GROUP]) for c in range(2))
                o = [bm[:, c, :, :].rearrange("p q (m c) -> p q m c", c=GROUP) for c in range(2)]
                for n, (x0, x1, op) in enumerate(((fr, fi, ALU.subtract), (fi, fr, ALU.add))):
                    tt(o[n], pr, x0, ALU.mult).then_inc(dve_steps, count())
                    if n == 1:
                        dve.wait_ge(dve_steps, count.n - 1)
                    elif qd > 0:
                        dve.wait_ge(b_mats_made, qd)
                    tt(tmp[:, :, :, :], pi, x1, ALU.mult).then_inc(dve_steps, count())
                    dve.wait_ge(dve_steps, count.n)
                    i = tt(o[n], o[n], tmp[:, :, :, :], op)
                    if n == 1:
                        i.then_inc(b_mats_made, 1)
                    else:
                        i.then_inc(dve_steps, count())

            def scan_states(qd):
                b = take(f"ssm{qd}.b")
                dve.wait_ge(turns_made, 1)
                q0 = PQ * qd
                ec, es = (turn[:, c, q0:q0 + PQ, :] for c in range(2))
                br, bi = (b[:, c * PQ * NSUB:(c + 1) * PQ * NSUB].rearrange("p (q k) -> p q k", k=NSUB) for c in range(2))
                s0, s1_, s2__, s3_ = (sw[:, c, :, :] for c in range(4))
                tt(s0, br, ec, ALU.mult).then_inc(dve_steps, count())
                tt(s1_, bi, es, ALU.mult).then_inc(dve_steps, count())
                tt(s2__, bi, ec, ALU.mult).then_inc(dve_steps, count())
                tt(s3_, br, es, ALU.mult).then_inc(state_terms_read, 1)
                dve.wait_ge(state_terms_read, qd + 1)
                tt(s0, s0, s1_, ALU.add).then_inc(dve_steps, count())
                tt(s2__, s2__, s3_, ALU.subtract).then_inc(dve_steps, count())
                dve.wait_ge(dve_steps, count.n)
                f2 = lambda x: x.rearrange("p q k -> p (q k)")
                for o, x in ((s1_, s0), (s3_, s2__)):
                    dve.tensor_tensor_scan(f2(o), f2(rho[:, q0:q0 + PQ, :]), f2(x), 0.0, ALU.mult, ALU.add).then_inc(dve_steps, count())
                dve.wait_ge(dve_steps, count.n)
                if qd > 1:
                    dve.wait_ge(gelu_made, qd - 1)
                g0, g1 = (gw[:, t, :].rearrange("p (q k) -> p q k", k=NSUB) for t in range(2))
                tt(s0, s1_, ec, ALU.mult).then_inc(dve_steps, count())
                tt(s2__, s3_, es, ALU.mult).then_inc(dve_steps, count())
                tt(g0, s3_, ec, ALU.mult).then_inc(dve_steps, count())
                tt(g1, s1_, es, ALU.mult).then_inc(dve_steps, count())
                dve.wait_ge(dve_steps, count.n)
                if qd > 0:
                    dve.wait_ge(mixed, mix_at[f"ssm{qd - 1}.y1"][0] + 1)
                n = NSUB - 1
                tt(st[:, 0, :, 1:], s0[:, :, 0:n], s2__[:, :, 0:n], ALU.subtract).then_inc(dve_steps, count())
                tt(st[:, 1, :, 1:], g0[:, :, 0:n], g1[:, :, 0:n], ALU.add).then_inc(states_made, 1)

            def gelu(qd):
                dve.wait_ge(y_in, 16 * TT * (qd + 1))
                g = gain_row(dve, "d_skip")
                cols = slice(qd * PCOLS, (qd + 1) * PCOLS)
                y, u, gg = yT[:, :, cols], uT[:, :, cols], gw[:, :, :]
                dve.wait_ge(states_made, min(qd + 2, PARTS))
                if qd > 0:
                    dve.wait_ge(gelu_made, qd)
                tt(gg, u, g[:, cols].unsqueeze(1).broadcast_to([P, TT, PCOLS]), ALU.mult).then_inc(dve_steps, count())
                dve.wait_ge(dve_steps, count.n)
                tt(y, y, gg, ALU.add).then_inc(dve_steps, count())
                dve.wait_ge(dve_steps, count.n)
                tt(gg, y, y, ALU.mult).then_inc(dve_steps, count())
                dve.wait_ge(dve_steps, count.n)
                ts(gg, gg, 0.044715, 1.0, ALU.mult, ALU.add).then_inc(dve_steps, count())
                dve.wait_ge(dve_steps, count.n)
                tt(gg, gg, y, ALU.mult).then_inc(gelu_in, 1)
                dve.wait_ge(gelu_tanh_made, qd + 1)
                stt(y, gg, 1.0, y, ALU.add).then_inc(gelu_made, 1)

            b_mats(0)
            run(8)
            for qd in range(PARTS):
                scan_states(qd)
                if qd + 1 < PARTS:
                    b_mats(qd + 1)
                if qd > 0:
                    gelu(qd - 1)
                run(2)
            gelu(PARTS - 1)
            turn_lo("y", f_hi, f_lo, DT, 0.5)
            run(8)
            turn_lo("yg", f_hi, f_lo, DT, 0.125)
            run(8)

            def qk_norm_rope(i):
                a = stats_of(f"qk{i}", 16)
                dst = (qT, kT)[i // 2]
                part = slice((i % 2) * 512, (i % 2 + 1) * 512)
                for t in range(TT):
                    dve.wait_ge(squares_made, 2 * i + t + 1)
                    dve.tensor_reduce(a[:, 4 * t:4 * t + 4], sq[:, t, :].rearrange("p (h d) -> p h d", d=HD), AX, ALU.add).then_inc(squares_summed, 1)
                dve.wait_ge(qk_roots, i + 1)
                dve.wait_ge(qk_gain_in, 32)
                v = [dst[:, t, part].rearrange("p (h d) -> p h d", d=HD) for t in range(TT)]
                for t in range(TT):
                    tt(v[t], v[t], a[:, 8 + 4 * t:12 + 4 * t].unsqueeze(2).broadcast_to([P, 4, HD]), ALU.mult).then_inc(dve_steps, count())
                dve.wait_ge(dve_steps, count.n)
                for t in range(TT):
                    tt(v[t], v[t], qkg[:, i // 2, :].unsqueeze(1).broadcast_to([P, 4, HD]), ALU.mult).then_inc(dve_steps, count())
                dve.wait_ge(dve_steps, count.n)
                half = ROT // 2
                if i > 0:
                    dve.wait_ge(attn_qk_roped, 2 * i)
                w = [[ropt[:, t, k, :].rearrange("p (h d) -> p h d", h=4) for k in range(4)] for t in range(TT)]
                for t in range(TT):
                    cs = [cst[:, c + t * half:c + (t + 1) * half].unsqueeze(1).broadcast_to([P, 4, half]) for c in (C_COS1, C_SIN1)]
                    x1, x2 = v[t][:, :, 0:half], v[t][:, :, half:ROT]
                    tt(w[t][0], x1, cs[0], ALU.mult).then_inc(dve_steps, count())
                    tt(w[t][1], x2, cs[1], ALU.mult).then_inc(dve_steps, count())
                    tt(w[t][2], x2, cs[0], ALU.mult).then_inc(dve_steps, count())
                    tt(w[t][3], x1, cs[1], ALU.mult).then_inc(dve_steps, count())
                dve.wait_ge(dve_steps, count.n)
                for t in range(TT):
                    tt(v[t][:, :, 0:half], w[t][0], w[t][1], ALU.subtract).then_inc(dve_steps, count())
                    tt(v[t][:, :, half:ROT], w[t][2], w[t][3], ALU.add).then_inc(attn_qk_roped, 1)

            def heads(tag, n_heads, dv, stt_, base, masked, out_of, spare, extra):
                def gap():
                    nonlocal spare
                    n = min(2, spare)
                    run(n)
                    spare -= n

                for i in range(n_heads + 1):
                    gap()
                    if i < n_heads:
                        b = take(f"{tag}.s{i}")
                        sc = b[:, :].rearrange("p (t k) -> p t k", t=TT)
                        m = stt_[:, i % 2, :]
                        if masked:
                            src = a_s[:, i % 2, :, :]
                            mask = cst[:, C_MASK:C_MASK + TT * SEQ].rearrange("p (t k) -> p t k", t=TT)
                            stt(src, sc, HD ** -0.5, mask, ALU.mult, ALU.add).then_inc(scores_masked, 1)
                            dve.wait_ge(scores_masked, base + i + 1)
                            dve.tensor_reduce(m[:, 0:2], src, AX, ALU.max, negate=True).then_inc(max_found, 1)
                        else:
                            dve.tensor_reduce(m[:, 0:2], sc, AX, ALU.max, negate=True).then_inc(dve_steps, count())
                            dve.wait_ge(dve_steps, count.n)
                            ts(m[:, 6:8], m[:, 0:2], MQK ** -0.5, None, ALU.mult).then_inc(max_found, 1)
                    extra(i)
                    gap()
                    if i > 0:
                        h = i - 1
                        dve.wait_ge(probs_made, 2 * (base + h + 1))
                        m = stt_[:, h % 2, :]
                        dve.reciprocal(m[:, 4:6], m[:, 2:4]).then_inc(dve_steps, count())
                        b = take(f"{tag}.o{h}")
                        dve.wait_ge(dve_steps, count.n)
                        for t in range(TT):
                            ts(out_of(t, h), b[:, t * dv:(t + 1) * dv], m[:, 4 + t:5 + t], None, ALU.mult).then_inc(outs_scaled, 1)

            dve.wait_ge(x_updated, 4)
            apply_norm(1, "norm1")
            turn_lo("h1", f_hi, f_lo, DT)
            run(16)
            heads("attn", HEADS, HD, a_st, 0, True, lambda t, h: hT[:, t, h * HD:(h + 1) * HD], 16, lambda i: None)
            dve.wait_ge(outs_scaled, 2 * HEADS)
            dve.wait_ge(attn_z_silu, 4)
            for t in range(TT):
                tt(hT[:, t, :], hT[:, t, :], szT[:, t, :], ALU.mult).then_inc(attn_rows, 1)
            turn_lo("attn_o", f_hi, f_lo, DT, 0.5)
            run(8)

            def latent(l):
                a = stats_of(f"L{l}.lat", 8)
                dve.wait_ge(lat_roots, l + 1)
                dve.wait_ge(layer_params_in, 48 * (l + 1))
                for t in range(TT):
                    stt(cnT[:, t, 0:QR], cT[:, t, 0:QR], a[:, 4 + t:5 + t], latp[:, 0:QR]).then_inc(dve_steps, count())
                    stt(cnT[:, t, QR:QR + KVR], cT[:, t, QR:QR + KVR], a[:, 6 + t:7 + t], latp[:, QR:QR + KVR]).then_inc(lat_rows, 1)

            def mla_rope(l):
                dve.wait_ge(mla_q_copied, 4 * (l + 1))
                half = ROPE // 2
                for t in range(TT):
                    c, s = (mcs[:, k, t, :].unsqueeze(1).broadcast_to([P, MLA_H, half]) for k in range(2))
                    x1, x2 = mq[:, t, :, NOPE:NOPE + half], mq[:, t, :, NOPE + half:MQK]
                    w = [mt[:, k, :, :] for k in range(4)]
                    if l + t > 0:
                        dve.wait_ge(mla_roped, 4 * l + t)
                    tt(w[0], x1, c, ALU.mult).then_inc(dve_steps, count())
                    tt(w[1], x2, s, ALU.mult).then_inc(dve_steps, count())
                    tt(w[2], x2, c, ALU.mult).then_inc(dve_steps, count())
                    tt(w[3], x1, s, ALU.mult).then_inc(dve_steps, count())
                    dve.wait_ge(dve_steps, count.n)
                    tt(x1, w[0], w[1], ALU.subtract).then_inc(dve_steps, count())
                    tt(x2, w[2], w[3], ALU.add).then_inc(mla_roped, 1)
                for t in range(TT):
                    c, s = (mcs[:, k, t, :] for k in range(2))
                    k1, k2 = cT[:, t, QR + KVR:QR + KVR + half], cT[:, t, QR + KVR + half:QR + KVR + ROPE]
                    w = [mt[:, k, 0, :] for k in range(4)]
                    dve.wait_ge(mla_roped, 4 * l + 2 + t)
                    tt(w[0], k1, c, ALU.mult).then_inc(dve_steps, count())
                    tt(w[1], k2, s, ALU.mult).then_inc(dve_steps, count())
                    tt(w[2], k2, c, ALU.mult).then_inc(dve_steps, count())
                    tt(w[3], k1, s, ALU.mult).then_inc(dve_steps, count())
                    dve.wait_ge(dve_steps, count.n)
                    every = [x.unsqueeze(1).broadcast_to([P, MLA_H, half]) for x in w]
                    tt(mk[:, t, :, NOPE:NOPE + half], every[0], every[1], ALU.subtract).then_inc(dve_steps, count())
                    tt(mk[:, t, :, NOPE + half:MQK], every[2], every[3], ALU.add).then_inc(mla_roped, 1)

            def ret_rope(l, i, t, b, read):
                half = RDK // 2
                w = [gt[:, k // 2, (k % 2) * 256:(k % 2 + 1) * 256].rearrange("p (h d) -> p h d", h=RH) for k in range(4)]
                v = b.rearrange("p (h d) -> p h d", h=RH)
                o = (rqT, rkT)[i][:, t, :].rearrange("p (h d) -> p h d", h=RH)
                c, s = (rcs[:, k, t, :].unsqueeze(1).broadcast_to([P, RH, half]) for k in range(2))
                if l + i + t > 0:
                    dve.wait_ge(ret_roped, 4 * l + 2 * i + t)
                tt(w[0], v[:, :, 0:half], c, ALU.mult).then_inc(dve_steps, count())
                tt(w[1], v[:, :, half:RDK], s, ALU.mult).then_inc(dve_steps, count())
                tt(w[2], v[:, :, half:RDK], c, ALU.mult).then_inc(dve_steps, count())
                tt(w[3], v[:, :, 0:half], s, ALU.mult).then_inc(read, 1)
                dve.wait_ge(read, 4 * l + 2 * i + t + 1)
                tt(o[:, :, 0:half], w[0], w[1], ALU.subtract).then_inc(dve_steps, count())
                tt(o[:, :, half:RDK], w[2], w[3], ALU.add).then_inc(ret_roped, 1)

            def residual(no, l, kind, gain):
                a = stats_of(f"L{l}.{kind}post", 8)
                dve.wait_ge(post_roots, no + 1)
                g = gain_row(dve, gain)
                for t in range(TT):
                    stt(hT[:, t, :], hT[:, t, :], a[:, 6 + t:7 + t], g).then_inc(dve_steps, count())
                scaled = count.n
                for t in range(TT):
                    dve.wait_ge(dve_steps, scaled - 1 + t)
                    tt(xT[:, t, :], xT[:, t, :], hT[:, t, :], ALU.add).then_inc(x_normed, 1)

            for l in range(DEPTH2):
                dve.wait_ge(x_updated, 8)
                if l > 0:
                    dve.wait_ge(x_normed, 4 * l)
                apply_norm(2 + 2 * l, f"L{l}.mix_pre")
                dve.memset(cp[:, :, 0:PAD], 0.0)
                dve.memset(cp[:, :, PAD + SEQ:], 0.0).then_inc(pads_zero, 1)
                turn_lo(f"L{l}.h", f_hi, f_lo, DT)
                run(12)
                turn_lo(f"L{l}.lat", c_hi, c_lo, 3)
                run(12)

                def taps(a, b):
                    dve.wait_ge(conv_in, 2 * (l + 1))
                    for n in range(a, b):
                        for k in range(4):
                            x = cp[:, k, n:n + SEQ]
                            if n == 0:
                                ts(cacc[:, k, :], x, cfp[:, k, 0:1], cfp[:, k, TAPS:TAPS + 1], ALU.mult, ALU.add).then_inc(dve_steps, count())
                            else:
                                dve.wait_ge(dve_steps, count.n - 3)
                                i = stt(cacc[:, k, :], x, cfp[:, k, n:n + 1], cacc[:, k, :], ALU.mult, ALU.add)
                                if n == TAPS - 1 and k == 3:
                                    i.then_inc(conv_summed, 1)
                                else:
                                    i.then_inc(dve_steps, count())

                def extra(i):
                    a, b = TAPS * i // 9, TAPS * (i + 1) // 9
                    mid = (a + b) // 2
                    taps(a, mid)
                    splits(pos + R)
                    taps(mid, b)

                heads(f"L{l}.mla", MLA_H, MV, m_st, HEADS + MLA_H * l, False, lambda t, h: mo[:, t, h, :], 36, extra)
                d_f, d_b = cst[:, C_DF:C_DB], cst[:, C_DB:C_INVR]
                dve.wait_ge(mixed, mix_at[f"L{l}.mla.o7"][0] + 1)
                for h in range(RH):
                    o = r_d[:, h, :, :].rearrange("p t k -> p (t k)")
                    c = 8 * l + h
                    ts(o, d_f, lg[:, c:c + 1], None, ALU.mult).then_inc(dve_steps, count())
                    dve.wait_ge(dve_steps, count.n)
                    stt(o, d_b, lg[:, c + RH:c + RH + 1], o, ALU.mult, ALU.add).then_inc(decay_args, 1)
                run(4)
                for h in range(RH):
                    dve.wait_ge(decays_made, RH * l + h + 1)
                    b = take(f"L{l}.rs{h}")
                    stt(r_s[:, h % 2, :, :].rearrange("p t k -> p (t k)"), b[:, :], RDK ** -0.5,
                        r_d[:, h, :, :].rearrange("p t k -> p (t k)")).then_inc(ret_scores, 1)
                turn_lo(f"L{l}.mo", f_hi, f_lo, 4)
                a = stats_of(f"L{l}.conv", 6)
                for t in range(TT):
                    b = take(f"L{l}.cback{t}")
                    dve.bn_stats(bns[:, t, 0:6], b[:, :]).then_inc(dve_steps, count())
                    dve.wait_ge(dve_steps, count.n)
                    dve.bn_aggr(a[:, 2 * t:2 * t + 2], bns[:, t, 0:6]).then_inc(conv_stats, 1)
                r = stats_of(f"L{l}.ret", 24)
                dve.wait_ge(ret_o_copied, RH * (l + 1))
                o_of = lambda t, h: (rqT, rkT)[h // 2][:, t, (h % 2) * RDV:(h % 2 + 1) * RDV]
                for t in range(TT):
                    for h in range(RH):
                        dve.bn_stats(bns[:, 2 + RH * t + h, 0:6], o_of(t, h)).then_inc(dve_steps, count())
                stats_done = count.n
                for t in range(TT):
                    dve.wait_ge(dve_steps, stats_done - RH * (1 - t))
                    for h in range(RH):
                        n = RH * t + h
                        i = dve.bn_aggr(r[:, 2 * n:2 * n + 2], bns[:, 2 + n, 0:6])
                        if n == 7:
                            i.then_inc(ret_stats, 1)
                        else:
                            i.then_inc(dve_steps, count())
                dve.wait_ge(conv_roots, l + 1)
                for t in range(TT):
                    b = mx[mix_at[f"L{l}.cback{t}"][0] % 2]
                    ts(gt[:, t, :], b[:, :], a[:, 2 * t:2 * t + 1], a[:, 4 + t:5 + t], ALU.subtract, ALU.mult).then_inc(conv_normed, 1)
                dve.wait_ge(mixed, mix_at[f"L{l}.ro3"][0] + 1)
                dve.wait_ge(ret_g_silu, 4 * (l + 1))
                dve.wait_ge(ret_stats, l + 1)
                for t in range(TT):
                    for h in range(RH):
                        n = RH * t + h
                        e = slice(h * RDV, (h + 1) * RDV)
                        stt(hT[:, t, e], o_of(t, h), r[:, 2 * n:2 * n + 1], rg[:, t, e], ALU.subtract, ALU.mult).then_inc(dve_steps, count())
                dve.wait_ge(ret_roots, l + 1)
                g = gain_row(dve, f"L{l}.gn")
                dve.wait_ge(dve_steps, count.n)
                for t in range(TT):
                    for h in range(RH):
                        n = RH * t + h
                        e = slice(h * RDV, (h + 1) * RDV)
                        i = stt(hT[:, t, e], hT[:, t, e], r[:, 16 + n:17 + n], g[:, e])
                        if h == RH - 1:
                            i.then_inc(ret_rows, 1)
                run(4)
                dve.wait_ge(conv_out_tanh, l + 1)
                flat = cacc[:, :, :].rearrange("p k t -> p (k t)")
                stt(flat, junk[:, :], 1.0, flat, ALU.add).then_inc(conv_silu, 1)
                dve.wait_ge(conv_hi, l + 1)
                stt(f_lo[:, 4:8, :].rearrange("p k t -> p (k t)"), flat, 0.5,
                    f_hi[:, 4:8, :].rearrange("p k t -> p (k t)").bitcast(F32), ALU.mult, ALU.subtract).then_inc(conv_split, 1)
                run(4)
                turn_lo(f"L{l}.ro", f_hi, f_lo, DT, 0.5)
                run(8)
                turn_lo(f"L{l}.merged", f_hi, f_lo, DT, 0.5)
                run(8)
                residual(2 * l, l, "out.", f"L{l}.mix_post")
                dve.wait_ge(x_normed, 4 * l + 2)
                apply_norm(3 + 2 * l, f"L{l}.ffn_pre")
                turn_lo(f"L{l}.h2", f_hi, f_lo, DT)
                for c in range(HT // 2 + 1):
                    if c < HT // 2:
                        run(4)
                    if c > 0:
                        turn_lo(f"L{l}.hid{c - 1}", h2_hi, h2_lo, 2, 0.5, 2 * (c - 1))
                run(22)
                residual(2 * l + 1, l, "down.", f"L{l}.ffn_post")

        @block.gpsimd
        def _(pool):
            count = Count()

            def tt(o, a, b, op):
                return pool.tensor_tensor(o, a, b, op)

            def load_gain(n):
                if n >= 2:
                    pool.wait_ge(GAINS[n - 2][1], GAINS[n - 2][2])
                pool.dma_start(gains[:, n % 2, :], rows[n, :].partition_broadcast(P)).then_inc(gain_in[n % 2], 16)

            def roots(o, sums, size, done):
                width = o.shape[1]
                pool.tensor_scalar(o, sums, 1.0 / size, EPS, ALU.mult, ALU.add).then_inc(pool_steps, count())
                pool.wait_ge(pool_steps, count.n)
                tt(o, o, minus_half[:, 0:width], ALU.pow).then_inc(done, 1)

            def roots_of_norm(no):
                pool.wait_ge(norm_sums, 2 * no + 2)
                a = stats_of(NORMS[no], 4)
                roots(a[:, 2:4], a[:, 0:2], D, norm_roots)

            load_gain(0)
            pool.dma_start(ab[:, :, :], ssm_ab).then_inc(ssm_in, 16)
            for e in range(2):
                pool.dma_start(pdt[64 * e:64 * e + 64, :], ssm_ldt[e, :].partition_broadcast(STATE)).then_inc(ssm_in, 16)
            pool.dma_start(posi[:, :], positions).then_inc(ssm_in, 16)
            pool.dma_start(lgw[:, 5, :], decay.partition_broadcast(P)).then_inc(decay_in, 16)
            pool.dma_start(bc[:, :, :, :], ssm_bc).then_inc(ssm_mats_in, 16)
            load_gain(1)
            pool.wait_ge(minus_half_set, 1)
            roots_of_norm(0)
            u8, v = par[:, 14:16, :], ev
            pool.wait_ge(turn_base, 1)
            pool.memset(turn[:, 0, :, 0:1], 1.0).then_inc(pool_steps, count())
            pool.memset(turn[:, 1, :, 0:1], 0.0).then_inc(pool_steps, count())
            pool.tensor_copy(v[:, 0:2, :], u8).then_inc(pool_steps, count())
            pool.tensor_copy(rho[:, :, :], par[:, 12, :].unsqueeze(2).broadcast_to([P, Q, NSUB])).then_inc(pool_steps, count())
            pool.wait_ge(pool_steps, count.n)
            pool.memset(rho[:, :, 0:1], 0.0).then_inc(pool_steps, count())
            n = 1
            while n < NSUB:
                a_r, a_i = (turn[:, c, :, 0:n] for c in range(2))
                b_r, b_i = (v[:, c, :].unsqueeze(2).broadcast_to([P, Q, n]) for c in range(2))
                w0, w1 = (x[:, 0:Q * n].rearrange("p (q k) -> p q k", k=n) for x in (
                    cm[:, 0, :, :].rearrange("p q n -> p (q n)"), cm[:, 1, :, :].rearrange("p q n -> p (q n)")))
                for o, x, y, op in ((0, b_r, b_i, ALU.subtract), (1, b_i, b_r, ALU.add)):
                    tt(w0, a_r, x, ALU.mult).then_inc(pool_steps, count())
                    tt(w1, a_i, y, ALU.mult).then_inc(pool_steps, count())
                    pool.wait_ge(pool_steps, count.n)
                    tt(turn[:, o, :, n:2 * n], w0, w1, op).then_inc(pool_steps, count())
                    pool.wait_ge(pool_steps, count.n)
                if 2 * n < NSUB:
                    tt(v[:, 2, :], v[:, 0, :], v[:, 0, :], ALU.mult).then_inc(pool_steps, count())
                    tt(v[:, 3, :], v[:, 1, :], v[:, 1, :], ALU.mult).then_inc(pool_steps, count())
                    tt(w0[:, :, 0:1].rearrange("p q k -> p (q k)"), v[:, 0, :], v[:, 1, :], ALU.mult).then_inc(pool_steps, count())
                    pool.wait_ge(pool_steps, count.n)
                    tt(v[:, 0, :], v[:, 2, :], v[:, 3, :], ALU.subtract).then_inc(pool_steps, count())
                    pool.tensor_scalar(v[:, 1, :], w0[:, :, 0:1].rearrange("p q k -> p (q k)"), 2.0, None, ALU.mult).then_inc(pool_steps, count())
                    pool.wait_ge(pool_steps, count.n)
                n *= 2
            pool.memset(ev[:, 3, 0:1], 0.0).then_inc(turns_made, 1)

            def c_mats(qd):
                if qd > 0:
                    pool.wait_ge(mixed, mix_at[f"ssm{qd - 1}.y1"][0] + 1)
                q0 = PQ * qd
                pr, pi = (pw[:, c, 1:SUB + 1, q0:q0 + PQ].rearrange("p m q -> p q m").unsqueeze(3).broadcast_to([P, PQ, SUB, GROUP]) for c in range(2))
                cr, ci = (bc[:, c, :, q0:q0 + PQ].rearrange("p c q -> p q c").unsqueeze(2).broadcast_to([P, PQ, SUB, GROUP]) for c in (2, 3))
                o = [cm[:, c, :, :].rearrange("p q (m c) -> p q m c", c=GROUP) for c in range(2)]
                for n, (x0, x1, op) in enumerate(((cr, ci, ALU.add), (ci, cr, ALU.subtract))):
                    tt(o[n], pr, x0, ALU.mult).then_inc(pool_steps, count())
                    if n == 1:
                        pool.wait_ge(pool_steps, count.n - 1)
                    elif qd > 0:
                        pool.wait_ge(c_mats_made, qd)
                    tt(tmp2[:, :, :, :], pi, x1, ALU.mult).then_inc(pool_steps, count())
                    pool.wait_ge(pool_steps, count.n)
                    i = tt(o[n], o[n], tmp2[:, :, :, :], op)
                    if n == 1:
                        i.then_inc(c_mats_made, 1)
                    else:
                        i.then_inc(pool_steps, count())

            def load_u(qd):
                pool.wait_ge(u_stored[qd // 2], 16 * TT)
                if qd > 0:
                    pool.wait_ge(u_ordered, qd)
                for j in range(JB):
                    col = qd * PCOLS + j * GB * GROUP
                    pool.dma_start(uk[32 * j:32 * j + 32, :, :],
                                   u_scr[:, col:col + GB * GROUP].rearrange("(k m) d -> k m d", m=SUB)).then_inc(u_sub_in, 16)

            pool.wait_ge(c_negated, 1)
            pool.wait_ge(powers_made, 1)
            c_mats(0)
            load_u(0)
            load_gain(2)
            for qd in range(PARTS):
                if qd + 1 < PARTS:
                    load_u(qd + 1)
                pool.wait_ge(y_stored, 16 * JB * (qd + 1))
                for t in range(TT):
                    cols = slice(qd * PCOLS, (qd + 1) * PCOLS)
                    pool.dma_start(yT[:, t, cols], y_scr[t * P:(t + 1) * P, cols]).then_inc(y_in, 16)
                if qd + 1 < PARTS:
                    c_mats(qd + 1)
            load_gain(3)
            load_gain(4)
            roots_of_norm(1)
            pool.wait_ge(rows_normed, 4)
            for n in range(2):
                pool.dma_start(qkg[:, n, :], qk_gain[n, :].partition_broadcast(P)).then_inc(qk_gain_in, 16)
            for i in range(4):
                pool.wait_ge(squares_summed, 2 * i + 2)
                a = stats_of(f"qk{i}", 16)
                roots(a[:, 8:16], a[:, 0:8], HD, qk_roots)
            load_gain(5)
            for l in range(DEPTH2):
                if l == 0:
                    pool.wait_ge(x_updated, 8)
                else:
                    pool.wait_ge(x_normed, 4 * l)
                roots_of_norm(2 + 2 * l)
                pool.dma_start(latp[:, 0:QR], lat_gain[l, 0:QR].partition_broadcast(P)).then_inc(layer_params_in, 16)
                pool.dma_start(latp[:, QR:QR + KVR], lat_gain[l, QR:QR + KVR].partition_broadcast(P)).then_inc(layer_params_in, 16)
                pool.dma_start(cfp[:, :, :], conv_p[l]).then_inc(layer_params_in, 16)
                load_gain(6 + 5 * l)
                a = stats_of(f"L{l}.lat", 8)
                pool.wait_ge(lat_sums, 4 * (l + 1))
                pool.tensor_scalar(a[:, 4:6], a[:, 0:2], 1.0 / QR, EPS, ALU.mult, ALU.add).then_inc(pool_steps, count())
                pool.tensor_scalar(a[:, 6:8], a[:, 2:4], 1.0 / KVR, EPS, ALU.mult, ALU.add).then_inc(pool_steps, count())
                pool.wait_ge(pool_steps, count.n)
                tt(a[:, 4:8], a[:, 4:8], minus_half[:, 0:4], ALU.pow).then_inc(lat_roots, 1)
                a = stats_of(f"L{l}.conv", 6)
                pool.wait_ge(conv_stats, 2 * (l + 1))
                roots(a[:, 4:6], a[:, 0:4].rearrange("p (t m) -> p m t", m=2)[:, 1], 1.0, conv_roots)
                r = stats_of(f"L{l}.ret", 24)
                pool.wait_ge(ret_stats, l + 1)
                roots(r[:, 16:24], r[:, 0:16].rearrange("p (n m) -> p m n", m=2)[:, 1], 1.0, ret_roots)
                load_gain(7 + 5 * l)
                for kind in ("out.", "down."):
                    a = stats_of(f"L{l}.{kind}post", 8)
                    no = 2 * l + (kind == "down.")
                    pool.wait_ge(post_sums, 4 * (no + 1))
                    v = a[:, 0:4].rearrange("p (t c) -> p c t", c=2)
                    tt(a[:, 4:6], v[:, 0], v[:, 1], ALU.add).then_inc(pool_steps, count())
                    pool.wait_ge(pool_steps, count.n)
                    roots(a[:, 6:8], a[:, 4:6], D, post_roots)
                    if kind == "out.":
                        load_gain(8 + 5 * l)
                        roots_of_norm(3 + 2 * l)
                        if l + 1 < DEPTH2:
                            load_gain(9 + 5 * l)
                if l + 1 < DEPTH2:
                    load_gain(10 + 5 * l)


def lay_out(inputs):
    a = {k: np.asarray(v) for k, v in inputs.items()}
    table, slots, total = weight_plan()

    def weights(name):
        l, kind = (int(name[1]), name.split(".", 1)[1]) if name[0] == "L" else (0, name)
        base = kind.rstrip("0123456789")
        i = int(kind[len(base):])
        c = slice(512 * i, 512 * (i + 1))
        if name[0] != "L":
            return {"ssm_in.": a["ssm_w_in"], "glu.": a["ssm_w_glu"], "ssm_out.": a["ssm_w_out"],
                    "attn_in.": a["attn_w_in"], "attn_out.": a["attn_w_out"]}[base][0][:, c]
        w_in = a["w_in_2"][l]
        lat, conv = QR + KVR + ROPE, 2 * CONV
        ret = 2 * RH * RDK + 2 * RH * RDV
        if base == "lat.":
            return w_in[:, 0:lat]
        if base == "glu.":
            return w_in[:, lat:lat + conv][:, c]
        if base == "ret.":
            return w_in[:, lat + conv:lat + conv + ret][:, c]
        if base == "gate.":
            return w_in[:, lat + conv + ret:][:, c]
        if base == "uq.":
            return a["mla_w_uq_2"][l][:, 384 * i:384 * (i + 1)]
        if base == "ffn.":
            f = slice(FCH * i, FCH * (i + 1))
            return np.concatenate([a["ffn_w_gate_2"][l][:, f], a["ffn_w_up_2"][l][:, f]], axis=1)
        return a[{"ukv.": "mla_w_ukv_2", "mla_o.": "mla_w_o_2", "conv_o.": "conv_w_pw_2", "ret_o.": "ret_w_o_2",
                  "out.": "w_out_2", "down.": "ffn_w_down_2"}[base]][l][:, c]

    parts, block, last = [], None, None
    for s in slots:
        if s["chunk"] != last:
            last = s["chunk"]
            block = weights(last)
        rows = block[s["k"] * P:(s["k"] + s["nk"]) * P]
        parts.append(rows.reshape(s["nk"], P, s["width"]).transpose(1, 0, 2).reshape(-1))

    def pairs(x):
        x = x.reshape(Q, 2, STATE, *x.shape[2:])
        return np.moveaxis(x, 0, -1).reshape(2 * STATE, *x.shape[3:], Q)

    def gain_rows():
        rows = [a["norm_g"][0], a["ssm_d"][0], a["ssm_b_glu"][0], a["norm_g"][1]]
        for l in range(DEPTH2):
            rows += [a["ln_mix_pre_2"][l], a["ret_gn_g_2"][l], a["ln_mix_post_2"][l], a["ln_ffn_pre_2"][l], a["ln_ffn_post_2"][l]]
        return np.stack(rows)

    conv = np.stack([np.concatenate([a["conv_w_dw_2"][l], a["conv_b_dw_2"][l][None], a["conv_ln_g_2"][l][None], a["conv_ln_b_2"][l][None]])
                     for l in range(DEPTH2)])
    return {
        "stream": np.concatenate(parts),
        "consts": shape_constants(),
        "x_in": a["x"][0].reshape(TT, P, D).transpose(1, 0, 2),
        "ssm_ab": np.stack([pairs(a["ssm_a_re"][0]), pairs(a["ssm_a_im"][0])], axis=1),
        "ssm_ldt": a["ssm_log_dt"][0].reshape(Q, 2).T,
        "ssm_bc": np.stack([pairs(a["ssm_b_re"][0]), pairs(a["ssm_b_im"][0]),
                            pairs(a["ssm_c_re"][0].transpose(0, 2, 1)), pairs(a["ssm_c_im"][0].transpose(0, 2, 1))], axis=1),
        "rows": gain_rows(),
        "qk_gain": np.stack([a["attn_q_gain"][0], a["attn_k_gain"][0]]),
        "positions": a["positions_2"][0].reshape(TT, P).T,
        "decay": a["ret_decay_logits_2"].reshape(-1),
        "conv_p": conv.reshape(DEPTH2, TAPS + 3, 4, P).transpose(0, 3, 2, 1),
        "lat_gain": np.concatenate([a["mla_q_norm_2"], a["mla_kv_norm_2"]], axis=1),
    }


def kernel(**inputs):
    import concourse.bacc as bacc
    from concourse.bass_utils import run_bass_kernel_spmd

    nc = bacc.Bacc("TRN2", target_bir_lowering=False, num_devices=1)
    arrays, args = {}, {}
    for name, x in lay_out(inputs).items():
        x = np.ascontiguousarray(x)
        arrays[name + "_dram"] = x
        args[name] = nc.dram_tensor(name + "_dram", x.shape, mybir.dt.from_np(x.dtype), kind="ExternalInput").ap()
    args["out"] = nc.dram_tensor("out_dram", (P, TT, D), F32, kind="ExternalOutput").ap()
    build(nc, **args)
    r = run_bass_kernel_spmd(nc, [arrays], core_ids=[0])
    return r.results[0]["out_dram"].transpose(1, 0, 2).reshape(1, SEQ, D)
```

```python
import math
from contextlib import ExitStack

import numpy as np

import concourse.bass as bass
from concourse import mybir

F32 = mybir.dt.float32
F32R = mybir.dt.float32r
I32 = mybir.dt.int32
ALU = mybir.AluOpType
ACT = mybir.ActivationFunctionType
AX = mybir.AxisListType.X

P = 128
SEQ = 256
TT = SEQ // P
D = 1024
DT = D // P
EPS = 1e-6

GROUPS, GROUP, STATE = 64, 16, 64
SUB = 8
NSUB = SEQ // SUB
Q = GROUPS // 2
PARTS = 4
PQ = Q // PARTS
PCOLS = D // PARTS
JB = P // NSUB
GB = GROUPS // PARTS // JB

HEADS, HD = 8, 128
ROT = HD // 4
DEPTH2 = 2
MLA_H, NOPE, ROPE, MV = 8, 64, 32, 64
MQK = NOPE + ROPE
QR, KVR = 256, 128
CONV, TAPS = 512, 31
PAD = TAPS // 2
RH, RDK, RDV = 4, 128, 256
HID = 2816
HT = HID // P
FCH = 256

SIDE_TAPS = 10
R = 4
SLOT = 1024


def weight_plan():
    chunks = []

    def add(name, n, width, ktiles):
        slots = [(k, min(2, ktiles - k)) for k in range(0, ktiles, 2)]
        for i in range(n):
            chunks.append((f"{name}{i}", width, slots))

    add("ssm_in.", 4, 512, DT)
    add("glu.", 2, 512, DT)
    add("ssm_out.", 2, 512, DT)
    add("attn_in.", 8, 512, DT)
    add("attn_out.", 2, 512, DT)
    for l in range(DEPTH2):
        add(f"L{l}.lat.", 1, QR + KVR + ROPE, DT)
        add(f"L{l}.glu.", 2, 512, DT)
        add(f"L{l}.uq.", 2, 384, QR // P)
        add(f"L{l}.ukv.", 2, 512, KVR // P)
        add(f"L{l}.ret.", 6, 512, DT)
        add(f"L{l}.gate.", 6, 512, DT)
        add(f"L{l}.mla_o.", 2, 512, 4)
        add(f"L{l}.ret_o.", 2, 512, DT)
        add(f"L{l}.conv_o.", 2, 512, 4)
        add(f"L{l}.out.", 2, 512, DT)
        add(f"L{l}.ffn.", HID // FCH, 2 * FCH, DT)
        add(f"L{l}.down.", 2, 512, HT)
    slot, off, table, slots = 0, 0, {}, []
    for c, (name, width, parts) in enumerate(chunks):
        table[name] = dict(index=c, width=width, first=slot, n=len(parts))
        for k, nk in parts:
            slots.append(dict(chunk=name, k=k, nk=nk, width=width, off=off))
            off += P * nk * width
            slot += 1
    return table, slots, off


def rope_tables_host(dim, theta, n):
    half = dim // 2
    inv = (np.float32(theta) ** (-(np.arange(half, dtype=np.float32) * np.float32(2.0)) / np.float32(dim))).astype(np.float32)
    ang = np.arange(n, dtype=np.float32)[:, None] * inv[None, :]
    return np.cos(ang.astype(np.float64)).astype(np.float32), np.sin(ang.astype(np.float64)).astype(np.float32)


C_ID, C_MASK = 0, 128
C_COS1 = C_MASK + TT * SEQ
C_SIN1 = C_COS1 + TT * ROT // 2
C_DF = C_SIN1 + TT * ROT // 2
C_DB = C_DF + TT * SEQ
C_INVR = C_DB + TT * SEQ
C_INVM = C_INVR + RDK // 2
N_CONST = C_INVM + ROPE // 2
N_ANG = GROUPS // 2 + RDK + ROPE

NORMS = ["hn", "h1"] + [f"L{l}.{n}" for l in range(DEPTH2) for n in ("h", "h2")]


def shape_constants():
    c = np.zeros((P, N_CONST), np.float32)
    c[:, C_ID:C_ID + P] = np.eye(P, dtype=np.float32)
    q = np.arange(SEQ).reshape(TT, P).T
    k = np.arange(SEQ)
    c[:, C_MASK:C_MASK + TT * SEQ] = np.where(k[None, None, :] <= q[:, :, None], 0.0, -1e30).reshape(P, -1)
    cos, sin = rope_tables_host(ROT, 500000.0, SEQ)
    c[:, C_COS1:C_SIN1] = cos.reshape(TT, P, -1).transpose(1, 0, 2).reshape(P, -1)
    c[:, C_SIN1:C_DF] = sin.reshape(TT, P, -1).transpose(1, 0, 2).reshape(P, -1)
    c[:, C_DF:C_DB] = np.maximum(k[None, None, :] - q[:, :, None], 0).reshape(P, -1)
    c[:, C_DB:C_INVR] = np.maximum(q[:, :, None] - k[None, None, :], 0).reshape(P, -1)
    base = np.float32(10000.0)
    c[:, C_INVR:C_INVM] = (base ** (-np.arange(0, RDK, 2, dtype=np.float32) / np.float32(RDK)))[None]
    c[:, C_INVM:N_CONST] = (base ** (-np.arange(0, ROPE, 2, dtype=np.float32) / np.float32(ROPE)))[None]
    return c


TWO_PI = 2.0 * math.pi
PI_A = 6.28125
PI_B = float(np.float32(round((TWO_PI - PI_A) * 2.0 ** 21) / 2.0 ** 21))
PI_C = TWO_PI - PI_A - PI_B
ROUND = 12582912.0
PI_IN = 3.1415925



class Count:

    def __init__(self):
        self.n = 0

    def __call__(self):
        self.n += 1
        return 1


def build(nc, stream, consts, x_in, ssm_ab, ssm_ldt, ssm_bc, rows, qk_gain, positions, decay, conv_p, lat_gain, out):
    table, slots, _ = weight_plan()
    NS = len(slots)
    u_scr = nc.dram_tensor("u_scratch", [SEQ, D], F32, kind="Internal").ap()
    y_scr = nc.dram_tensor("y_scratch", [SEQ, D], F32, kind="Internal").ap()

    ctx = ExitStack()
    with ctx:
        def sb(name, shape, dt=F32, scope=None):
            return (scope or ctx).enter_context(nc.sbuf_tensor(name, shape, dt))

        def sem(name):
            return ctx.enter_context(nc.semaphore(name))

        raw = sb("weights_raw", [P, R, SLOT])
        w_hi = sb("weights_hi", [P, R, SLOT], F32R)
        w_lo = sb("weights_lo", [P, R, SLOT], F32R)
        const = sb("consts", [P, N_CONST])
        ident = const[:, C_ID:C_ID + P]
        xT = sb("x_T", [P, TT, D])
        hT = sb("h_T", [P, TT, D])
        gains = sb("gains", [P, 2, D])
        junk = sb("junk", [P, D])
        stat = sb("stat", [P, 256])
        minus_half = sb("minus_half", [P, 16])
        lg = sb("log_gamma", [P, 16])
        lgw = sb("log_gamma_work", [P, 6, 16])
        ret_rot = sb("ret_cos_sin", [P, 2, TT, RDK // 2])
        mla_rot = sb("mla_cos_sin", [P, 2, TT, ROPE // 2])
        posf = sb("positions_f", [P, TT])
        posi = sb("positions_i", [P, TT], I32)

        with ExitStack() as s0:
            f0_hi = sb("hn_F_hi", [P, DT, SEQ], F32R, s0)
            f0_lo = sb("hn_F_lo", [P, DT, SEQ], F32R, s0)
        with ExitStack() as s0:
            toep = sb("toeplitz", [P, 2, SUB, PCOLS], F32, s0)
        f_hi = sb("act_F_hi", [P, DT, SEQ], F32R)
        f_lo = sb("act_F_lo", [P, DT, SEQ], F32R)

        with ExitStack() as s1:
            uT = sb("u_T", [P, TT, D], F32, s1)
            zT = sb("z_T", [P, TT, D], F32, s1)
            ab = sb("ssm_ab", [P, 2, Q], F32, s1)
            pdt = sb("ssm_dt", [P, Q], F32, s1)
            par = sb("ssm_par", [P, 20, Q], F32, s1)
            pw = sb("powers", [P, 2, SUB + 1, Q], F32, s1)
            pwb = sb("powers_reversed", [P, 2, SUB, Q], F32, s1)
            bc = sb("ssm_bc", [P, 4, GROUP, Q], F32, s1)
            turn = sb("turns", [P, 2, Q, NSUB], F32, s1)
            rho = sb("decays", [P, Q, NSUB], F32, s1)
            b_mat = sb("b_mats", [P, 2, PQ, SUB * GROUP], F32, s1)
            c_mat = sb("c_mats", [P, 2, 2, PQ, SUB * GROUP], F32, s1)
            b_mat_T = sb("b_mats_T", [P, 2, PQ, P], F32, s1)
            c_pair = sb("c_pairs", [P, 2, PQ, 2, GROUP], F32, s1)
            taps_sb = sb("taps", [P, 2 * P], F32, s1)
            taps_T = sb("taps_T", [P, PQ, 2, GROUP], F32, s1)
            u_sub = sb("u_sub", [P, 2, SUB, GB * GROUP], F32, s1)
            u_by_group = sb("u_by_group", [P, GB, SUB, GROUP], F32, s1)
            u_group_F = sb("u_groups", [P, 2, GB, P], F32, s1)
            scan_w = sb("scan_work", [P, 4, PQ, NSUB], F32, s1)
            st = sb("states", [P, 2, 2, PQ, NSUB], F32, s1)
            y_sub = sb("y_sub", [P, SUB, GB * GROUP], F32, s1)
            gelu_w = sb("gelu_work", [P, TT, PCOLS], F32, s1)
            tmp2 = sb("c_mat_tmp", [P, PQ, SUB, GROUP], F32, s1)
            ev = sb("turn_step", [P, 4, Q], F32, s1)
            yT = hT
        with ExitStack() as s2:
            qT = sb("q_T", [P, TT, D], F32, s2)
            kT = sb("k_T", [P, TT, D], F32, s2)
            vT = sb("v_T", [P, TT, D], F32, s2)
            szT = sb("silu_z_T", [P, TT, D], F32, s2)
            qkg = sb("qk_gain", [P, 2, HD], F32, s2)
            sq = sb("squares", [P, TT, 512], F32, s2)
            ropt = sb("rope_tmp", [P, TT, 4, 64], F32, s2)
            a_qk = sb("a_qk_F", [P, 2, 512], F32, s2)
            a_s = sb("a_scores", [P, 2, TT, SEQ], F32, s2)
            a_p = sb("a_probs", [P, 2, TT, SEQ], F32, s2)
            a_pt = sb("a_probs_T", [P, 2, TT, TT, P], F32, s2)
            a_st = sb("a_stat", [P, 2, 8], F32, s2)
        with ExitStack() as s3:
            h2_hi = sb("ffn_F_hi", [P, HT, SEQ], F32R, s3)
            h2_lo = sb("ffn_F_lo", [P, HT, SEQ], F32R, s3)
            ffn_t = sb("ffn_tanh_rows", [P, 2, TT, FCH], F32, s3)
            ffn_h = sb("ffn_h", [P, 2, TT, FCH], F32, s3)
        with ExitStack() as s4:
            latp = sb("lat_gain", [P, QR + KVR], F32, s4)
            cfp = sb("conv_params", [P, 4, TAPS + 3], F32, s4)
            c_hi = sb("lat_F_hi", [P, 3, SEQ], F32R, s4)
            c_lo = sb("lat_F_lo", [P, 3, SEQ], F32R, s4)
            mla_o = sb("mla_o_T", [P, TT, MLA_H, MV], F32, s4)
            conv_a = sb("conv_a", [P, TT, CONV], F32, s4)
            conv_t = sb("conv_tanh", [P, TT, CONV], F32, s4)
            conv_F = sb("conv_in_F", [P, 4, SEQ + 2 * PAD], F32, s4)
            conv_sum = sb("conv_acc_F", [P, 4, SEQ], F32, s4)
            bns = sb("bn_stats", [P, 10, 8], F32, s4)
            rope_w = conv_t[:, 0, :].rearrange("p (k h d) -> p k h d", k=4, h=MLA_H)
            rqT = sb("ret_q_T", [P, TT, 512], F32, s4)
            rkT = sb("ret_k_T", [P, TT, 512], F32, s4)
            ret_g = sb("ret_g_T", [P, TT, D], F32, s4)
            gates = sb("gates_T", [P, 3, TT, D], F32, s4)
            with ExitStack() as s5:
                cT = sb("lat_T", [P, TT, QR + KVR + ROPE], F32, s5)
                cnT = sb("lat_norm_T", [P, TT, QR + KVR], F32, s5)
            r_d = sb("r_decay_T", [P, RH, TT, SEQ], F32, s4)
            with ExitStack() as s5:
                mq = sb("mla_q_T", [P, TT, MLA_H, MQK], F32, s5)
                mk = sb("mla_k_T", [P, TT, MLA_H, MQK], F32, s5)
                mv = sb("mla_v_T", [P, TT, MLA_H, MV], F32, s5)
                m_qk = sb("m_qk_F", [P, 2, 512], F32, s5)
                m_p = sb("m_probs", [P, 2, TT, SEQ], F32, s5)
                m_pt = sb("m_probs_T", [P, 2, TT, TT, P], F32, s5)
                m_st = sb("m_stat", [P, 2, 8], F32, s5)
            with ExitStack() as s6:
                r_qk = sb("r_qk_F", [P, RH, 512], F32, s6)
                r_s = sb("r_scores_T", [P, 2, TT, SEQ], F32, s6)
                cf_hi = sb("conv_F_hi", [P, 4, SEQ], F32R, s6)
                cf_lo = sb("conv_F_lo", [P, 4, SEQ], F32R, s6)
        rv = hT

        acc = [[ctx.enter_context(nc.psum_tensor(f"acc{p}{t}", [P, 512], F32)) for t in range(TT)] for p in range(2)]
        turned_bank = [ctx.enter_context(nc.psum_tensor(f"turned{i}", [P, 512], F32)) for i in range(2)]
        mixed_bank = [ctx.enter_context(nc.psum_tensor(f"mixed{i}", [P, 512], F32)) for i in range(2)]

        consts_in, x_ld, ssm_in = sem("consts_in"), sem("x_in"), sem("ssm_in")
        raw_in = [sem(f"weights_in{i}") for i in range(R)]
        hi_made = sem("weights_hi_made")
        lo_made = sem("weights_lo_made")
        slot_used = sem("slots_used")
        turned = sem("turned_ready")
        turned_hi = sem("turned_hi_made")
        turned_lo = sem("turned_lo_made")
        mixed = sem("mixed_ready")

        dt_exp = sem("dt_exp")
        norm_sums = sem("norm_sums")
        norm_roots = sem("norm_roots")
        rows_normed = sem("rows_normed")
        ssm_rates = sem("ssm_rates")
        ssm_mag = sem("ssm_mag")
        decay_abs = sem("decay_abs")
        decay_exp = sem("decay_exp")
        angles = sem("angles")
        sines = sem("sines")
        turn_base = sem("turn_base")
        turns_made = sem("turns_made")
        powers_made = sem("powers_made")
        c_negated = sem("c_negated")
        minus_half_set = sem("minus_half_set")
        toeplitz_zero = sem("toeplitz_zero")
        b_mats_made = sem("b_mats_made")
        c_mats_made = sem("c_mats_made")
        c_pairs_zero = sem("c_pairs_zero")
        c_paired = sem("c_paired")
        taps_out = sem("taps_out")
        taps_copied = sem("taps_copied")
        b_T_copied = sem("b_T_copied")
        y_ready = sem("y_ready")
        u_copied = sem("u_copied")
        z_tanh = sem("z_tanh")
        z_silu = sem("z_silu")
        u_ordered = sem("u_ordered")
        u_groups_copied = sem("u_groups_copied")
        state_terms_read = sem("state_terms_read")
        states_made = sem("states_made")
        y_copied = sem("y_copied")
        gelu_in = sem("gelu_in")
        gelu_tanh_made = sem("gelu_tanh_made")
        gelu_made = sem("gelu_made")
        glu_biased = sem("glu_biased")
        glu_tanh = sem("glu_tanh")
        glu_rows = sem("glu_rows")
        x_updated = sem("x_updated")
        squares_made = sem("squares_made")
        squares_summed = sem("squares_summed")
        qk_roots = sem("qk_roots")
        attn_qk_roped = sem("attn_qk_roped")
        v_copied = sem("v_copied")
        attn_z_tanh = sem("attn_z_tanh")
        attn_z_silu = sem("attn_z_silu")
        attn_rows = sem("attn_rows")
        qk_copied = sem("qk_copied")
        scores_masked = sem("scores_masked")
        max_found = sem("max_found")
        probs_made = sem("probs_made")
        probs_T_copied = sem("probs_T_copied")
        outs_scaled = sem("outs_scaled")
        lat_copied = sem("lat_copied")
        lat_sums = sem("lat_sums")
        lat_roots = sem("lat_roots")
        lat_rows = sem("lat_rows")
        conv_a_copied = sem("conv_a_copied")
        conv_tanh_made = sem("conv_tanh_made")
        conv_glu_rows = sem("conv_glu_rows")
        conv_in = sem("conv_in")
        pads_zero = sem("pads_zero")
        conv_side = sem("conv_side")
        conv_summed = sem("conv_summed")
        conv_stats = sem("conv_stats")
        conv_roots = sem("conv_roots")
        conv_normed = sem("conv_normed")
        conv_affine = sem("conv_affine")
        conv_out_tanh = sem("conv_out_tanh")
        conv_silu = sem("conv_silu")
        conv_hi = sem("conv_hi")
        conv_split = sem("conv_split")
        mla_q_copied = sem("mla_q_copied")
        mla_v_copied = sem("mla_v_copied")
        mla_roped = sem("mla_roped")
        ret_rope_read = sem("ret_rope_read")
        ret_roped = sem("ret_roped")
        ret_v_copied = sem("ret_v_copied")
        ret_g_tanh = sem("ret_g_tanh")
        ret_g_silu = sem("ret_g_silu")
        ret_qk_copied = sem("ret_qk_copied")
        lg_made = sem("lg_made")
        decay_args = sem("decay_args")
        decays_made = sem("decays_made")
        ret_scores = sem("ret_scores")
        ret_o_copied = sem("ret_o_copied")
        ret_g_gained = sem("ret_g_gained")
        ret_normed = sem("ret_normed")
        ret_stats = sem("ret_stats")
        ret_roots = sem("ret_roots")
        ret_rows = sem("ret_rows")
        gate_tanh = sem("gate_tanh")
        mla_weighed = sem("mla_weighed")
        conv_weighed = sem("conv_weighed")
        ret_weighed = sem("ret_weighed")
        merged = sem("merged")
        mix_scaled = sem("mix_scaled")
        ffn_scaled = sem("ffn_scaled")
        post_sums = sem("post_sums")
        post_roots = sem("post_roots")
        x_normed = sem("x_normed")
        ffn_tanh = sem("ffn_tanh")
        ffn_rows = sem("ffn_rows")
        decay_in = sem("decay_in")
        ssm_mats_in = sem("ssm_mats_in")
        u_sub_in = [sem(f"u_sub_in{i}") for i in range(2)]
        toeplitz_in = sem("toeplitz_in")
        y_stored = sem("y_stored")
        y_in = sem("y_in")
        qk_gain_in = sem("qk_gain_in")
        layer_params_in = sem("layer_params_in")
        out_stored = sem("out_stored")
        dve_steps = sem("dve_steps")
        pool_steps = sem("pool_steps")
        tables_in = sem("tables_in")
        u_stored = [sem(f"u_stored{i}") for i in range(2)]

        mix_at, turn_at = {}, {}

        stat_cols = {}

        def stats_of(name, n):
            if name not in stat_cols:
                stat_cols[name] = (sum(k for _, k in stat_cols.values()), n)
            a = stat_cols[name][0]
            return stat[:, a:a + n]

        def split_name(name):
            layer = int(name[1]) if name[0] == "L" else 0
            kind = name.split(".", 1)[1] if name[0] == "L" else name
            base = kind.rstrip("0123456789")
            return layer, base, int(kind[len(base):])

        def reader_of(name, t):
            l, kind, i = split_name(name)
            n = 2 * i + t + 1
            return {
                "ssm_in.": (u_copied, n) if i < 2 else (z_silu, n - 4),
                "glu.": ((glu_biased, n) if name[0] != "L" else
                         (conv_a_copied, 2 * l + t + 1) if i == 0 else (conv_tanh_made, 2 * l + t + 1)),
                "ssm_out.": (x_updated, n), "attn_out.": (x_updated, 4 + n),
                "attn_in.": (squares_made, n) if i < 4 else (v_copied, n - 8) if i < 6 else (attn_z_silu, n - 12),
                "lat.": (lat_copied, 2 * l + t + 1),
                "uq.": (mla_q_copied, 4 * l + n), "ukv.": (mla_v_copied, 4 * l + n),
                "ret.": ((ret_rope_read, 4 * l + n) if i < 2 else (ret_v_copied, 4 * l + n - 4) if i < 4
                         else (ret_g_silu, 4 * l + n - 8)),
                "gate.": (gate_tanh, 12 * l + n),
                "mla_o.": (mla_weighed, 4 * l + n), "conv_o.": (conv_weighed, 4 * l + n),
                "ret_o.": (ret_weighed, 4 * l + n),
                "out.": (mix_scaled, 4 * l + n), "down.": (ffn_scaled, 4 * l + n),
                "ffn.": (ffn_rows, HT * l + n),
            }[kind]

        GAINS = [("norm0", rows_normed, 2), ("d_skip", gelu_made, 4), ("b_glu", glu_biased, 4),
                 ("norm1", rows_normed, 4)]
        for l in range(DEPTH2):
            GAINS += [(f"L{l}.mix_pre", rows_normed, 6 + 4 * l), (f"L{l}.gn", ret_g_gained, l + 1),
                      (f"L{l}.mix_post", mix_scaled, 4 * l + 4), (f"L{l}.ffn_pre", rows_normed, 8 + 4 * l),
                      (f"L{l}.ffn_post", ffn_scaled, 4 * l + 4)]
        gain_no = {g[0]: n for n, g in enumerate(GAINS)}
        gain_in = [sem(f"gain_in{i}") for i in range(2)]

        def gain_row(eng, name):
            n = gain_no[name]
            eng.wait_ge(gain_in[n % 2], 16 * (n // 2 + 1))
            return gains[:, n % 2, :]

        def chunks_ending(a, b):
            return [(n, c["first"] + c["n"]) for n, c in table.items() if a < c["first"] + c["n"] <= b]

        def splitter(make):
            state = [0]

            def upto(n):
                while state[0] < min(n, NS):
                    make(state[0])
                    state[0] += 1
            return upto

        def banks_of(eng, name):
            c = table[name]
            eng.wait_ge(slot_used, c["first"] + c["n"])
            return [acc[c["index"] % 2][t][:, 0:c["width"]] for t in range(TT)]

        block = ctx.enter_context(nc.Block())

        @block.tensor
        def _(pe):
            pos = 0
            acc_user = [None, None]
            mix_user = [None, None]

            def f_tiles(chunk):
                if ".uq." in chunk:
                    return c_hi, c_lo, 0
                if ".ukv." in chunk:
                    return c_hi, c_lo, QR // P
                if ".down." in chunk:
                    return h2_hi, h2_lo, 0
                if ".conv_o." in chunk:
                    return cf_hi, cf_lo, 0
                return (f0_hi, f0_lo, 0) if chunk.startswith("ssm_in") else (f_hi, f_lo, 0)

            def run(n):
                nonlocal pos
                for _ in range(n):
                    s = slots[pos]
                    c = table[s["chunk"]]
                    par, w = c["index"] % 2, s["width"]
                    hi, lo, k0 = f_tiles(s["chunk"])
                    first, last = pos == c["first"], pos == c["first"] + c["n"] - 1
                    pe.wait_ge(lo_made, pos + 1)
                    for t in range(TT):
                        if first and acc_user[par]:
                            who, value = reader_of(acc_user[par], t)
                            pe.wait_ge(who, value)
                        for kk in range(s["nk"]):
                            k = k0 + s["k"] + kk
                            wh = w_hi[:, pos % R, kk * w:(kk + 1) * w]
                            wl = w_lo[:, pos % R, kk * w:(kk + 1) * w]
                            xh, xl = (f[:, k, t * P:(t + 1) * P] for f in (hi, lo))
                            o = acc[par][t][:, 0:w]
                            pe.matmul(o, xh, wh, start=first and kk == 0, stop=False)
                            pe.matmul(o, xh, wl, start=False, stop=False)
                            i = pe.matmul(o, xl, wh, start=False, stop=last and kk == s["nk"] - 1)
                    i.then_inc(slot_used, 1)
                    acc_user[par] = s["chunk"]
                    pos += 1

            def mix(name, who, value):
                n = len(mix_at)
                mix_at[name] = (n, pos)
                if mix_user[n % 2]:
                    pe.wait_ge(mix_user[n % 2][0], mix_user[n % 2][1])
                mix_user[n % 2] = (who, value)
                return mixed_bank[n % 2]

            def turn(name, ktiles, src, ready, feeds=False, late=None):
                start = len(turn_at)
                fed = start

                def feed(upto):
                    nonlocal fed
                    while fed < upto:
                        fed += 1
                        pe.wait_ge(turned_lo, fed)
                        run(1)

                for k in range(0, ktiles, 2):
                    if k == late:
                        feed(len(turn_at))
                    n = len(turn_at)
                    turn_at[f"{name}.{k // 2}"] = (n, pos)
                    if n >= 2:
                        pe.wait_ge(turned_lo, n - 1)
                    for t in range(TT):
                        who, value = ready(t, k)
                        pe.wait_ge(who, value)
                        for kk in range(min(2, ktiles - k)):
                            i = pe.transpose(turned_bank[n % 2][:, kk * SEQ + t * P:kk * SEQ + (t + 1) * P], src(t, k + kk), ident)
                    i.then_inc(turned, 1)
                    if feeds:
                        feed(n - 1)
                if feeds:
                    feed(len(turn_at))

            def split_made():
                pe.wait_ge(turned_lo, len(turn_at))

            def tiles_of(tensor):
                return lambda t, k: tensor[:, t, k * P:(k + 1) * P]

            pe.wait_ge(consts_in, 16)
            turn("hn", DT, tiles_of(hT), lambda t, k: (rows_normed, t + 1), True)
            run(12)

            def taps_and_turned_b(qd, between):
                pe.wait_ge(b_mats_made, qd + 1)
                pe.wait_ge(c_paired, 2 * (qd + 1))
                b = mix(f"ssm{qd}.taps", taps_out, qd + 1)
                for q in range(PQ):
                    o = b[32 * (q % 4):32 * (q % 4) + 32, (q // 4) * P:(q // 4 + 1) * P]
                    for c in range(2):
                        i = pe.matmul(o, c_pair[:, c, q, :, :].rearrange("p e c -> p (e c)"), b_mat[:, c, q, :],
                                      start=(c == 0), stop=(c == 1), skip_group_check=True)
                i.then_inc(mixed, 1)

                def turned_b(n):
                    b = mix(f"ssm{qd}.bt{n}", b_T_copied, 4 * qd + n + 1)
                    for k in range(4):
                        c, q = divmod(4 * n + k, PQ)
                        i = pe.transpose(b[:, k * P:(k + 1) * P], b_mat[:, c, q, :], ident)
                    i.then_inc(mixed, 1)

                turned_b(0)
                pe.wait_ge(taps_out, qd + 1)
                b = mix(f"ssm{qd}.taps_T", taps_copied, qd + 1)
                for n in range(2):
                    i = pe.transpose(b[:, n * P:(n + 1) * P], taps_sb[:, n * P:(n + 1) * P], ident)
                i.then_inc(mixed, 1)
                for n in range(1, 4):
                    turned_b(n)
                    between(n - 1)

            def state_terms(qd):
                pe.wait_ge(u_ordered, qd + 1)
                b = mix(f"ssm{qd}.u", u_groups_copied, qd + 1)
                for g in range(GB):
                    i = pe.transpose(b[:, g * P:(g + 1) * P], u_by_group[:, g, :, :].rearrange("p m c -> p (m c)"), ident)
                i.then_inc(mixed, 1)
                pe.wait_ge(b_T_copied, 4 * (qd + 1))
                pe.wait_ge(u_groups_copied, qd + 1)
                b = mix(f"ssm{qd}.b", state_terms_read, qd + 1)
                for j in range(JB):
                    for g in range(GB):
                        q, e = 2 * j + g // 2, g % 2
                        for c in range(2):
                            i = pe.matmul(b[64 * e:64 * e + 64, (c * PQ + q) * NSUB:(c * PQ + q + 1) * NSUB],
                                          b_mat_T[:, c, q, 64 * e:64 * e + 64], u_group_F[:, qd % 2, g, j * NSUB:(j + 1) * NSUB],
                                          start=True, stop=True, skip_group_check=True)
                i.then_inc(mixed, 1)

            def own_steps(qd, j):
                if j == 0:
                    pe.wait_ge(toeplitz_in, 16 * SUB * (qd + 1))
                    if qd > 0:
                        pe.wait_ge(y_copied, 2 * qd)
                for g in range(GB):
                    col = (GB * j + g) * GROUP
                    o = turned_bank[g % 2][32 * j:32 * j + 32, (g // 2) * P:(g // 2 + 1) * P]
                    pe.matmul(o, u_group_F[:, qd % 2, g, j * NSUB:(j + 1) * NSUB], toep[:, qd % 2, :, col:col + GROUP],
                              start=(g < 2), stop=False, skip_group_check=True)

            def states_part(qd):
                pe.wait_ge(states_made, qd + 1)
                pe.wait_ge(c_mats_made, qd + 1)
                for q in range(PQ):
                    for c in range(2):
                        for e in range(2):
                            o = turned_bank[e][32 * (q // 2):32 * (q // 2) + 32, (q % 2) * P:(q % 2 + 1) * P]
                            rowsel = slice(64 * e, 64 * e + 64)
                            i = pe.matmul(o, st[rowsel, qd % 2, c, q, :], c_mat[rowsel, qd % 2, c, q, :], start=False,
                                          stop=(c == 1), skip_group_check=True)
                            if q == PQ - 1 and c == 1:
                                i.then_inc(y_ready, 1)

            taps_and_turned_b(0, lambda n: None)
            state_terms(0)
            for qd in range(PARTS):
                done = 0
                if qd + 1 < PARTS:
                    done = 3 if qd > 0 else 0
                    taps_and_turned_b(qd + 1, lambda n: own_steps(qd, n) if qd > 0 else None)
                    state_terms(qd + 1)
                for j in range(done, JB):
                    own_steps(qd, j)
                states_part(qd)
            pe.wait_ge(y_copied, 2 * PARTS)
            turn("y", DT, tiles_of(yT), lambda t, k: (gelu_made, k // 2 + 1), True, DT - 2)
            run(4)
            turn("yg", DT, tiles_of(yT), lambda t, k: (glu_rows, 2 * (k // 4) + t + 1), True)
            run(4)
            turn("h1", DT, tiles_of(hT), lambda t, k: (rows_normed, 2 + t + 1), True)
            run(15)

            def heads(tag, n_heads, dk, dv, src_q, src_k, src_v, qk, probs, probs_t, base, masked, v_ready, spare, per_gap):
                def fill_gap():
                    nonlocal spare
                    n = min(per_gap, spare)
                    run(n)
                    spare -= n

                for i in range(n_heads + 1):
                    h, done = i - 1, base + i
                    if i < n_heads:
                        b = mix(f"{tag}.qk{i}", qk_copied, done + 1)
                        for n, src in enumerate((src_q, src_k)):
                            for t in range(TT):
                                x = pe.transpose(b[0:dk, (2 * n + t) * P:(2 * n + t + 1) * P], src(t, i), ident)
                        x.then_inc(mixed, 1)
                    fill_gap()
                    if i > 0:
                        pe.wait_ge(probs_made, 2 * done)
                        b = mix(f"{tag}.pt{h}", probs_T_copied, done)
                        for qt in range(TT):
                            for kt in range(TT):
                                x = pe.transpose(b[:, (2 * qt + kt) * P:(2 * qt + kt + 1) * P],
                                                 probs[:, h % 2, qt, kt * P:(kt + 1) * P], ident)
                        x.then_inc(mixed, 1)
                    if i < n_heads:
                        pe.wait_ge(qk_copied, done + 1)
                        b = mix(f"{tag}.s{i}", *((scores_masked, done + 1) if masked else (probs_made, 2 * done + 2)))
                        for qt in range(TT):
                            x = pe.matmul(b[:, qt * SEQ:(qt + 1) * SEQ], qk[0:dk, i % 2, qt * P:(qt + 1) * P],
                                          qk[0:dk, i % 2, SEQ:2 * SEQ], start=True, stop=True)
                        x.then_inc(mixed, 1)
                    fill_gap()
                    if i > 0:
                        pe.wait_ge(probs_T_copied, done)
                        pe.wait_ge(v_copied if masked else mla_v_copied, v_ready(h))
                        b = mix(f"{tag}.o{h}", outs_scaled, 2 * done)
                        for qt in range(TT):
                            for kt in range(TT):
                                x = pe.matmul(b[:, qt * dv:(qt + 1) * dv], probs_t[:, h % 2, qt, kt, :],
                                              src_v(kt, h), start=(kt == 0), stop=(kt == TT - 1))
                        x.then_inc(mixed, 1)

            pe.wait_ge(attn_qk_roped, 8)
            heads("attn", HEADS, HD, HD, lambda t, h: qT[:, t, h * HD:(h + 1) * HD],
                  lambda t, h: kT[:, t, h * HD:(h + 1) * HD], lambda t, h: vT[:, t, h * HD:(h + 1) * HD],
                  a_qk, a_p, a_pt, 0, True, lambda h: 2 * (h // 4) + 2, 13, 1)
            turn("attn_o", DT, tiles_of(hT), lambda t, k: (attn_rows, t + 1) if k < HEADS - 2 else (outs_scaled, 2 * HEADS - 1 + t), True)
            run(4)
            for l in range(DEPTH2):
                turn(f"L{l}.h", DT, tiles_of(hT), lambda t, k: (rows_normed, 4 + 4 * l + t + 1), True)
                run(8)
                turn(f"L{l}.lat", 3, tiles_of(cnT), lambda t, k: (lat_rows, 2 * l + t + 1))
                split_made()
                run(12)
                pe.wait_ge(conv_glu_rows, TT * (l + 1))
                for n in range(2):
                    b = mix(f"L{l}.cin{n}", conv_in, 2 * l + n + 1)
                    for kk in range(2):
                        for t in range(TT):
                            k = 2 * n + kk
                            x = pe.transpose(b[:, kk * SEQ + t * P:kk * SEQ + (t + 1) * P], conv_a[:, t, k * P:(k + 1) * P], ident)
                    x.then_inc(mixed, 1)
                pe.wait_ge(mla_roped, 2 * TT * (l + 1))
                pe.wait_ge(mla_v_copied, 4 * (l + 1))
                heads(f"L{l}.mla", MLA_H, MQK, MV, lambda t, h: mq[:, t, h, :], lambda t, h: mk[:, t, h, :],
                      lambda t, h: mv[:, t, h, :], m_qk, m_p, m_pt, HEADS + MLA_H * l, False,
                      lambda h: 4 * (l + 1), 36, 2)
                pe.wait_ge(ret_roped, 2 * TT * (l + 1))
                for h in range(RH):
                    b = mix(f"L{l}.rqk{h}", ret_qk_copied, RH * l + h + 1)
                    for n, src in enumerate((rqT, rkT)):
                        for t in range(TT):
                            x = pe.transpose(b[:, (2 * n + t) * P:(2 * n + t + 1) * P], src[:, t, h * RDK:(h + 1) * RDK], ident)
                    x.then_inc(mixed, 1)
                run(4)
                pe.wait_ge(ret_v_copied, 4 * (l + 1))
                for h in range(RH + 1):
                    if h < RH:
                        pe.wait_ge(ret_qk_copied, RH * l + h + 1)
                        b = mix(f"L{l}.rs{h}", ret_scores, RH * l + h + 1)
                        for m in range(TT):
                            x = pe.matmul(b[:, m * SEQ:(m + 1) * SEQ], r_qk[:, h, SEQ + m * P:SEQ + (m + 1) * P],
                                          r_qk[:, h, 0:SEQ], start=True, stop=True)
                        x.then_inc(mixed, 1)
                    if h > 0:
                        pe.wait_ge(ret_scores, RH * l + h)
                        b = mix(f"L{l}.ro{h - 1}", ret_o_copied, RH * l + h)
                        for n in range(TT):
                            for m in range(TT):
                                x = pe.matmul(b[:, n * RDV:(n + 1) * RDV], r_s[:, (h - 1) % 2, m, n * P:(n + 1) * P],
                                              rv[:, m, (h - 1) * RDV:h * RDV], start=(m == 0), stop=(m == TT - 1))
                        x.then_inc(mixed, 1)
                turn(f"L{l}.mo", 4, lambda t, k: mla_o[:, t, 2 * k:2 * k + 2, :].rearrange("p h d -> p (h d)"),
                     lambda t, k: (outs_scaled, 2 * (HEADS + MLA_H * (l + 1))))
                pe.wait_ge(conv_summed, l + 1)
                for t in range(TT):
                    b = mix(f"L{l}.cback{t}", conv_normed, 2 * l + t + 1)
                    for k in range(4):
                        x = pe.transpose(b[:, k * P:(k + 1) * P], conv_sum[:, k, t * P:(t + 1) * P], ident)
                    x.then_inc(mixed, 1)
                split_made()
                run(2)
                pe.wait_ge(conv_normed, TT * (l + 1))
                for n in range(2):
                    b = mix(f"L{l}.cn{n}", conv_affine, 4 * l + 2 * n + 2)
                    for kk in range(2):
                        for t in range(TT):
                            k = 2 * n + kk
                            x = pe.transpose(b[:, kk * SEQ + t * P:kk * SEQ + (t + 1) * P], conv_t[:, t, k * P:(k + 1) * P], ident)
                    x.then_inc(mixed, 1)
                run(2)
                turn(f"L{l}.ro", DT, tiles_of(hT), lambda t, k: (ret_rows, 2 * l + t + 1), True)
                run(4)
                pe.wait_ge(conv_split, l + 1)
                run(4)
                turn(f"L{l}.merged", DT, lambda t, k: gates[:, 0, t, k * P:(k + 1) * P], lambda t, k: (merged, 4 * l + 2 * (k // 4) + t + 1), True)
                run(4)
                turn(f"L{l}.h2", DT, tiles_of(hT), lambda t, k: (rows_normed, 6 + 4 * l + t + 1), True)
                for c in range(HT // 2 + 1):
                    if 0 < c < HT // 2:
                        run(4)
                    if c > 0:
                        turn(f"L{l}.hid{c - 1}", 2, lambda t, k: ffn_h[:, (c - 1) % 2, t, k * P:(k + 1) * P],
                             lambda t, k: (ffn_rows, HT * l + 2 * c - 1 + t))
                run(10)
                split_made()
                run(12)
            assert pos == NS, (pos, NS)

        @block.sync
        def _(sp):
            def load_u(qd):
                sp.wait_ge(u_stored[qd // 2], 16 * TT)
                if qd > 1:
                    sp.wait_ge(u_ordered, qd - 1)
                for j in range(JB):
                    col = qd * PCOLS + j * GB * GROUP
                    sp.dma_start(u_sub[32 * j:32 * j + 32, qd % 2, :, :],
                                   u_scr[:, col:col + GB * GROUP].rearrange("(k m) d -> k m d", m=SUB)).then_inc(u_sub_in[qd % 2], 16)

            def toeplitz(qd):
                sp.wait_ge(taps_copied, qd + 1)
                sp.wait_ge(toeplitz_zero, 1)
                if qd > 1:
                    sp.wait_ge(y_ready, 2 * qd - 2)
                taps = taps_T[:, :, :, :].rearrange("p q e c -> p (q e c)")
                for s in range(SUB):
                    sp.dma_start(toep[0:GROUP * (s + 1), qd % 2, s, :], taps[GROUP * (SUB - 1 - s):P, :]).then_inc(toeplitz_in, 16)

            def y_to_rows(qd):
                sp.wait_ge(y_copied, 2 * qd + 2)
                for j in range(JB):
                    col = qd * PCOLS + j * GB * GROUP
                    sp.dma_start(y_scr[:, col:col + GB * GROUP].rearrange("(k l) d -> k l d", l=SUB),
                                 y_sub[32 * j:32 * j + 32, :, :]).then_inc(y_stored, 16)
                sp.wait_ge(y_stored, 16 * JB * (qd + 1))
                cols = slice(qd * PCOLS, (qd + 1) * PCOLS)
                for t in range(TT):
                    sp.dma_start(yT[:, t, cols], y_scr[t * P:(t + 1) * P, cols]).then_inc(y_in, 16)

            sp.dma_start(xT[:, :, :], x_in).then_inc(x_ld, 16)
            sp.dma_start(const[:, C_ID:C_ID + P], consts[:, C_ID:C_ID + P]).then_inc(consts_in, 16)
            for s, d in enumerate(slots):
                n = d["nk"] * d["width"]
                if s >= R:
                    sp.wait_ge(lo_made, s - R + 1)
                src = stream[d["off"]:d["off"] + P * n].rearrange("(p n) -> p n", p=P)
                sp.dma_start(raw[:, s % R, 0:n], src).then_inc(raw_in[s % R], 16)
                if s == 0:
                    sp.dma_start(ab[:, :, :], ssm_ab).then_inc(ssm_in, 16)
                    for e in range(2):
                        sp.dma_start(pdt[64 * e:64 * e + 64, :], ssm_ldt[e, :].partition_broadcast(STATE)).then_inc(ssm_in, 16)
                    sp.dma_start(posi[:, :], positions).then_inc(ssm_in, 16)
                if s == 2:
                    sp.dma_start(const[:, C_MASK:], consts[:, C_MASK:]).then_inc(tables_in, 16)
                if s == 9:
                    for qd in range(2):
                        load_u(qd)
                if s == 18:
                    toeplitz(0)
                    for qd in range(PARTS):
                        if qd + 1 < PARTS:
                            toeplitz(qd + 1)
                        if qd + 2 < PARTS:
                            load_u(qd + 2)
                        y_to_rows(qd)
            for t in range(TT):
                sp.wait_ge(x_normed, 4 * DEPTH2 - 1 + t)
                sp.dma_start(out[:, t, :], xT[:, t, :]).then_inc(out_stored, 16)
            sp.wait_ge(out_stored, 16 * TT)

        @block.scalar
        def _(act):
            pos = 0

            def make_hi(s):
                n = slots[s]["nk"] * slots[s]["width"]
                act.wait_ge(raw_in[s % R], 16 * (s // R + 1))
                if s >= R:
                    act.wait_ge(slot_used, s - R + 1)
                act.activation(w_hi[:, s % R, 0:n], raw[:, s % R, 0:n], ACT.Copy).then_inc(hi_made, 1)

            splits = splitter(make_hi)

            def take(name):
                n, p = mix_at[name]
                splits(p + R - 1)
                act.wait_ge(mixed, n + 1)
                return mixed_bank[n % 2]

            def run(n):
                nonlocal pos
                for name, end in chunks_ending(pos, pos + n):
                    splits(end + R - 1)
                    evac(name)
                pos += n

            def turn_hi(name, dst, ktiles, scale=1.0, k0=0, begin=0, ahead=R - 1):
                for k in range(begin, ktiles, 2):
                    n, p = turn_at[f"{name}.{k // 2}"]
                    splits(p + ahead)
                    act.wait_ge(turned, n + 1)
                    nk = min(2, ktiles - k)
                    act.activation(dst[:, k0 + k:k0 + k + nk, :], turned_bank[n % 2][:, 0:nk * SEQ].rearrange("p (k t) -> p k t", t=SEQ),
                                   ACT.Copy, scale=scale).then_inc(turned_hi, 1)

            last_squares = None

            def squares(src, total, done, value, scale=1.0):
                nonlocal last_squares
                if last_squares:
                    act.wait_ge(last_squares[0], last_squares[1])
                act.activation(junk[:, 0:src.shape[1]], src, ACT.Square, scale=scale, accum_out=total).then_inc(done, 1)
                last_squares = (done, value)

            def square_sums(name, ready, value, each=1):
                a = stats_of(name, 4)
                for t in range(TT):
                    act.wait_ge(ready, value + t * each)
                    squares(xT[:, t, :], a[:, t:t + 1], norm_sums, 2 * NORMS.index(name) + t + 1)

            def evac(name):
                l, kind, i = split_name(name)
                cols = slice(i * 512, (i + 1) * 512)
                odd = slice((i % 2) * 512, (i % 2 + 1) * 512)
                who = [reader_of(name, t) for t in range(TT)]
                if kind in ("ssm_out.", "attn_out.", "mla_o.", "conv_o.", "ret_o.") or (kind == "ret." and i < 2):
                    return
                if kind == "glu." and name[0] != "L":
                    for t in range(TT):
                        act.wait_ge(glu_biased, 2 * i + t + 1)
                        part = junk[:, 512 * t:512 * (t + 1)]
                        act.activation(part, part, ACT.Tanh, scale=0.5).then_inc(glu_tanh, 1)
                    return
                for t, b in enumerate(banks_of(act, name)):
                    read, value = who[t][0], who[t][1]
                    if kind == "ssm_in." and i < 2:
                        act.activation(uT[:, t, cols], b, ACT.Copy).then_inc(read, 1)
                        act.wait_ge(read, value)
                        act.dma_start(u_scr[t * P:(t + 1) * P, cols], uT[:, t, cols]).then_inc(u_stored[i], 16)
                    elif kind == "ssm_in.":
                        act.activation(zT[:, t, odd], b, ACT.Tanh, scale=0.5).then_inc(z_tanh, 1)
                    elif kind == "attn_in." and i < 4:
                        if 2 * i + t >= 2:
                            act.wait_ge(squares_summed, 2 * i + t - 1)
                        act.activation((qT, kT)[i // 2][:, t, odd], b, ACT.Copy)
                        act.activation(sq[:, t, :], b, ACT.Square).then_inc(read, 1)
                    elif kind == "attn_in." and i < 6:
                        act.activation(vT[:, t, odd], b, ACT.Copy).then_inc(read, 1)
                    elif kind == "attn_in.":
                        act.activation(szT[:, t, odd], b, ACT.Tanh, scale=0.5).then_inc(attn_z_tanh, 1)
                    elif kind == "lat.":
                        a = stats_of(f"L{l}.lat", 8)
                        act.activation(cT[:, t, :], b, ACT.Copy).then_inc(read, 1)
                        act.wait_ge(read, value)
                        squares(cT[:, t, 0:QR], a[:, t:t + 1], lat_sums, 4 * l + 2 * t + 1)
                        squares(cT[:, t, QR:QR + KVR], a[:, 2 + t:3 + t], lat_sums, 4 * l + 2 * t + 2)
                    elif kind == "glu." and i == 0:
                        act.activation(conv_a[:, t, :], b, ACT.Copy).then_inc(read, 1)
                    elif kind == "glu.":
                        act.activation(conv_t[:, t, :], b, ACT.Tanh, scale=0.5).then_inc(read, 1)
                    elif kind == "uq.":
                        act.activation(mq[:, t, 4 * i:4 * i + 4, :], b.rearrange("p (h d) -> p h d", h=4), ACT.Copy).then_inc(read, 1)
                    elif kind == "ukv.":
                        v = b.rearrange("p (h d) -> p h d", h=4)
                        act.activation(mk[:, t, 4 * i:4 * i + 4, 0:NOPE], v[:, :, 0:NOPE], ACT.Copy)
                        act.activation(mv[:, t, 4 * i:4 * i + 4, :], v[:, :, NOPE:NOPE + MV], ACT.Copy).then_inc(read, 1)
                    elif kind == "ret." and i < 4:
                        act.activation(rv[:, t, odd], b, ACT.Copy).then_inc(read, 1)
                    elif kind == "ret.":
                        act.activation(ret_g[:, t, odd], b, ACT.Tanh, scale=0.5).then_inc(ret_g_tanh, 1)
                    elif kind == "gate.":
                        act.activation(gates[:, i // 2, t, odd], b, ACT.Tanh, scale=0.5).then_inc(read, 1)
                    elif kind in ("out.", "down."):
                        a = stats_of(f"L{l}.{kind}post", 8)
                        squares(b, a[:, 2 * t + i:2 * t + i + 1], post_sums,
                                8 * l + (kind == "down.") * 4 + 2 * i + t + 1, D ** -0.5)
                    elif kind == "ffn.":
                        n = HT * l + 2 * i + t
                        if n >= 4:
                            act.wait_ge(ffn_rows, n - 3)
                        act.activation(ffn_t[:, i % 2, t, :], b[:, 0:FCH], ACT.Tanh, scale=0.5).then_inc(ffn_tanh, 1)

            square_sums("hn", x_ld, 16, 0)
            turn_hi("hn", f0_hi, DT, ahead=1)
            splits(R)
            act.wait_ge(ssm_in, 64)
            act.activation(pdt[:, :], pdt[:, :], ACT.Exp).then_inc(dt_exp, 1)
            act.wait_ge(ssm_rates, 1)
            act.activation(par[:, 2, :], par[:, 0, :], ACT.Exp).then_inc(ssm_mag, 1)
            act.wait_ge(angles, 1)
            flat = scan_w[:, :, :, :].rearrange("p a q k -> p (a q k)")
            act.activation(flat[:, 2 * N_ANG:4 * N_ANG], flat[:, 2 * N_ANG:4 * N_ANG], ACT.Sin).then_inc(sines, 1)
            run(16)

            def pair_c(qd):
                if qd > 0:
                    act.wait_ge(mixed, mix_at[f"ssm{qd - 1}.taps"][0] + 1)
                for e in range(2):
                    rowsel = slice(64 * e, 64 * e + 64)
                    for c in range(2):
                        x = act.activation(c_pair[rowsel, c, :, e, :], bc[rowsel, 2 + c, :, PQ * qd:PQ * (qd + 1)].rearrange("p c q -> p q c"), ACT.Copy)
                    x.then_inc(c_paired, 1)

            def taps_and_turned_b(qd):
                b = take(f"ssm{qd}.taps")
                act.activation(taps_sb[:, :], b[:, 0:2 * P], ACT.Copy).then_inc(taps_out, 1)

                def turned_b(n):
                    b = take(f"ssm{qd}.bt{n}")
                    act.activation(b_mat_T[:, n // 2, 4 * (n % 2):4 * (n % 2) + 4, :], b[:, :].rearrange("p (q c) -> p q c", c=P),
                                   ACT.Copy).then_inc(b_T_copied, 1)

                turned_b(0)
                b = take(f"ssm{qd}.taps_T")
                if qd > 0:
                    act.wait_ge(toeplitz_in, 16 * SUB * qd)
                act.activation(taps_T[:, :, :, :].rearrange("p q e c -> p (q e c)"), b[:, 0:2 * P], ACT.Copy).then_inc(taps_copied, 1)
                for n in range(1, 4):
                    turned_b(n)
                if qd + 1 < PARTS:
                    pair_c(qd + 1)

            def y_out(qd):
                for e in range(2):
                    act.wait_ge(y_ready, 2 * qd + e + 1)
                    b = turned_bank[e]
                    if qd > 0:
                        act.wait_ge(y_stored, 16 * JB * qd)
                    for g in range(GB // 2):
                        col = (2 * g + e) * GROUP
                        x = act.activation(y_sub[:, :, col:col + GROUP], b[:, g * P:(g + 1) * P].rearrange("p (l c) -> p l c", c=GROUP), ACT.Copy)
                    x.then_inc(y_copied, 1)

            def gelu_tanh(qd):
                act.wait_ge(gelu_in, qd + 1)
                act.activation(gelu_w[:, :, :], gelu_w[:, :, :], ACT.Tanh, scale=math.sqrt(2.0 / math.pi)).then_inc(gelu_tanh_made, 1)

            def u_groups(qd):
                act.wait_ge(u_sub_in[qd % 2], 16 * JB * (qd // 2 + 1))
                if qd > 0:
                    act.wait_ge(mixed, mix_at[f"ssm{qd - 1}.u"][0] + 1)
                act.activation(u_by_group[:, :, :, :], u_sub[:, qd % 2, :, :].rearrange("p m (g c) -> p g m c", c=GROUP), ACT.Copy).then_inc(u_ordered, 1)
                b = take(f"ssm{qd}.u")
                if qd > 1:
                    act.wait_ge(y_ready, 2 * qd - 2)
                act.activation(u_group_F[:, qd % 2, :, :], b[:, :].rearrange("p (g k) -> p g k", k=P), ACT.Copy).then_inc(u_groups_copied, 1)

            act.wait_ge(c_pairs_zero, 1)
            act.wait_ge(c_negated, 1)
            pair_c(0)
            taps_and_turned_b(0)
            u_groups(0)
            for qd in range(PARTS):
                if qd + 1 < PARTS:
                    taps_and_turned_b(qd + 1)
                    u_groups(qd + 1)
                if 0 < qd < PARTS - 1:
                    gelu_tanh(qd - 1)
                y_out(qd)
            gelu_tanh(PARTS - 2)
            turn_hi("y", f_hi, DT - 2, 0.5)
            gelu_tanh(PARTS - 1)
            turn_hi("y", f_hi, DT, 0.5, begin=DT - 2)
            run(8)
            turn_hi("yg", f_hi, DT, 0.125)
            run(8)
            square_sums("h1", x_updated, 3)
            turn_hi("h1", f_hi, DT)
            run(19)

            def heads(tag, n_heads, dk, qk, probs, probs_t, stt, base, masked, spare, per_gap):
                def gap():
                    nonlocal spare
                    n = min(per_gap, spare)
                    run(n)
                    spare -= n

                for i in range(n_heads + 1):
                    if i < n_heads:
                        b = take(f"{tag}.qk{i}")
                        act.activation(qk[0:dk, i % 2, :], b[0:dk, :], ACT.Copy).then_inc(qk_copied, 1)
                    gap()
                    if i > 0:
                        b = take(f"{tag}.pt{i - 1}")
                        act.activation(probs_t[:, (i - 1) % 2, :, :, :].rearrange("p a b c -> p (a b c)"), b[:, :],
                                       ACT.Copy).then_inc(probs_T_copied, 1)
                    if i < n_heads:
                        b = take(f"{tag}.s{i}")
                        act.wait_ge(max_found, base + i + 1)
                        for t in range(TT):
                            src, col, scale = ((a_s[:, i % 2, t, :], t, 1.0) if masked else
                                               (b[:, t * SEQ:(t + 1) * SEQ], 6 + t, MQK ** -0.5))
                            act.activation(probs[:, i % 2, t, :], src, ACT.Exp, bias=stt[:, i % 2, col:col + 1], scale=scale,
                                           accum_out=stt[:, i % 2, 2 + t:3 + t]).then_inc(probs_made, 1)
                    gap()

            heads("attn", HEADS, HD, a_qk, a_p, a_pt, a_st, 0, True, 13, 1)
            turn_hi("attn_o", f_hi, DT, 0.5)
            act.wait_ge(decay_abs, 1)
            act.activation(lgw[:, 1, :], lgw[:, 0, :], ACT.Exp, scale=-1.0).then_inc(decay_exp, 1)
            run(8)
            for l in range(DEPTH2):
                square_sums(f"L{l}.h", *((x_normed, 4 * l - 1) if l else (x_updated, 7)))
                turn_hi(f"L{l}.h", f_hi, DT)
                run(12)
                turn_hi(f"L{l}.lat", c_hi, 3)
                run(12)
                act.wait_ge(pads_zero, l + 1)
                for n in range(2):
                    b = take(f"L{l}.cin{n}")
                    act.activation(conv_F[:, 2 * n:2 * n + 2, PAD:PAD + SEQ], b[:, :].rearrange("p (k t) -> p k t", t=SEQ),
                                   ACT.Copy, scale=0.5).then_inc(conv_in, 1)
                heads(f"L{l}.mla", MLA_H, MQK, m_qk, m_p, m_pt, m_st, HEADS + MLA_H * l, False, 36, 2)
                for h in range(RH):
                    b = take(f"L{l}.rqk{h}")
                    act.activation(r_qk[:, h, :], b[:, :], ACT.Copy).then_inc(ret_qk_copied, 1)
                for h in range(RH):
                    act.wait_ge(decay_args, RH * l + h + 1)
                    act.activation(r_d[:, h, :, :], r_d[:, h, :, :], ACT.Exp).then_inc(decays_made, 1)
                run(4)
                for h in range(RH):
                    b = take(f"L{l}.ro{h}")
                    o = (rqT, rkT)[h // 2][:, :, (h % 2) * RDV:(h % 2 + 1) * RDV]
                    act.activation(o, b[:, :].rearrange("p (t e) -> p t e", t=TT), ACT.Copy).then_inc(ret_o_copied, 1)
                turn_hi(f"L{l}.mo", f_hi, 4)
                r = stats_of(f"L{l}.ret", 32)
                for t in range(TT):
                    act.wait_ge(ret_roots, TT * l + t + 1)
                    for h in range(RH):
                        n = RH * t + h
                        o = (rqT, rkT)[h // 2][:, t, (h % 2) * RDV:(h % 2 + 1) * RDV]
                        act.activation(o, o, ACT.Identity, scale=r[:, 16 + n:17 + n], bias=r[:, 24 + n:25 + n]).then_inc(ret_normed, 1)
                run(2)
                for n in range(2):
                    b = take(f"L{l}.cn{n}")
                    for kk in range(2):
                        k = 2 * n + kk
                        act.activation(conv_sum[:, k, :], b[:, kk * SEQ:(kk + 1) * SEQ], ACT.Identity,
                                       scale=cfp[:, k, TAPS + 1:TAPS + 2], bias=cfp[:, k, TAPS + 2:TAPS + 3]).then_inc(conv_affine, 1)
                act.wait_ge(conv_affine, 4 * l + 4)
                flat = conv_sum[:, :, :].rearrange("p k t -> p (k t)")
                act.activation(junk[:, :], flat, ACT.Tanh, scale=0.5).then_inc(conv_out_tanh, 1)
                run(2)
                turn_hi(f"L{l}.ro", f_hi, DT, 0.5)
                act.wait_ge(conv_silu, l + 1)
                act.activation(cf_hi[:, :, :].rearrange("p k t -> p (k t)"), flat, ACT.Copy, scale=0.5).then_inc(conv_hi, 1)
                run(12)
                turn_hi(f"L{l}.merged", f_hi, DT, 0.5)
                run(8)
                square_sums(f"L{l}.h2", x_normed, 4 * l + 1)
                turn_hi(f"L{l}.h2", f_hi, DT)
                for c in range(HT // 2 + 1):
                    if c < HT // 2:
                        run(4)
                    if c > 0:
                        turn_hi(f"L{l}.hid{c - 1}", h2_hi, 2, 0.5, 2 * (c - 1))
                run(22)

        @block.vector
        def _(dve):
            count = Count()
            pos = 0

            def make_lo(s):
                n = slots[s]["nk"] * slots[s]["width"]
                dve.wait_ge(hi_made, s + 1)
                if s >= R:
                    dve.wait_ge(slot_used, s - R + 1)
                dve.tensor_tensor(w_lo[:, s % R, 0:n], raw[:, s % R, 0:n], w_hi[:, s % R, 0:n].bitcast(F32),
                                  ALU.subtract).then_inc(lo_made, 1)

            splits = splitter(make_lo)

            def take(name):
                n, p = mix_at[name]
                splits(p + R - 1)
                dve.wait_ge(mixed, n + 1)
                return mixed_bank[n % 2]

            def run(n):
                nonlocal pos
                for name, end in chunks_ending(pos, pos + n):
                    splits(end + R - 1)
                    evac(name)
                pos += n

            def turn_lo(name, hi, lo, ktiles, scale=1.0, k0=0, begin=0, ahead=R - 1):
                for k in range(begin, ktiles, 2):
                    n, p = turn_at[f"{name}.{k // 2}"]
                    splits(p + ahead)
                    dve.wait_ge(turned_hi, n + 1)
                    nk = min(2, ktiles - k)
                    dve.scalar_tensor_tensor(out=lo[:, k0 + k:k0 + k + nk, :].rearrange("p k t -> p (k t)"),
                                             in0=turned_bank[n % 2][:, 0:nk * SEQ], scalar=scale,
                                             in1=hi[:, k0 + k:k0 + k + nk, :].rearrange("p k t -> p (k t)").bitcast(F32),
                                             op0=ALU.mult, op1=ALU.subtract).then_inc(turned_lo, 1)

            def stt(o, a, s, b, op0=ALU.mult, op1=ALU.mult):
                return dve.scalar_tensor_tensor(out=o, in0=a, scalar=s, in1=b, op0=op0, op1=op1)

            def tt(o, a, b, op):
                return dve.tensor_tensor(o, a, b, op)

            def ts(o, a, s1_, s2_, op0, op1=None):
                return dve.tensor_scalar(o, a, s1_, s2_, op0, op1) if op1 else dve.tensor_scalar(o, a, s1_, s2_, op0)

            def cmul(o_r, o_i, a_r, a_i, b_r, b_i, w):
                tt(w[0], a_r, b_r, ALU.mult).then_inc(dve_steps, count())
                tt(w[1], a_i, b_i, ALU.mult).then_inc(dve_steps, count())
                tt(w[2], a_r, b_i, ALU.mult).then_inc(dve_steps, count())
                tt(w[3], a_i, b_r, ALU.mult).then_inc(dve_steps, count())
                dve.wait_ge(dve_steps, count.n)
                tt(o_r, w[0], w[1], ALU.subtract).then_inc(dve_steps, count())
                tt(o_i, w[2], w[3], ALU.add).then_inc(dve_steps, count())
                dve.wait_ge(dve_steps, count.n)

            def apply_norm(no, gain):
                g = gain_row(dve, gain)
                a = stats_of(NORMS[no], 4)
                for t in range(TT):
                    dve.wait_ge(norm_roots, 2 * no + t + 1)
                    stt(hT[:, t, :], xT[:, t, :], a[:, 2 + t:3 + t], g).then_inc(rows_normed, 1)

            def evac(name):
                l, kind, i = split_name(name)
                cols = slice(i * 512, (i + 1) * 512)
                odd = slice((i % 2) * 512, (i % 2 + 1) * 512)
                who = [reader_of(name, t) for t in range(TT)]
                if kind == "attn_in." and i < 4:
                    qk_norm_rope(i)
                    return
                if kind == "lat.":
                    latent(l)
                    return
                if kind == "uq." and i == 1:
                    mla_rope(l)
                    return
                if (kind in ("uq.", "ukv.", "gate.") or (kind == "ssm_in." and i < 2)
                        or (kind == "attn_in." and i < 6) or (kind == "ret." and 2 <= i < 4)
                        or (kind == "glu." and name[0] == "L" and i == 0)):
                    return
                for t, b in enumerate(banks_of(dve, name)):
                    read = who[t][0]
                    if kind == "ssm_in.":
                        dve.wait_ge(z_tanh, 2 * (i - 2) + t + 1)
                        stt(zT[:, t, odd], zT[:, t, odd], 1.0, b, ALU.add).then_inc(read, 1)
                    elif kind == "glu." and name[0] != "L":
                        g = gain_row(dve, "b_glu")
                        if i > 0:
                            dve.wait_ge(glu_rows, t + 1)
                        tt(junk[:, 512 * t:512 * (t + 1)], b, g[:, cols], ALU.add).then_inc(read, 1)
                    elif kind in ("ssm_out.", "attn_out."):
                        tt(xT[:, t, cols], b, xT[:, t, cols], ALU.add).then_inc(read, 1)
                    elif kind == "attn_in.":
                        dve.wait_ge(attn_z_tanh, 2 * (i - 6) + t + 1)
                        stt(szT[:, t, odd], szT[:, t, odd], 1.0, b, ALU.add).then_inc(read, 1)
                    elif kind == "glu.":
                        dve.wait_ge(conv_tanh_made, 2 * l + t + 1)
                        stt(conv_a[:, t, :], conv_t[:, t, :], 1.0, conv_a[:, t, :], ALU.add).then_inc(conv_glu_rows, 1)
                    elif kind == "ret." and i < 2:
                        ret_rope(l, i, t, b, read)
                    elif kind == "ret.":
                        dve.wait_ge(ret_g_tanh, 4 * l + 2 * (i - 4) + t + 1)
                        stt(ret_g[:, t, odd], ret_g[:, t, odd], 1.0, b, ALU.add).then_inc(read, 1)
                    elif kind == "mla_o.":
                        stt(gates[:, 0, t, cols], gates[:, 0, t, cols], 1.0, b, ALU.add).then_inc(read, 1)
                    elif kind in ("conv_o.", "ret_o."):
                        n = 1 if kind == "conv_o." else 2
                        stt(gates[:, n, t, cols], gates[:, n, t, cols], 1.0, b, ALU.add).then_inc(read, 1)
                        dve.wait_ge(read, who[t][1])
                        x = tt(gates[:, 0, t, cols], gates[:, 0, t, cols], gates[:, n, t, cols], ALU.add)
                        if n == 1:
                            x.then_inc(merged, 1)
                        else:
                            x.then_inc(dve_steps, count())
                    elif kind in ("out.", "down."):
                        dve.wait_ge(post_sums, 8 * l + (kind == "down.") * 4 + 2 * i + t + 1)
                        g = gain_row(dve, f"L{l}.mix_post" if kind == "out." else f"L{l}.ffn_post")
                        tt(hT[:, t, cols], b, g[:, cols], ALU.mult).then_inc(read, 1)
                    elif kind == "ffn.":
                        n = HT * l + 2 * i + t
                        dve.wait_ge(ffn_tanh, n + 1)
                        stt(ffn_t[:, i % 2, t, :], ffn_t[:, i % 2, t, :], 1.0, b[:, 0:FCH], ALU.add).then_inc(dve_steps, count())
                        dve.wait_ge(dve_steps, count.n)
                        tt(ffn_h[:, i % 2, t, :], ffn_t[:, i % 2, t, :], b[:, FCH:2 * FCH], ALU.mult).then_inc(read, 1)
                if kind == "glu." and name[0] != "L":
                    for t in range(TT):
                        dve.wait_ge(glu_tanh, 2 * i + t + 1)
                        stt(yT[:, t, cols], junk[:, 512 * t:512 * (t + 1)], 1.0, yT[:, t, cols], ALU.add).then_inc(glu_rows, 1)

            dve.memset(minus_half[:, :], -0.5).then_inc(minus_half_set, 1)
            dve.memset(c_pair[:, :, :, :, :], 0.0).then_inc(c_pairs_zero, 1)
            dve.memset(pw[:, 0, 0, :], 1.0).then_inc(dve_steps, count())
            dve.memset(pw[:, 1, 0, :], 0.0).then_inc(dve_steps, count())
            dve.memset(st[:, :, :, :, 0:1], 0.0).then_inc(dve_steps, count())
            apply_norm(0, "norm0")
            turn_lo("hn", f0_hi, f0_lo, DT, ahead=1)
            splits(R)
            dve.wait_ge(tables_in, 16)
            dve.wait_ge(ssm_in, 64)
            flat = scan_w[:, :, :, :].rearrange("p a q k -> p (a q k)")
            ang = flat[:, 0:N_ANG]
            turns_w, cos_w, sin_w = (flat[:, k * N_ANG:(k + 1) * N_ANG] for k in (1, 2, 3))
            lr, li = ab[:, 0, :], ab[:, 1, :]
            dve.tensor_copy(posf[:, :], posi[:, :]).then_inc(dve_steps, count())
            dve.wait_ge(dt_exp, 1)
            tt(par[:, 0, :], lr, pdt[:, :], ALU.mult).then_inc(ssm_rates, 1)
            tt(ang[:, 0:Q], li, pdt[:, :], ALU.mult).then_inc(dve_steps, count())
            dve.wait_ge(dve_steps, count.n)
            for t in range(TT):
                a = Q + t * (RDK // 2)
                ts(ang[:, a:a + RDK // 2], const[:, C_INVR:C_INVM], posf[:, t:t + 1], None, ALU.mult).then_inc(dve_steps, count())
                a = Q + RDK + t * (ROPE // 2)
                ts(ang[:, a:a + ROPE // 2], const[:, C_INVM:N_CONST], posf[:, t:t + 1], None, ALU.mult).then_inc(dve_steps, count())
            dve.wait_ge(dve_steps, count.n)
            for w, quarter in ((sin_w, 0.0), (cos_w, 0.25)):
                ts(turns_w, ang, 1.0 / TWO_PI, quarter, ALU.mult, ALU.add).then_inc(dve_steps, count())
                dve.wait_ge(dve_steps, count.n)
                ts(turns_w, turns_w, ROUND, ROUND, ALU.add, ALU.subtract).then_inc(dve_steps, count())
                dve.wait_ge(dve_steps, count.n)
                stt(w, turns_w, -PI_A, ang, ALU.mult, ALU.add).then_inc(dve_steps, count())
                dve.wait_ge(dve_steps, count.n)
                stt(w, turns_w, -PI_B, w, ALU.mult, ALU.add).then_inc(dve_steps, count())
                dve.wait_ge(dve_steps, count.n)
                stt(w, turns_w, -PI_C, w, ALU.mult, ALU.add).then_inc(dve_steps, count())
                dve.wait_ge(dve_steps, count.n)
                if quarter:
                    ts(w, w, math.pi / 2, None, ALU.add).then_inc(dve_steps, count())
                    dve.wait_ge(dve_steps, count.n)
                last = ts(w, w, PI_IN, -PI_IN, ALU.min, ALU.max)
                if not quarter:
                    last.then_inc(dve_steps, count())
            last.then_inc(angles, 1)
            dve.wait_ge(sines, 1)
            dve.wait_ge(ssm_mag, 1)
            both = flat[:, 2 * N_ANG:4 * N_ANG].rearrange("p (a n) -> p a n", a=2)
            dve.tensor_copy(ret_rot[:, :, :, :].rearrange("p a t n -> p a (t n)"), both[:, :, Q:Q + RDK]).then_inc(dve_steps, count())
            dve.tensor_copy(mla_rot[:, :, :, :].rearrange("p a t n -> p a (t n)"), both[:, :, Q + RDK:N_ANG]).then_inc(dve_steps, count())
            dve.tensor_copy(par[:, 3:5, :], both[:, :, 0:Q]).then_inc(dve_steps, count())
            splits(R + 2)
            dve.wait_ge(dve_steps, count.n)
            c_, sn_, mag = par[:, 3, :], par[:, 4, :], par[:, 2, :]
            tt(pw[:, 0, 1, :], mag, c_, ALU.mult).then_inc(dve_steps, count())
            tt(pw[:, 1, 1, :], mag, sn_, ALU.mult).then_inc(dve_steps, count())
            w4 = [par[:, k, :] for k in (16, 17, 18, 19)]
            for k in range(3):
                src = (c_, sn_) if k == 0 else (par[:, 14, :], par[:, 15, :])
                cmul(par[:, 14, :], par[:, 15, :], *src, *src, w4)
                tt(par[:, 13, :], *((mag, mag) if k == 0 else (par[:, 13, :], par[:, 13, :])), ALU.mult).then_inc(dve_steps, count())
                dve.wait_ge(dve_steps, count.n)
            dve.tensor_copy(par[:, 12, :], par[:, 13, :]).then_inc(turn_base, 1)
            splits(R + 4)
            wide = gelu_w[:, :, :].rearrange("p t n -> p (t n)").rearrange("p (a t q) -> p a t q", a=4, q=Q)
            cmul(pw[:, 0, 2, :], pw[:, 1, 2, :], pw[:, 0, 1, :], pw[:, 1, 1, :], pw[:, 0, 1, :], pw[:, 1, 1, :], w4)
            for k, n in ((2, 2), (4, 4)):
                by = [pw[:, c, k:k + 1, :].broadcast_to([P, n, Q]) for c in range(2)]
                cmul(pw[:, 0, k + 1:k + 1 + n, :], pw[:, 1, k + 1:k + 1 + n, :], *by,
                     pw[:, 0, 1:1 + n, :], pw[:, 1, 1:1 + n, :], [wide[:, a, 0:n, :] for a in range(4)])
            for m in range(SUB):
                x = dve.tensor_copy(pwb[:, :, m, :], pw[:, :, SUB - 1 - m, :])
                if m < SUB - 1:
                    x.then_inc(dve_steps, count())
                else:
                    x.then_inc(powers_made, 1)
            splits(R + 6)
            den, rden, nr, t1, t2 = (par[:, k, :] for k in (5, 6, 7, 8, 9))
            f_r, f_i = par[:, 10, :], par[:, 11, :]
            tt(t1, lr, lr, ALU.mult).then_inc(dve_steps, count())
            tt(t2, li, li, ALU.mult).then_inc(dve_steps, count())
            ts(nr, pw[:, 0, 1, :], -1.0, None, ALU.add).then_inc(dve_steps, count())
            dve.wait_ge(dve_steps, count.n)
            tt(den, t1, t2, ALU.add).then_inc(dve_steps, count())
            dve.wait_ge(dve_steps, count.n)
            dve.reciprocal(rden, den).then_inc(dve_steps, count())
            ni = pw[:, 1, 1, :]
            for o, a, b, op in ((f_r, lr, li, ALU.add), (f_i, li, lr, ALU.subtract)):
                tt(t1, nr if op == ALU.add else ni, lr, ALU.mult).then_inc(dve_steps, count())
                tt(t2, ni if op == ALU.add else nr, li, ALU.mult).then_inc(dve_steps, count())
                dve.wait_ge(dve_steps, count.n)
                tt(t1, t1, t2, op).then_inc(dve_steps, count())
                dve.wait_ge(dve_steps, count.n)
                tt(o, t1, rden, ALU.mult).then_inc(dve_steps, count())
                dve.wait_ge(dve_steps, count.n)
            splits(R + 7)
            dve.wait_ge(ssm_mats_in, 16)
            fbb = [f.unsqueeze(1).broadcast_to([P, GROUP, Q]) for f in (f_r, f_i)]
            w = [x[:, n:n + 512].rearrange("p (c q) -> p c q", q=Q) for x in (junk, flat) for n in (0, 512)]
            tt(w[0], bc[:, 0, :, :], fbb[0], ALU.mult).then_inc(dve_steps, count())
            tt(w[1], bc[:, 1, :, :], fbb[1], ALU.mult).then_inc(dve_steps, count())
            tt(w[2], bc[:, 1, :, :], fbb[0], ALU.mult).then_inc(dve_steps, count())
            tt(w[3], bc[:, 0, :, :], fbb[1], ALU.mult).then_inc(dve_steps, count())
            dve.wait_ge(dve_steps, count.n)
            tt(bc[:, 0, :, :], w[0], w[1], ALU.subtract).then_inc(dve_steps, count())
            tt(bc[:, 1, :, :], w[2], w[3], ALU.add).then_inc(dve_steps, count())
            dve.wait_ge(dve_steps, count.n)
            ts(bc[:, 3, :, :], bc[:, 3, :, :], -1.0, None, ALU.mult).then_inc(c_negated, 1)
            dve.wait_ge(c_negated, 1)

            def b_mats(qd):
                if qd > 0:
                    dve.wait_ge(mixed, mix_at[f"ssm{qd - 1}.bt3"][0] + 1)
                q0 = PQ * qd
                tmp = junk[:, :].rearrange("p (q m c) -> p q m c", m=SUB, c=GROUP)
                pr, pi = (pwb[:, c, :, q0:q0 + PQ].rearrange("p m q -> p q m").unsqueeze(3).broadcast_to([P, PQ, SUB, GROUP]) for c in range(2))
                fr, fi = (bc[:, c, :, q0:q0 + PQ].rearrange("p c q -> p q c").unsqueeze(2).broadcast_to([P, PQ, SUB, GROUP]) for c in range(2))
                o = [b_mat[:, c, :, :].rearrange("p q (m c) -> p q m c", c=GROUP) for c in range(2)]
                for n, (x0, x1, op) in enumerate(((fr, fi, ALU.subtract), (fi, fr, ALU.add))):
                    tt(o[n], pr, x0, ALU.mult).then_inc(dve_steps, count())
                    if n == 1:
                        dve.wait_ge(dve_steps, count.n - 1)
                    elif qd > 0:
                        dve.wait_ge(b_mats_made, qd)
                    tt(tmp, pi, x1, ALU.mult).then_inc(dve_steps, count())
                    dve.wait_ge(dve_steps, count.n)
                    i = tt(o[n], o[n], tmp, op)
                    if n == 1:
                        i.then_inc(b_mats_made, 1)
                    else:
                        i.then_inc(dve_steps, count())

            def scan_states(qd):
                b = take(f"ssm{qd}.b")
                dve.wait_ge(turns_made, 1)
                q0 = PQ * qd
                ec, es = (turn[:, c, q0:q0 + PQ, :] for c in range(2))
                br, bi = (b[:, c * PQ * NSUB:(c + 1) * PQ * NSUB].rearrange("p (q k) -> p q k", k=NSUB) for c in range(2))
                s0, s1_, s2__, s3_ = (scan_w[:, c, :, :] for c in range(4))
                tt(s0, br, ec, ALU.mult).then_inc(dve_steps, count())
                tt(s1_, bi, es, ALU.mult).then_inc(dve_steps, count())
                tt(s2__, bi, ec, ALU.mult).then_inc(dve_steps, count())
                tt(s3_, br, es, ALU.mult).then_inc(state_terms_read, 1)
                dve.wait_ge(state_terms_read, qd + 1)
                tt(s0, s0, s1_, ALU.add).then_inc(dve_steps, count())
                tt(s2__, s2__, s3_, ALU.subtract).then_inc(dve_steps, count())
                dve.wait_ge(dve_steps, count.n)
                f2 = lambda x: x.rearrange("p q k -> p (q k)")
                for o, x in ((s1_, s0), (s3_, s2__)):
                    dve.tensor_tensor_scan(f2(o), f2(rho[:, q0:q0 + PQ, :]), f2(x), 0.0, ALU.mult, ALU.add).then_inc(dve_steps, count())
                dve.wait_ge(dve_steps, count.n)
                if qd > 1:
                    dve.wait_ge(gelu_made, qd - 1)
                g0, g1 = (gelu_w[:, t, :].rearrange("p (q k) -> p q k", k=NSUB) for t in range(2))
                tt(s0, s1_, ec, ALU.mult).then_inc(dve_steps, count())
                tt(s2__, s3_, es, ALU.mult).then_inc(dve_steps, count())
                tt(g0, s3_, ec, ALU.mult).then_inc(dve_steps, count())
                tt(g1, s1_, es, ALU.mult).then_inc(dve_steps, count())
                dve.wait_ge(dve_steps, count.n)
                if qd > 1:
                    dve.wait_ge(y_ready, 2 * qd - 2)
                n = NSUB - 1
                tt(st[:, qd % 2, 0, :, 1:], s0[:, :, 0:n], s2__[:, :, 0:n], ALU.subtract).then_inc(dve_steps, count())
                tt(st[:, qd % 2, 1, :, 1:], g0[:, :, 0:n], g1[:, :, 0:n], ALU.add).then_inc(states_made, 1)

            def gelu(qd):
                dve.wait_ge(y_in, 16 * TT * (qd + 1))
                g = gain_row(dve, "d_skip")
                cols = slice(qd * PCOLS, (qd + 1) * PCOLS)
                y, u, gg = yT[:, :, cols], uT[:, :, cols], gelu_w[:, :, :]
                dve.wait_ge(states_made, min(qd + 2, PARTS))
                if qd > 0:
                    dve.wait_ge(gelu_made, qd)
                tt(gg, u, g[:, cols].unsqueeze(1).broadcast_to([P, TT, PCOLS]), ALU.mult).then_inc(dve_steps, count())
                dve.wait_ge(dve_steps, count.n)
                tt(y, y, gg, ALU.add).then_inc(dve_steps, count())
                dve.wait_ge(dve_steps, count.n)
                tt(gg, y, y, ALU.mult).then_inc(dve_steps, count())
                dve.wait_ge(dve_steps, count.n)
                ts(gg, gg, 0.044715, 1.0, ALU.mult, ALU.add).then_inc(dve_steps, count())
                dve.wait_ge(dve_steps, count.n)
                tt(gg, gg, y, ALU.mult).then_inc(gelu_in, 1)
                dve.wait_ge(gelu_tanh_made, qd + 1)
                stt(y, gg, 1.0, y, ALU.add).then_inc(gelu_made, 1)

            splits(R + 9)
            b_mats(0)
            run(16)
            b_mats(1)
            for qd in range(PARTS):
                scan_states(qd)
                if qd + 2 < PARTS:
                    b_mats(qd + 2)
                if qd > 0:
                    gelu(qd - 1)
            turn_lo("y", f_hi, f_lo, DT - 2, 0.5)
            gelu(PARTS - 1)
            turn_lo("y", f_hi, f_lo, DT, 0.5, begin=DT - 2)
            for t in range(TT):
                tt(yT[:, t, :], yT[:, t, :], zT[:, t, :], ALU.mult).then_inc(dve_steps, count())
            dve.wait_ge(dve_steps, count.n)
            run(8)
            turn_lo("yg", f_hi, f_lo, DT, 0.125)
            run(8)

            def qk_norm_rope(i):
                a = stats_of(f"qk{i}", 16)
                dst = (qT, kT)[i // 2]
                part = slice((i % 2) * 512, (i % 2 + 1) * 512)
                for t in range(TT):
                    dve.wait_ge(squares_made, 2 * i + t + 1)
                    dve.tensor_reduce(a[:, 4 * t:4 * t + 4], sq[:, t, :].rearrange("p (h d) -> p h d", d=HD), AX, ALU.add).then_inc(squares_summed, 1)
                c = table[f"attn_in.{i}"]
                if i < 3:
                    splits(c["first"] + c["n"] + R)
                dve.wait_ge(qk_roots, i + 1)
                dve.wait_ge(qk_gain_in, 32)
                v = [dst[:, t, part].rearrange("p (h d) -> p h d", d=HD) for t in range(TT)]
                for t in range(TT):
                    for h in range(4):
                        n = 8 + 4 * t + h
                        stt(v[t][:, h, :], v[t][:, h, :], a[:, n:n + 1], qkg[:, i // 2, :]).then_inc(dve_steps, count())
                if i < 3:
                    splits(c["first"] + c["n"] + R + 1)
                dve.wait_ge(dve_steps, count.n)
                half = ROT // 2
                if i > 0:
                    dve.wait_ge(attn_qk_roped, 2 * i)
                w = [[ropt[:, t, k, :].rearrange("p (h d) -> p h d", h=4) for k in range(4)] for t in range(TT)]
                for t in range(TT):
                    cs = [const[:, c + t * half:c + (t + 1) * half].unsqueeze(1).broadcast_to([P, 4, half]) for c in (C_COS1, C_SIN1)]
                    x1, x2 = v[t][:, :, 0:half], v[t][:, :, half:ROT]
                    tt(w[t][0], x1, cs[0], ALU.mult).then_inc(dve_steps, count())
                    tt(w[t][1], x2, cs[1], ALU.mult).then_inc(dve_steps, count())
                    tt(w[t][2], x2, cs[0], ALU.mult).then_inc(dve_steps, count())
                    tt(w[t][3], x1, cs[1], ALU.mult).then_inc(dve_steps, count())
                dve.wait_ge(dve_steps, count.n)
                for t in range(TT):
                    tt(v[t][:, :, 0:half], w[t][0], w[t][1], ALU.subtract).then_inc(dve_steps, count())
                    tt(v[t][:, :, half:ROT], w[t][2], w[t][3], ALU.add).then_inc(attn_qk_roped, 1)

            def heads(tag, n_heads, dv, stt_, base, masked, scale_out, spare, per_gap, extra):
                def gap():
                    nonlocal spare
                    n = min(per_gap, spare)
                    run(n)
                    spare -= n

                for i in range(n_heads + 1):
                    gap()
                    if i < n_heads:
                        b = take(f"{tag}.s{i}")
                        sc = b[:, :].rearrange("p (t k) -> p t k", t=TT)
                        m = stt_[:, i % 2, :]
                        if masked:
                            src = a_s[:, i % 2, :, :]
                            mask = const[:, C_MASK:C_MASK + TT * SEQ].rearrange("p (t k) -> p t k", t=TT)
                            stt(src, sc, HD ** -0.5, mask, ALU.mult, ALU.add).then_inc(scores_masked, 1)
                            dve.wait_ge(scores_masked, base + i + 1)
                            dve.tensor_reduce(m[:, 0:2], src, AX, ALU.max, negate=True).then_inc(max_found, 1)
                        else:
                            dve.tensor_reduce(m[:, 0:2], sc, AX, ALU.max, negate=True).then_inc(dve_steps, count())
                            dve.wait_ge(dve_steps, count.n)
                            ts(m[:, 6:8], m[:, 0:2], MQK ** -0.5, None, ALU.mult).then_inc(max_found, 1)
                    if i < n_heads:
                        extra(i)
                    gap()
                    if i > 0:
                        h = i - 1
                        dve.wait_ge(probs_made, 2 * (base + h + 1))
                        m = stt_[:, h % 2, :]
                        dve.reciprocal(m[:, 4:6], m[:, 2:4]).then_inc(dve_steps, count())
                        b = take(f"{tag}.o{h}")
                        dve.wait_ge(dve_steps, count.n)
                        for t in range(TT):
                            scale_out(t, h, b[:, t * dv:(t + 1) * dv], m[:, 4 + t:5 + t]).then_inc(outs_scaled, 1)
                extra(n_heads)

            dve.wait_ge(x_updated, 4)
            apply_norm(1, "norm1")
            turn_lo("h1", f_hi, f_lo, DT)
            run(19)
            def scale_out(t, h, o, inv):
                e = slice(h * HD, (h + 1) * HD)
                if h < HEADS - 2:
                    return ts(hT[:, t, e], o, inv, None, ALU.mult)
                return stt(hT[:, t, e], o, inv, szT[:, t, e])

            def gate_rows(i):
                if i == HEADS - 1:
                    dve.wait_ge(outs_scaled, 2 * (HEADS - 2))
                    dve.wait_ge(attn_z_silu, 4)
                    e = slice(0, (HEADS - 2) * HD)
                    for t in range(TT):
                        tt(hT[:, t, e], hT[:, t, e], szT[:, t, e], ALU.mult).then_inc(attn_rows, 1)

            heads("attn", HEADS, HD, a_st, 0, True, scale_out, 13, 1, gate_rows)
            turn_lo("attn_o", f_hi, f_lo, DT, 0.5)
            dve.wait_ge(decay_in, 16)
            ts(lgw[:, 2, :], lgw[:, 5, :], -1.0, None, ALU.mult).then_inc(dve_steps, count())
            dve.wait_ge(dve_steps, count.n)
            tt(lgw[:, 0, :], lgw[:, 2, :], lgw[:, 5, :], ALU.max).then_inc(decay_abs, 1)
            dve.wait_ge(decay_exp, 1)
            e_, s_, s2_, p_ = (lgw[:, k, :] for k in (1, 2, 3, 4))
            ts(p_, e_, 2.0, None, ALU.add).then_inc(dve_steps, count())
            dve.wait_ge(dve_steps, count.n)
            dve.reciprocal(s2_, p_).then_inc(dve_steps, count())
            dve.wait_ge(dve_steps, count.n)
            tt(s_, e_, s2_, ALU.mult).then_inc(dve_steps, count())
            dve.wait_ge(dve_steps, count.n)
            tt(s2_, s_, s_, ALU.mult).then_inc(dve_steps, count())
            dve.wait_ge(dve_steps, count.n)
            ts(p_, s2_, 1.0 / 21, None, ALU.mult).then_inc(dve_steps, count())
            dve.wait_ge(dve_steps, count.n)
            for k in range(19, 1, -2):
                stt(p_, p_, 1.0 / k, s2_, ALU.add, ALU.mult).then_inc(dve_steps, count())
                dve.wait_ge(dve_steps, count.n)
            stt(p_, p_, 1.0, s_, ALU.add, ALU.mult).then_inc(dve_steps, count())
            ts(e_, lgw[:, 5, :], 0.0, None, ALU.min).then_inc(dve_steps, count())
            dve.wait_ge(dve_steps, count.n)
            stt(lg[:, :], p_, -2.0, e_, ALU.mult, ALU.add).then_inc(lg_made, 1)
            run(8)

            def latent(l):
                a = stats_of(f"L{l}.lat", 8)
                dve.wait_ge(lat_roots, l + 1)
                dve.wait_ge(layer_params_in, 48 * (l + 1))
                for t in range(TT):
                    stt(cnT[:, t, 0:QR], cT[:, t, 0:QR], a[:, 4 + t:5 + t], latp[:, 0:QR]).then_inc(dve_steps, count())
                    stt(cnT[:, t, QR:QR + KVR], cT[:, t, QR:QR + KVR], a[:, 6 + t:7 + t], latp[:, QR:QR + KVR]).then_inc(lat_rows, 1)

            def mla_rope(l):
                dve.wait_ge(mla_q_copied, 4 * (l + 1))
                half = ROPE // 2
                dve.wait_ge(conv_glu_rows, TT * (l + 1))
                for t in range(TT):
                    c, s = (mla_rot[:, k, t, :].unsqueeze(1).broadcast_to([P, MLA_H, half]) for k in range(2))
                    x1, x2 = mq[:, t, :, NOPE:NOPE + half], mq[:, t, :, NOPE + half:MQK]
                    w = [rope_w[:, k, :, :] for k in range(4)]
                    if l + t > 0:
                        dve.wait_ge(mla_roped, 4 * l + t)
                    tt(w[0], x1, c, ALU.mult).then_inc(dve_steps, count())
                    tt(w[1], x2, s, ALU.mult).then_inc(dve_steps, count())
                    tt(w[2], x2, c, ALU.mult).then_inc(dve_steps, count())
                    tt(w[3], x1, s, ALU.mult).then_inc(dve_steps, count())
                    dve.wait_ge(dve_steps, count.n)
                    tt(x1, w[0], w[1], ALU.subtract).then_inc(dve_steps, count())
                    tt(x2, w[2], w[3], ALU.add).then_inc(mla_roped, 1)
                for t in range(TT):
                    c, s = (mla_rot[:, k, t, :] for k in range(2))
                    k1, k2 = cT[:, t, QR + KVR:QR + KVR + half], cT[:, t, QR + KVR + half:QR + KVR + ROPE]
                    w = [rope_w[:, k, 0, :] for k in range(4)]
                    dve.wait_ge(mla_roped, 4 * l + 2 + t)
                    tt(w[0], k1, c, ALU.mult).then_inc(dve_steps, count())
                    tt(w[1], k2, s, ALU.mult).then_inc(dve_steps, count())
                    tt(w[2], k2, c, ALU.mult).then_inc(dve_steps, count())
                    tt(w[3], k1, s, ALU.mult).then_inc(dve_steps, count())
                    dve.wait_ge(dve_steps, count.n)
                    every = [x.unsqueeze(1).broadcast_to([P, MLA_H, half]) for x in w]
                    tt(mk[:, t, :, NOPE:NOPE + half], every[0], every[1], ALU.subtract).then_inc(dve_steps, count())
                    tt(mk[:, t, :, NOPE + half:MQK], every[2], every[3], ALU.add).then_inc(mla_roped, 1)

            def ret_rope(l, i, t, b, read):
                half = RDK // 2
                w = [conv_t[:, k // 2, (k % 2) * 256:(k % 2 + 1) * 256].rearrange("p (h d) -> p h d", h=RH) for k in range(4)]
                dve.wait_ge(mla_roped, 4 * (l + 1))
                v = b.rearrange("p (h d) -> p h d", h=RH)
                o = (rqT, rkT)[i][:, t, :].rearrange("p (h d) -> p h d", h=RH)
                c, s = (ret_rot[:, k, t, :].unsqueeze(1).broadcast_to([P, RH, half]) for k in range(2))
                if l + i + t > 0:
                    dve.wait_ge(ret_roped, 4 * l + 2 * i + t)
                tt(w[0], v[:, :, 0:half], c, ALU.mult).then_inc(dve_steps, count())
                tt(w[1], v[:, :, half:RDK], s, ALU.mult).then_inc(dve_steps, count())
                tt(w[2], v[:, :, half:RDK], c, ALU.mult).then_inc(dve_steps, count())
                tt(w[3], v[:, :, 0:half], s, ALU.mult).then_inc(read, 1)
                dve.wait_ge(read, 4 * l + 2 * i + t + 1)
                tt(o[:, :, 0:half], w[0], w[1], ALU.subtract).then_inc(dve_steps, count())
                tt(o[:, :, half:RDK], w[2], w[3], ALU.add).then_inc(ret_roped, 1)

            def residual(no, l, kind):
                a = stats_of(f"L{l}.{kind}post", 8)
                done = (mix_scaled if kind == "out." else ffn_scaled)
                dve.wait_ge(done, 4 * (l + 1))
                for t in range(TT):
                    dve.wait_ge(post_roots, 2 * no + t + 1)
                    stt(xT[:, t, :], hT[:, t, :], a[:, 6 + t:7 + t], xT[:, t, :], ALU.mult, ALU.add).then_inc(x_normed, 1)

            for l in range(DEPTH2):
                dve.wait_ge(x_updated, 8)
                if l > 0:
                    dve.wait_ge(x_normed, 4 * l)
                apply_norm(2 + 2 * l, f"L{l}.mix_pre")
                dve.memset(conv_F[:, :, 0:PAD], 0.0)
                dve.memset(conv_F[:, :, PAD + SEQ:], 0.0).then_inc(pads_zero, 1)
                turn_lo(f"L{l}.h", f_hi, f_lo, DT)
                run(12)
                turn_lo(f"L{l}.lat", c_hi, c_lo, 3)
                run(12)

                def taps(a, b):
                    dve.wait_ge(conv_in, 2 * (l + 1))
                    for n in range(a, b):
                        for k in range(4):
                            x = conv_F[:, k, n:n + SEQ]
                            if n == 0:
                                ts(conv_sum[:, k, :], x, cfp[:, k, 0:1], cfp[:, k, TAPS:TAPS + 1], ALU.mult, ALU.add).then_inc(dve_steps, count())
                            else:
                                dve.wait_ge(dve_steps, count.n - 3)
                                stt(conv_sum[:, k, :], x, cfp[:, k, n:n + 1], conv_sum[:, k, :], ALU.mult, ALU.add).then_inc(dve_steps, count())

                def extra(i):
                    own = TAPS - SIDE_TAPS
                    a, b = own * i // (MLA_H + 1), own * (i + 1) // (MLA_H + 1)
                    mid = (a + b) // 2
                    taps(a, mid)
                    splits(pos + R)
                    taps(mid, b)
                    if i == MLA_H:
                        dve.wait_ge(conv_side, l + 1)
                        dve.wait_ge(dve_steps, count.n)
                        flat = conv_sum[:, :, :].rearrange("p k t -> p (k t)")
                        tt(flat, flat, conv_a[:, :, :].rearrange("p t n -> p (t n)"), ALU.add).then_inc(conv_summed, 1)

                heads(f"L{l}.mla", MLA_H, MV, m_st, HEADS + MLA_H * l, False, lambda t, h, o, inv: ts(mla_o[:, t, h, :], o, inv, None, ALU.mult), 36, 2, extra)
                run(4)
                for h in range(RH):
                    dve.wait_ge(decays_made, RH * l + h + 1)
                    b = take(f"L{l}.rs{h}")
                    stt(r_s[:, h % 2, :, :].rearrange("p t k -> p (t k)"), b[:, :], RDK ** -0.5,
                        r_d[:, h, :, :].rearrange("p t k -> p (t k)")).then_inc(ret_scores, 1)
                turn_lo(f"L{l}.mo", f_hi, f_lo, 4)
                r = stats_of(f"L{l}.ret", 32)
                dve.wait_ge(ret_o_copied, RH * (l + 1))
                for t in range(TT):
                    for h in range(RH):
                        o = (rqT, rkT)[h // 2][:, t, (h % 2) * RDV:(h % 2 + 1) * RDV]
                        dve.bn_stats(bns[:, 2 + RH * t + h, 0:6], o).then_inc(dve_steps, count())
                    dve.wait_ge(dve_steps, count.n)
                    for h in range(RH):
                        n = RH * t + h
                        dve.bn_aggr(r[:, 2 * n:2 * n + 2], bns[:, 2 + n, 0:6]).then_inc(ret_stats, 1)
                a = stats_of(f"L{l}.conv", 6)
                for t in range(TT):
                    b = take(f"L{l}.cback{t}")
                    dve.bn_stats(bns[:, t, 0:6], b[:, :]).then_inc(dve_steps, count())
                    dve.wait_ge(dve_steps, count.n)
                    dve.bn_aggr(a[:, 2 * t:2 * t + 2], bns[:, t, 0:6]).then_inc(conv_stats, 1)
                dve.wait_ge(conv_roots, l + 1)
                for t in range(TT):
                    b = mixed_bank[mix_at[f"L{l}.cback{t}"][0] % 2]
                    ts(conv_t[:, t, :], b[:, :], a[:, 2 * t:2 * t + 1], a[:, 4 + t:5 + t], ALU.subtract, ALU.mult).then_inc(conv_normed, 1)
                run(2)
                splits(pos + R - 1)
                dve.wait_ge(mixed, mix_at[f"L{l}.ro3"][0] + 1)
                dve.wait_ge(ret_g_gained, l + 1)
                for t in range(TT):
                    dve.wait_ge(ret_normed, TT * RH * l + RH * (t + 1))
                    for h2 in range(2):
                        e = slice(h2 * 2 * RDV, (h2 + 1) * 2 * RDV)
                        i = tt(hT[:, t, e], (rqT, rkT)[h2][:, t, :], ret_g[:, t, e], ALU.mult)
                    i.then_inc(ret_rows, 1)
                turn_lo(f"L{l}.ro", f_hi, f_lo, DT, 0.5)
                run(2)
                dve.wait_ge(conv_out_tanh, l + 1)
                flat = conv_sum[:, :, :].rearrange("p k t -> p (k t)")
                stt(flat, junk[:, :], 1.0, flat, ALU.add).then_inc(conv_silu, 1)
                dve.wait_ge(conv_hi, l + 1)
                stt(cf_lo[:, :, :].rearrange("p k t -> p (k t)"), flat, 0.5,
                    cf_hi[:, :, :].rearrange("p k t -> p (k t)").bitcast(F32), ALU.mult, ALU.subtract).then_inc(conv_split, 1)
                run(12)
                turn_lo(f"L{l}.merged", f_hi, f_lo, DT, 0.5)
                run(8)
                residual(2 * l, l, "out.")
                dve.wait_ge(x_normed, 4 * l + 2)
                apply_norm(3 + 2 * l, f"L{l}.ffn_pre")
                turn_lo(f"L{l}.h2", f_hi, f_lo, DT)
                for c in range(HT // 2 + 1):
                    if c < HT // 2:
                        run(4)
                    if c > 0:
                        turn_lo(f"L{l}.hid{c - 1}", h2_hi, h2_lo, 2, 0.5, 2 * (c - 1))
                run(22)
                residual(2 * l + 1, l, "down.")

        @block.gpsimd
        def _(pool):
            count = Count()

            def tt(o, a, b, op):
                return pool.tensor_tensor(o, a, b, op)

            def load_gain(n):
                if n >= 2:
                    pool.wait_ge(GAINS[n - 2][1], GAINS[n - 2][2])
                pool.dma_start(gains[:, n % 2, :], rows[n, :].partition_broadcast(P)).then_inc(gain_in[n % 2], 16)

            def roots(o, sums, size, done):
                width = o.shape[1]
                pool.tensor_scalar(o, sums, 1.0 / size, EPS, ALU.mult, ALU.add).then_inc(pool_steps, count())
                pool.wait_ge(pool_steps, count.n)
                tt(o, o, minus_half[:, 0:width], ALU.pow).then_inc(done, 1)

            def roots_of_norm(no):
                a = stats_of(NORMS[no], 4)
                for t in range(TT):
                    pool.wait_ge(norm_sums, 2 * no + t + 1)
                    roots(a[:, 2 + t:3 + t], a[:, t:t + 1], D, norm_roots)

            load_gain(0)
            pool.wait_ge(minus_half_set, 1)
            roots_of_norm(0)
            pool.dma_start(bc[:, :, :, :], ssm_bc).then_inc(ssm_mats_in, 16)
            pool.dma_start(lgw[:, 5, :], decay.partition_broadcast(P)).then_inc(decay_in, 16)
            load_gain(1)
            u8, v = par[:, 14:16, :], ev
            pool.wait_ge(turn_base, 1)
            pool.memset(turn[:, 0, :, 0:1], 1.0).then_inc(pool_steps, count())
            pool.memset(turn[:, 1, :, 0:1], 0.0).then_inc(pool_steps, count())
            pool.tensor_copy(v[:, 0:2, :], u8).then_inc(pool_steps, count())
            pool.tensor_copy(rho[:, :, :], par[:, 12, :].unsqueeze(2).broadcast_to([P, Q, NSUB])).then_inc(pool_steps, count())
            pool.wait_ge(pool_steps, count.n)
            pool.memset(rho[:, :, 0:1], 0.0).then_inc(pool_steps, count())
            n = 1
            while n < NSUB:
                a_r, a_i = (turn[:, c, :, 0:n] for c in range(2))
                b_r, b_i = (v[:, c, :].unsqueeze(2).broadcast_to([P, Q, n]) for c in range(2))
                w0, w1 = (x[:, 0:Q * n].rearrange("p (q k) -> p q k", k=n) for x in (
                    c_mat[:, 0, 0, :, :].rearrange("p q n -> p (q n)"), c_mat[:, 0, 1, :, :].rearrange("p q n -> p (q n)")))
                for o, x, y, op in ((0, b_r, b_i, ALU.subtract), (1, b_i, b_r, ALU.add)):
                    tt(w0, a_r, x, ALU.mult).then_inc(pool_steps, count())
                    tt(w1, a_i, y, ALU.mult).then_inc(pool_steps, count())
                    pool.wait_ge(pool_steps, count.n)
                    tt(turn[:, o, :, n:2 * n], w0, w1, op).then_inc(pool_steps, count())
                    pool.wait_ge(pool_steps, count.n)
                if 2 * n < NSUB:
                    tt(v[:, 2, :], v[:, 0, :], v[:, 0, :], ALU.mult).then_inc(pool_steps, count())
                    tt(v[:, 3, :], v[:, 1, :], v[:, 1, :], ALU.mult).then_inc(pool_steps, count())
                    tt(w0[:, :, 0:1].rearrange("p q k -> p (q k)"), v[:, 0, :], v[:, 1, :], ALU.mult).then_inc(pool_steps, count())
                    pool.wait_ge(pool_steps, count.n)
                    tt(v[:, 0, :], v[:, 2, :], v[:, 3, :], ALU.subtract).then_inc(pool_steps, count())
                    pool.tensor_scalar(v[:, 1, :], w0[:, :, 0:1].rearrange("p q k -> p (q k)"), 2.0, None, ALU.mult).then_inc(pool_steps, count())
                    pool.wait_ge(pool_steps, count.n)
                n *= 2
            pool.memset(ev[:, 3, 0:1], 0.0).then_inc(turns_made, 1)

            def c_mats(qd):
                if qd > 1:
                    pool.wait_ge(y_ready, 2 * qd - 2)
                q0 = PQ * qd
                pr, pi = (pw[:, c, 1:SUB + 1, q0:q0 + PQ].rearrange("p m q -> p q m").unsqueeze(3).broadcast_to([P, PQ, SUB, GROUP]) for c in range(2))
                cr, ci = (bc[:, c, :, q0:q0 + PQ].rearrange("p c q -> p q c").unsqueeze(2).broadcast_to([P, PQ, SUB, GROUP]) for c in (2, 3))
                o = [c_mat[:, qd % 2, c, :, :].rearrange("p q (m c) -> p q m c", c=GROUP) for c in range(2)]
                for n, (x0, x1, op) in enumerate(((cr, ci, ALU.add), (ci, cr, ALU.subtract))):
                    tt(o[n], pr, x0, ALU.mult).then_inc(pool_steps, count())
                    if n == 1:
                        pool.wait_ge(pool_steps, count.n - 1)
                    elif qd > 0:
                        pool.wait_ge(c_mats_made, qd)
                    tt(tmp2[:, :, :, :], pi, x1, ALU.mult).then_inc(pool_steps, count())
                    pool.wait_ge(pool_steps, count.n)
                    i = tt(o[n], o[n], tmp2[:, :, :, :], op)
                    if n == 1:
                        i.then_inc(c_mats_made, 1)
                    else:
                        i.then_inc(pool_steps, count())

            pool.wait_ge(c_negated, 1)
            pool.wait_ge(powers_made, 1)
            c_mats(0)
            pool.wait_ge(slot_used, 16)
            pool.memset(toep[:, :, :, :], 0.0).then_inc(toeplitz_zero, 1)
            load_gain(2)
            for qd in range(1, PARTS):
                c_mats(qd)
            load_gain(3)
            load_gain(4)
            roots_of_norm(1)
            pool.wait_ge(rows_normed, 4)
            for n in range(2):
                pool.dma_start(qkg[:, n, :], qk_gain[n, :].partition_broadcast(P)).then_inc(qk_gain_in, 16)
            for i in range(4):
                pool.wait_ge(squares_summed, 2 * i + 2)
                a = stats_of(f"qk{i}", 16)
                roots(a[:, 8:16], a[:, 0:8], HD, qk_roots)
            load_gain(5)
            for l in range(DEPTH2):
                if l == 0:
                    pool.wait_ge(x_updated, 8)
                else:
                    pool.wait_ge(x_normed, 4 * l)
                roots_of_norm(2 + 2 * l)
                pool.dma_start(latp[:, 0:QR], lat_gain[l, 0:QR].partition_broadcast(P)).then_inc(layer_params_in, 16)
                pool.dma_start(latp[:, QR:QR + KVR], lat_gain[l, QR:QR + KVR].partition_broadcast(P)).then_inc(layer_params_in, 16)
                pool.dma_start(cfp[:, :, :], conv_p[l]).then_inc(layer_params_in, 16)
                load_gain(6 + 5 * l)
                a = stats_of(f"L{l}.lat", 8)
                pool.wait_ge(lat_sums, 4 * (l + 1))
                pool.tensor_scalar(a[:, 4:6], a[:, 0:2], 1.0 / QR, EPS, ALU.mult, ALU.add).then_inc(pool_steps, count())
                pool.tensor_scalar(a[:, 6:8], a[:, 2:4], 1.0 / KVR, EPS, ALU.mult, ALU.add).then_inc(pool_steps, count())
                pool.wait_ge(pool_steps, count.n)
                tt(a[:, 4:8], a[:, 4:8], minus_half[:, 0:4], ALU.pow).then_inc(lat_roots, 1)
                pool.wait_ge(lg_made, 1)
                pool.wait_ge(mla_roped, 4 * (l + 1))
                pool.wait_ge(turned, turn_at[f"L{l}.lat.1"][0] + 1)
                d_f, d_b = const[:, C_DF:C_DB], const[:, C_DB:C_INVR]
                for h in range(RH):
                    o, w = r_d[:, h, :, :].rearrange("p t k -> p (t k)"), junk[:, 512 * (h % 2):512 * (h % 2 + 1)]
                    c = 8 * l + h
                    if h > 1:
                        pool.wait_ge(decay_args, RH * l + h - 1)
                    pool.tensor_scalar(o, d_f, lg[:, c:c + 1], None, ALU.mult).then_inc(pool_steps, count())
                    pool.tensor_scalar(w, d_b, lg[:, c + RH:c + RH + 1], None, ALU.mult).then_inc(pool_steps, count())
                    pool.wait_ge(pool_steps, count.n)
                    tt(o, o, w, ALU.add).then_inc(decay_args, 1)
                pool.wait_ge(conv_in, 2 * (l + 1))
                side = conv_a[:, :, :].rearrange("p t (a c) -> p (t a) c", a=2)
                w = junk[:, :].rearrange("p (k c) -> p k c", k=4)
                pool.wait_ge(decay_args, RH * (l + 1))
                for n in range(TAPS - SIDE_TAPS, TAPS):
                    first = n == TAPS - SIDE_TAPS
                    for k in range(4):
                        pool.tensor_scalar((side if first else w)[:, k, :], conv_F[:, k, n:n + SEQ], cfp[:, k, n:n + 1], None,
                                           ALU.mult).then_inc(pool_steps, count())
                    pool.wait_ge(pool_steps, count.n)
                    if not first:
                        i = tt(side, side, w, ALU.add)
                        if n == TAPS - 1:
                            i.then_inc(conv_side, 1)
                        else:
                            i.then_inc(pool_steps, count())
                            pool.wait_ge(pool_steps, count.n)
                pool.wait_ge(ret_g_silu, 4 * (l + 1))
                g = gain_row(pool, f"L{l}.gn")
                tt(ret_g[:, :, :], ret_g[:, :, :], g.unsqueeze(1).broadcast_to([P, TT, D]), ALU.mult).then_inc(ret_g_gained, 1)
                r = stats_of(f"L{l}.ret", 32)
                for t in range(TT):
                    m = RH * t
                    pool.wait_ge(ret_stats, TT * RH * l + RH * (t + 1))
                    mean, var = (r[:, 2 * m:2 * m + 2 * RH].rearrange("p (n m) -> p m n", m=2)[:, k] for k in range(2))
                    scale, offset = r[:, 16 + m:16 + m + RH], r[:, 24 + m:24 + m + RH]
                    pool.tensor_scalar(offset, mean, -1.0, None, ALU.mult).then_inc(pool_steps, count())
                    roots(scale, var, 1.0, pool_steps)
                    count()
                    pool.wait_ge(pool_steps, count.n)
                    tt(offset, offset, scale, ALU.mult).then_inc(ret_roots, 1)
                a = stats_of(f"L{l}.conv", 6)
                pool.wait_ge(conv_stats, 2 * (l + 1))
                roots(a[:, 4:6], a[:, 0:4].rearrange("p (t m) -> p m t", m=2)[:, 1], 1.0, conv_roots)
                load_gain(7 + 5 * l)
                for kind in ("out.", "down."):
                    a = stats_of(f"L{l}.{kind}post", 8)
                    no = 2 * l + (kind == "down.")
                    for t in range(TT):
                        pool.wait_ge(post_sums, 4 * no + 3 + t)
                        pool.tensor_scalar(a[:, 4 + t:5 + t], a[:, 2 * t:2 * t + 1], a[:, 2 * t + 1:2 * t + 2], EPS, ALU.add,
                                           ALU.add).then_inc(pool_steps, count())
                        pool.wait_ge(pool_steps, count.n)
                        tt(a[:, 6 + t:7 + t], a[:, 4 + t:5 + t], minus_half[:, 0:1], ALU.pow).then_inc(post_roots, 1)
                    if kind == "out.":
                        load_gain(8 + 5 * l)
                        roots_of_norm(3 + 2 * l)
                        if l + 1 < DEPTH2:
                            load_gain(9 + 5 * l)
                if l + 1 < DEPTH2:
                    load_gain(10 + 5 * l)


def lay_out(inputs):
    a = {k: np.asarray(v) for k, v in inputs.items()}
    table, slots, total = weight_plan()

    def weights(name):
        l, kind = (int(name[1]), name.split(".", 1)[1]) if name[0] == "L" else (0, name)
        base = kind.rstrip("0123456789")
        i = int(kind[len(base):])
        c = slice(512 * i, 512 * (i + 1))
        if name[0] != "L":
            return {"ssm_in.": a["ssm_w_in"], "glu.": a["ssm_w_glu"], "ssm_out.": a["ssm_w_out"],
                    "attn_in.": a["attn_w_in"], "attn_out.": a["attn_w_out"]}[base][0][:, c]
        w_in = a["w_in_2"][l]
        lat, conv = QR + KVR + ROPE, 2 * CONV
        ret = 2 * RH * RDK + 2 * RH * RDV
        if base == "lat.":
            return w_in[:, 0:lat]
        if base == "glu.":
            return w_in[:, lat:lat + conv][:, c]
        if base == "ret.":
            return w_in[:, lat + conv:lat + conv + ret][:, c]
        if base == "gate.":
            return w_in[:, lat + conv + ret:][:, c]
        if base == "uq.":
            return a["mla_w_uq_2"][l][:, 384 * i:384 * (i + 1)]
        if base == "ffn.":
            f = slice(FCH * i, FCH * (i + 1))
            return np.concatenate([a["ffn_w_gate_2"][l][:, f], a["ffn_w_up_2"][l][:, f]], axis=1)
        return a[{"ukv.": "mla_w_ukv_2", "mla_o.": "mla_w_o_2", "conv_o.": "conv_w_pw_2", "ret_o.": "ret_w_o_2",
                  "out.": "w_out_2", "down.": "ffn_w_down_2"}[base]][l][:, c]

    parts, block, last = [], None, None
    for s in slots:
        if s["chunk"] != last:
            last = s["chunk"]
            block = weights(last)
        rows = block[s["k"] * P:(s["k"] + s["nk"]) * P]
        parts.append(rows.reshape(s["nk"], P, s["width"]).transpose(1, 0, 2).reshape(-1))

    def pairs(x):
        x = x.reshape(Q, 2, STATE, *x.shape[2:])
        return np.moveaxis(x, 0, -1).reshape(2 * STATE, *x.shape[3:], Q)

    def gain_rows():
        rows = [a["norm_g"][0], a["ssm_d"][0], a["ssm_b_glu"][0], a["norm_g"][1]]
        for l in range(DEPTH2):
            rows += [a["ln_mix_pre_2"][l], a["ret_gn_g_2"][l], a["ln_mix_post_2"][l], a["ln_ffn_pre_2"][l], a["ln_ffn_post_2"][l]]
        return np.stack(rows)

    conv = np.stack([np.concatenate([a["conv_w_dw_2"][l], a["conv_b_dw_2"][l][None], a["conv_ln_g_2"][l][None], a["conv_ln_b_2"][l][None]])
                     for l in range(DEPTH2)])
    return {
        "stream": np.concatenate(parts),
        "consts": shape_constants(),
        "x_in": a["x"][0].reshape(TT, P, D).transpose(1, 0, 2),
        "ssm_ab": np.stack([pairs(a["ssm_a_re"][0]), pairs(a["ssm_a_im"][0])], axis=1),
        "ssm_ldt": a["ssm_log_dt"][0].reshape(Q, 2).T,
        "ssm_bc": np.stack([pairs(a["ssm_b_re"][0]), pairs(a["ssm_b_im"][0]),
                            pairs(a["ssm_c_re"][0].transpose(0, 2, 1)), pairs(a["ssm_c_im"][0].transpose(0, 2, 1))], axis=1),
        "rows": gain_rows(),
        "qk_gain": np.stack([a["attn_q_gain"][0], a["attn_k_gain"][0]]),
        "positions": a["positions_2"][0].reshape(TT, P).T,
        "decay": a["ret_decay_logits_2"].reshape(-1),
        "conv_p": conv.reshape(DEPTH2, TAPS + 3, 4, P).transpose(0, 3, 2, 1),
        "lat_gain": np.concatenate([a["mla_q_norm_2"], a["mla_kv_norm_2"]], axis=1),
    }


def kernel(**inputs):
    import concourse.bacc as bacc
    from concourse.bass_utils import run_bass_kernel_spmd

    nc = bacc.Bacc("TRN2", target_bir_lowering=False, num_devices=1)
    arrays, args = {}, {}
    for name, x in lay_out(inputs).items():
        x = np.ascontiguousarray(x)
        arrays[name + "_dram"] = x
        args[name] = nc.dram_tensor(name + "_dram", x.shape, mybir.dt.from_np(x.dtype), kind="ExternalInput").ap()
    args["out"] = nc.dram_tensor("out_dram", (P, TT, D), F32, kind="ExternalOutput").ap()
    build(nc, **args)
    r = run_bass_kernel_spmd(nc, [arrays], core_ids=[0])
    return r.results[0]["out_dram"].transpose(1, 0, 2).reshape(1, SEQ, D)
```
